# Optimizing a Trainium2 kernel written in Bass

```python
import math
import jax, jax.numpy as jnp
from jax import lax
import numpy as np

D_MODEL = 1024
BATCH = 1
SEQ = 1024
DEPTH = 1

CHUNK = 64
Q_BLOCK = 128
HEAD_DIM = 64
ROPE_DIM = 64
ROPE_THETA = 10000.0
A_WIDTH = D_MODEL // 2
A_HEADS = A_WIDTH // HEAD_DIM
IDX_HEADS = 8
IDX_DIM = 64
IDX_TOPK_MAX = 256
B_WIDTH = D_MODEL - A_WIDTH
B_QK_DIM = HEAD_DIM
B_V_DIM = 2 * B_QK_DIM
B_HEADS = B_WIDTH // B_V_DIM
SPLIT_SIZES = (
    A_HEADS * HEAD_DIM, A_HEADS * HEAD_DIM, A_HEADS * HEAD_DIM,
    IDX_HEADS * IDX_DIM, IDX_DIM, IDX_HEADS,
    B_HEADS * 2 * B_QK_DIM, B_HEADS * 2 * B_QK_DIM, B_HEADS * B_V_DIM,
)
PROJ_WIDTH = sum(SPLIT_SIZES)
SPLIT_POINTS = tuple(int(v) for v in np.cumsum(SPLIT_SIZES)[:-1])
N_EXPERTS = 64
TOP_K = 8
N_GROUPS = 8
TOPK_GROUPS = 4
EXPERT_DIM = 256
SHARED_DIM = 256
ROUTED_SCALE = 2.5
MOE_BLOCK = 256
PLE_DIM = 256
LN_EPS = 1e-5
RMS_EPS = 1e-5
DEEPNORM_ALPHA = (2.0 * DEPTH) ** 0.25
DEEPNORM_BETA = (8.0 * DEPTH) ** -0.25

kernel_name = "hybrid_dsa_diffattn_moe_deepnorm_block"

def layer_norm(x, g, b):
    xf = x.astype(jnp.float32)
    mu = jnp.mean(xf, axis=-1, keepdims=True)
    var = jnp.mean(jnp.square(xf - mu), axis=-1, keepdims=True)
    return ((xf - mu) * lax.rsqrt(var + LN_EPS) * g + b).astype(x.dtype)

def rope_tables(positions):
    inv = ROPE_THETA ** (-jnp.arange(0, ROPE_DIM, 2, dtype=jnp.float32) / ROPE_DIM)
    ang = positions.astype(jnp.float32)[..., None] * inv
    return jnp.cos(ang), jnp.sin(ang)

def apply_rope(x, cos, sin):
    x1, x2 = jnp.split(x.astype(jnp.float32), 2, axis=-1)
    c = cos[:, :, None, :]
    s = sin[:, :, None, :]
    return jnp.concatenate([x1 * c - x2 * s, x2 * c + x1 * s], axis=-1).astype(x.dtype)

def dsa_mixer(q, k, v, q_idx, k_idx, w_idx, n_keep):
    bsz, seq, n_heads, dh = q.shape
    n_blocks = seq // Q_BLOCK
    key_chunk = jnp.arange(seq) // CHUNK
    attn_scale = dh ** -0.5
    w_scale = (IDX_HEADS ** -0.5) * (IDX_DIM ** -0.5)

    def block(i):
        t0 = i * Q_BLOCK
        qb = lax.dynamic_slice_in_dim(q, t0, Q_BLOCK, axis=1)
        qib = lax.dynamic_slice_in_dim(q_idx, t0, Q_BLOCK, axis=1)
        wb = lax.dynamic_slice_in_dim(w_idx, t0, Q_BLOCK, axis=1).astype(jnp.float32) * w_scale
        q_chunk = (t0 + jnp.arange(Q_BLOCK)) // CHUNK
        admissible = key_chunk[None, :] <= q_chunk[:, None]
        rel = jax.nn.relu(jnp.einsum('bthd,bsd->bths', qib, k_idx,
                                     preferred_element_type=jnp.float32))
        score = jnp.einsum('bth,bths->bts', wb, rel)
        score = jnp.where(admissible[None], score, -jnp.inf)
        _, sel = lax.top_k(score, n_keep)
        sel_ok = key_chunk[sel] <= q_chunk[None, :, None]
        k_sel = jax.vmap(lambda kb, ib: kb[ib])(k, sel)
        v_sel = jax.vmap(lambda vb, ib: vb[ib])(v, sel)
        logits = jnp.einsum('bthd,btkhd->bhtk', qb, k_sel,
                            preferred_element_type=jnp.float32) * attn_scale
        logits = jnp.where(sel_ok[:, None], logits, -jnp.inf)
        prob = jax.nn.softmax(logits, axis=-1).astype(v.dtype)
        return jnp.einsum('bhtk,btkhd->bthd', prob, v_sel)

    out = lax.map(block, jnp.arange(n_blocks))
    return out.transpose(1, 0, 2, 3, 4).reshape(bsz, seq, n_heads * dh)

def diff_mixer(q, k, v, lam, subln_g, lambda_init):
    bsz, seq, n_heads, _, dq = q.shape
    dv = v.shape[-1]
    n_blocks = seq // Q_BLOCK
    key_chunk = jnp.arange(seq) // CHUNK
    scale = dq ** -0.5

    def block(i):
        t0 = i * Q_BLOCK
        qb = lax.dynamic_slice_in_dim(q, t0, Q_BLOCK, axis=1)
        q_chunk = (t0 + jnp.arange(Q_BLOCK)) // CHUNK
        mask = key_chunk[None, :] <= q_chunk[:, None]
        logits = jnp.einsum('bthmd,bshmd->bhmts', qb, k,
                            preferred_element_type=jnp.float32) * scale
        logits = jnp.where(mask[None, None, None], logits, -jnp.inf)
        prob = jax.nn.softmax(logits, axis=-1)
        attn = prob[:, :, 0] - lam * prob[:, :, 1]
        return jnp.einsum('bhts,bshd->bthd', attn.astype(v.dtype), v)

    out = lax.map(block, jnp.arange(n_blocks))
    out = out.transpose(1, 0, 2, 3, 4).reshape(bsz, seq, n_heads, dv)
    of = out.astype(jnp.float32)
    of = of * lax.rsqrt(jnp.mean(jnp.square(of), axis=-1, keepdims=True) + RMS_EPS)
    of = of * subln_g * (1.0 - lambda_init)
    return of.astype(v.dtype).reshape(bsz, seq, n_heads * dv)

def moe(h, w_router, router_bias, w_exp_gate, w_exp_up, w_exp_down, w_sh_gate, w_sh_up, w_sh_down):
    bsz, seq, d = h.shape
    n_tok = bsz * seq
    xt = h.reshape(n_tok, d)
    scores = jax.nn.sigmoid(jnp.einsum('td,de->te', xt, w_router,
                                       preferred_element_type=jnp.float32))
    biased = scores + router_bias.astype(jnp.float32)
    grp = biased.reshape(n_tok, N_GROUPS, N_EXPERTS // N_GROUPS)
    grp_score = jnp.sum(lax.top_k(grp, 2)[0], axis=-1)
    _, top_g = lax.top_k(grp_score, TOPK_GROUPS)
    gmask = jnp.any(top_g[..., None] == jnp.arange(N_GROUPS), axis=-2)
    emask = jnp.repeat(gmask, N_EXPERTS // N_GROUPS, axis=-1)
    _, eidx = lax.top_k(jnp.where(emask, biased, -jnp.inf), TOP_K)
    gate = jnp.take_along_axis(scores, eidx, axis=-1)
    gate = gate / jnp.sum(gate, axis=-1, keepdims=True) * ROUTED_SCALE

    n_assign = n_tok * TOP_K
    flat_e = eidx.reshape(n_assign)
    flat_tok = jnp.repeat(jnp.arange(n_tok, dtype=jnp.int32), TOP_K)
    flat_w = gate.reshape(n_assign)
    order = jnp.argsort(flat_e)
    e_sorted = flat_e[order]
    counts = jnp.zeros((N_EXPERTS,), jnp.int32).at[flat_e].add(1)
    padded = (counts + MOE_BLOCK - 1) // MOE_BLOCK * MOE_BLOCK
    start = jnp.cumsum(counts) - counts
    pend = jnp.cumsum(padded)
    pstart = pend - padded
    dest = pstart[e_sorted] + (jnp.arange(n_assign, dtype=jnp.int32) - start[e_sorted])
    n_blocks = (n_assign + N_EXPERTS * (MOE_BLOCK - 1) + MOE_BLOCK - 1) // MOE_BLOCK
    n_rows = n_blocks * MOE_BLOCK
    tok_buf = jnp.zeros((n_rows,), jnp.int32).at[dest].set(flat_tok[order])
    w_buf = jnp.zeros((n_rows,), gate.dtype).at[dest].set(flat_w[order])
    blk_e = jnp.minimum(jnp.searchsorted(pend, jnp.arange(n_blocks, dtype=jnp.int32) * MOE_BLOCK,
                                         side='right'), N_EXPERTS - 1)

    def step(acc, b):
        toks = lax.dynamic_slice_in_dim(tok_buf, b * MOE_BLOCK, MOE_BLOCK)
        wts = lax.dynamic_slice_in_dim(w_buf, b * MOE_BLOCK, MOE_BLOCK)
        e = blk_e[b]
        xb = xt[toks]
        hid = jax.nn.silu(xb @ w_exp_gate[e]) * (xb @ w_exp_up[e])
        y = (hid @ w_exp_down[e]) * wts[:, None]
        return acc.at[toks].add(y.astype(acc.dtype)), None

    routed, _ = lax.scan(step, jnp.zeros_like(xt), jnp.arange(n_blocks))
    shared = (jax.nn.silu(xt @ w_sh_gate) * (xt @ w_sh_up)) @ w_sh_down
    return (routed + shared).reshape(bsz, seq, d)

def setup_inputs(seed: int = 0) -> dict:
    key = jax.random.key(seed)
    ks = jax.random.split(key, 24)

    def nrm(k, shape, scale):
        return jax.random.normal(k, shape, jnp.float32) * scale

    d = D_MODEL
    col_scale = jnp.concatenate([
        jnp.ones((2 * A_HEADS * HEAD_DIM,), jnp.float32),
        jnp.full((A_HEADS * HEAD_DIM,), DEEPNORM_BETA, jnp.float32),
        jnp.ones((IDX_HEADS * IDX_DIM + IDX_DIM + IDX_HEADS + 2 * B_HEADS * 2 * B_QK_DIM,), jnp.float32),
        jnp.full((B_HEADS * B_V_DIM,), DEEPNORM_BETA, jnp.float32),
    ])
    return {
        "x": nrm(ks[0], (BATCH, SEQ, d), 1.0),
        "p": nrm(ks[1], (DEPTH, BATCH, SEQ, PLE_DIM), 1.0),
        "positions": jnp.broadcast_to(jnp.arange(SEQ, dtype=jnp.int32), (BATCH, SEQ)),
        "ln_emb_g": 1.0 + nrm(ks[2], (d,), 0.02),
        "ln_emb_b": nrm(ks[3], (d,), 0.02),
        "w_in": nrm(ks[4], (DEPTH, d, PROJ_WIDTH), d ** -0.5) * col_scale,
        "w_o": nrm(ks[5], (DEPTH, d, d), DEEPNORM_BETA * d ** -0.5),
        "diff_lq1": nrm(ks[6], (DEPTH, B_QK_DIM), 0.1),
        "diff_lk1": nrm(ks[7], (DEPTH, B_QK_DIM), 0.1),
        "diff_lq2": nrm(ks[8], (DEPTH, B_QK_DIM), 0.1),
        "diff_lk2": nrm(ks[9], (DEPTH, B_QK_DIM), 0.1),
        "diff_subln_g": 1.0 + nrm(ks[10], (DEPTH, B_V_DIM), 0.02),
        "ln1_g": 1.0 + nrm(ks[11], (DEPTH, d), 0.02),
        "ln1_b": nrm(ks[12], (DEPTH, d), 0.02),
        "w_router": nrm(ks[13], (DEPTH, d, N_EXPERTS), d ** -0.5),
        "router_bias": nrm(ks[14], (DEPTH, N_EXPERTS), 0.01),
        "w_exp_gate": nrm(ks[15], (DEPTH, N_EXPERTS, d, EXPERT_DIM), d ** -0.5),
        "w_exp_up": nrm(ks[16], (DEPTH, N_EXPERTS, d, EXPERT_DIM), d ** -0.5),
        "w_exp_down": nrm(ks[17], (DEPTH, N_EXPERTS, EXPERT_DIM, d), DEEPNORM_BETA * EXPERT_DIM ** -0.5),
        "w_sh_gate": nrm(ks[18], (DEPTH, d, SHARED_DIM), d ** -0.5),
        "w_sh_up": nrm(ks[19], (DEPTH, d, SHARED_DIM), d ** -0.5),
        "w_sh_down": nrm(ks[20], (DEPTH, SHARED_DIM, d), DEEPNORM_BETA * SHARED_DIM ** -0.5),
        "ln2_g": 1.0 + nrm(ks[21], (DEPTH, d), 0.02),
        "ln2_b": nrm(ks[22], (DEPTH, d), 0.02),
        "w_ple_gate": nrm(jax.random.fold_in(ks[23], 0), (DEPTH, d, d), d ** -0.5),
        "b_ple_gate": nrm(jax.random.fold_in(ks[23], 1), (DEPTH, d), 0.02),
        "w_ple_proj": nrm(jax.random.fold_in(ks[23], 2), (DEPTH, PLE_DIM, d), 0.5 * PLE_DIM ** -0.5),
    }

def reference(x, p, positions, ln_emb_g, ln_emb_b, w_in, w_o, diff_lq1, diff_lk1, diff_lq2, diff_lk2,
              diff_subln_g, ln1_g, ln1_b, w_router, router_bias, w_exp_gate, w_exp_up, w_exp_down,
              w_sh_gate, w_sh_up, w_sh_down, ln2_g, ln2_b, w_ple_gate, b_ple_gate, w_ple_proj):
    bsz, seq, _ = x.shape
    n_keep = min(IDX_TOPK_MAX, seq // 4)
    cos, sin = rope_tables(positions)
    h = layer_norm(x, ln_emb_g, ln_emb_b)
    for i in range(DEPTH):
        lambda_init = 0.8 - 0.6 * math.exp(-0.3 * i)
        proj = jnp.einsum('bsd,de->bse', h, w_in[i])
        a_q, a_k, a_v, i_q, i_k, i_w, b_q, b_k, b_v = jnp.split(proj, SPLIT_POINTS, axis=-1)
        a_q = apply_rope(a_q.reshape(bsz, seq, A_HEADS, HEAD_DIM), cos, sin)
        a_k = apply_rope(a_k.reshape(bsz, seq, A_HEADS, HEAD_DIM), cos, sin)
        a_v = a_v.reshape(bsz, seq, A_HEADS, HEAD_DIM)
        i_q = apply_rope(i_q.reshape(bsz, seq, IDX_HEADS, IDX_DIM), cos, sin)
        i_k = apply_rope(i_k.reshape(bsz, seq, 1, IDX_DIM), cos, sin)[:, :, 0]
        out_a = dsa_mixer(a_q, a_k, a_v, i_q, i_k, i_w, n_keep)
        b_q = apply_rope(b_q.reshape(bsz, seq, B_HEADS * 2, B_QK_DIM), cos, sin)
        b_k = apply_rope(b_k.reshape(bsz, seq, B_HEADS * 2, B_QK_DIM), cos, sin)
        b_q = b_q.reshape(bsz, seq, B_HEADS, 2, B_QK_DIM)
        b_k = b_k.reshape(bsz, seq, B_HEADS, 2, B_QK_DIM)
        b_v = b_v.reshape(bsz, seq, B_HEADS, B_V_DIM)
        lam = (jnp.exp(jnp.sum(diff_lq1[i].astype(jnp.float32) * diff_lk1[i]))
               - jnp.exp(jnp.sum(diff_lq2[i].astype(jnp.float32) * diff_lk2[i])) + lambda_init)
        out_b = diff_mixer(b_q, b_k, b_v, lam, diff_subln_g[i], lambda_init)
        mix = jnp.einsum('bse,ed->bsd', jnp.concatenate([out_a, out_b], axis=-1), w_o[i])
        h = layer_norm(DEEPNORM_ALPHA * h + mix, ln1_g[i], ln1_b[i])
        ffn = moe(h, w_router[i], router_bias[i], w_exp_gate[i], w_exp_up[i], w_exp_down[i],
                  w_sh_gate[i], w_sh_up[i], w_sh_down[i])
        h = layer_norm(DEEPNORM_ALPHA * h + ffn, ln2_g[i], ln2_b[i])
        gate = jax.nn.sigmoid(jnp.einsum('bsd,de->bse', h, w_ple_gate[i]) + b_ple_gate[i])
        h = h + gate * jnp.einsum('bsk,kd->bsd', p[i], w_ple_proj[i])
    return h


_drawn_inputs = setup_inputs


def setup_inputs(seed=0):
    import zlib

    import numpy as np

    out = dict(_drawn_inputs(seed))
    spreads = {}
    factors = {'diff_lk2': 4.021, 'ln2_g': 2.833, 'ln2_b': 2.912, 'b_ple_gate': 8.0}
    for name, (base, spread) in spreads.items():
        noise = np.random.default_rng([zlib.crc32(name.encode()), seed]).standard_normal(out[name].shape)
        drawn = base * np.exp(spread * noise) if base else spread * noise
        out[name] = __import__('jax').numpy.asarray(drawn.astype(out[name].dtype))
    for name, factor in factors.items():
        out[name] = (out[name] * factor).astype(out[name].dtype)
    return out
```

```python
from contextlib import ExitStack

import concourse.bass as bass
from concourse import mybir

F32 = mybir.dt.float32
BF16 = mybir.dt.bfloat16
I32 = mybir.dt.int32
U32 = mybir.dt.uint32
ALU = mybir.AluOpType
ACT = mybir.ActivationFunctionType
AX = mybir.AxisListType

P = 128
D = 1024
S = 1024
NT = S // P
KC = D // P
HD = 64
HALF = HD // 2
AH = 8
BH = 4
CH = 64
NKEEP = 256
ALPHA = 2.0 ** 0.25
EPS = 1e-5
LAMBDA_INIT = 0.8 - 0.6
SCALE = HD ** -0.5
WSCALE = (8 ** -0.5) * (64 ** -0.5)
NE = 64
NG = 8
TOPG = 4
TOPK = 8
ED = 256
ROUTED = 2.5
PLE = 256
MASK = -1e30
FILL = -3.0e38
TAKEN = -3.4e38
SHB = NT
MAXB = SHB + (S * TOPK + NE * P) // P
NW = 4
EW = 3 * 2 * D

C_QA, C_KA, C_VA, C_QI, C_KI, C_QB, C_KB, C_VB = 0, 512, 1024, 1536, 2048, 2120, 2632, 3144
GROUPS = [("qi", C_QI, 512), ("ki", C_KI, 72), ("va", C_VA, 512), ("vb", C_VB, 512),
          ("qa", C_QA, 512), ("ka", C_KA, 512), ("qb", C_QB, 512), ("kb", C_KB, 512)]
NGR = len(GROUPS)
ROPED = [g for g, (n, _, _) in enumerate(GROUPS) if n[0] in "qk"]


def build(nc, x, p, positions, ln_emb_g, ln_emb_b, w_in, w_o, lq1, lk1, lq2, lk2, subln_g, ln1_g, ln1_b,
          w_router, router_bias, w_gate, w_up, w_down, w_sh_gate, w_sh_up, w_sh_down, ln2_g, ln2_b,
          w_ple_gate, b_ple_gate, w_ple_proj, inv_freq, out):
    x_t = x.rearrange("a (t q) d -> t (a q) d", q=P)
    out_t = out.rearrange("a (t q) d -> t (a q) d", q=P)
    p_t = p.rearrange("l a (t q) d -> t (l a q) d", q=P)
    w_in_k = w_in.rearrange("l (k q) n -> q (l k) n", q=P)
    w_o_k = w_o.rearrange("l (k q) n -> q (l k) n", q=P)
    w_r_k = w_router.rearrange("l (k q) n -> q (l k) n", q=P)
    w_pg_k = w_ple_gate.rearrange("l (k q) n -> q (l k) n", q=P)
    w_pp_k = w_ple_proj.rearrange("l (k q) n -> q (l k) n", q=P)
    w_g_e = w_gate.rearrange("l e (q k) f -> (l e) q (k f)", q=P)
    w_u_e = w_up.rearrange("l e (q k) f -> (l e) q (k f)", q=P)
    w_d_e = w_down.rearrange("l e (q k) f -> (l e) q (k f)", q=P)
    w_sg = w_sh_gate.rearrange("l (q k) f -> q (l k f)", q=P)
    w_su = w_sh_up.rearrange("l (q k) f -> q (l k f)", q=P)
    w_sd = w_sh_down.rearrange("l (q k) f -> q (l k f)", q=P)

    h_d = nc.dram_tensor("h_emb", (S, D), F32).ap()
    h1_d = nc.dram_tensor("h_mix", (S, D), F32).ap()
    y_d = nc.dram_tensor("y_slots", (MAXB * P, D), F32).ap()

    ctx = ExitStack()
    with ctx:
        arena = ctx.enter_context(nc.sbuf_tensor("arena", [P, 53200], F32))

        def at(off, *dims, dt=F32):
            n = 1
            for d in dims:
                n *= d
            if dt == BF16:
                v = arena[:, off:off + n // 2].bitcast(BF16)
            else:
                v = arena[:, off:off + n]
                if dt != F32:
                    v = v.bitcast(dt)
            if len(dims) == 1:
                return v
            names = "abcd"[:len(dims)]
            return v.rearrange(f"p ({' '.join(names)}) -> p {' '.join(names)}", **dict(zip(names[1:], dims[1:])))

        hT = at(0, KC, S)
        w_sl = [at(8192, KC, 512), at(12288, KC, 512)]
        raw = [at(16384, 512), at(16896, 512)]
        rot = [at(17408, 512), at(17920, 512)]
        rot2 = at(18432, 512)
        rel = [at(18944, 1024), at(19968, 1024)]
        qiT = qbT = at(20992, 4, S)
        kiT = at(25088, S)
        qaT, kaT, kbT = at(26112, 4, S), at(30208, 4, S), at(34304, 4, S)
        va, vb = at(38400, NT, 512), at(42496, NT, 512)
        h0 = at(26112, NT, D)
        g_emb, b_emb = at(34304, D), at(35328, D)
        off_sc = [46592 + 64 * t * (t + 1) for t in range(NT)]
        score = [at(off_sc[t], P * (t + 1)) for t in range(NT)]
        wo = at(0, KC, D)
        prob = [at(8192 + 1024 * i, 1024) for i in range(4)]
        pT = [at(12288 + 1024 * i, NT, P) for i in range(2)]
        mix = at(14336, D)
        mixT = at(15360, KC, P)
        h_in = at(16384, D)
        h1 = at(17408, D)
        g1, b1 = at(18432, D), at(19456, D)
        sq = at(20480, BH, P)
        wr = at(25088, KC, NE)
        rl = at(25600, NT, NE)
        w_e = at(0, NW, EW)
        y_sb = at(26112, D)
        xg = at(27136, D)
        xT = at(28160, KC, P)
        onehot = at(29184, NT, P, dt=BF16)
        sg, hid, hidT = at(29696, ED), at(29952, ED), at(30208, 2, P)
        slotm = at(30464, NT, NE + 1)
        gate = at(30984, NT, NE)
        iota_s = at(31496, P)
        slot8 = at(31624, NT, TOPK)
        slot8i = at(31688, NT, TOPK, dt=U32)
        gate8 = at(31752, NT, TOPK)
        tab = at(31816, 2, 2 * P, dt=I32)
        bend_i = at(32328, NE + 1, dt=I32)
        bend = at(32396, NE + 1)
        nblk = at(32464, NE)
        sig, biased = at(32528, NT, NE), at(33040, NT, NE)
        tmp1, tmp2, tmp3 = at(33552, 512), at(34064, 512), at(34576, 512)
        sel_b = at(35088, NT, NE, dt=BF16)
        g8 = at(35344, NT * NG, 8)
        rbias = at(35856, NE)
        w_up_v = w_e[:, :, 0:4096].rearrange("p s (j k f) -> p s j k f", j=2, k=KC)
        w_dn_v = w_e[:, :, 4096:6144].rearrange("p s (j n) -> p s j n", j=2)
        xg_v = xg.rearrange("p (q k) -> p k q", k=KC)
        hid_v = hid.rearrange("p (q j) -> p j q", j=2)
        wpg, wpp = at(36864, KC, D), at(45056, 2, D)
        g2, b2, bp = at(47104, D), at(48128, D), at(49152, D)
        acc = [at(1024 * i, D) for i in range(2)]
        ysh = [at(2048 + 1024 * i, D) for i in range(2)]
        yk = [at(4096 + 1024 * i, D) for i in range(8)]
        h2T = at(12288, KC, P)
        zt, ot = at(13312, D), [at(14336 + 1024 * i, D) for i in range(2)]
        pt_sb = [at(16384 + 256 * i, PLE) for i in range(2)]
        ppT = at(16896, 2, P)
        ident = at(51200, P)
        cosd, sind = at(51328, NT, HD), at(51840, NT, HD)
        used = [52352]

        def small(*dims, dt=F32):
            n = 1
            for d in dims:
                n *= d
            o = used[0]
            used[0] += (n + 1) // 2 if dt == BF16 else n
            assert used[0] <= 53200, used
            return at(o, *dims, dt=dt)

        iws = small(NT, 8)
        stats, mv = small(2, 6), small(2)
        rs, nmr = small(2, 1), small(2, 1)
        vareps = small(2, 1)
        mhalf = small(8)
        m8 = small(8)
        mx, nmx = small(12 + BH), small(12 + BH)
        ssum = [small(12 + BH) for _ in range(2)]
        rsum = small(12 + BH)
        cB = small(2)
        ms = small(BH)
        rms = small(BH)
        subg = small(P)
        lam2 = small(4)
        neglam = small(1)
        posi, posf = small(NT, dt=I32), small(NT)
        rowneg = small(HD)
        colq = small(P)
        tokpair = small(NT, 2, dt=BF16)
        gbase = small(1)
        idx = small(1, dt=U32)
        ang = at(46592, NT, HALF)
        tn, tr, tc, tw = (at(46592 + 256 * i, NT, HALF) for i in range(1, 5))
        inv = at(48128, HALF)
        lam4 = at(48192, 4, HD)
        gsub = at(50304, P)
        thr = at(50432, 7)
        tri = at(50496, NG, NG)
        gs = at(50560, NT, NG)
        gpen = at(50624, NT, NG)
        den8 = at(50688, NT)
        eobc = at(50696, 2)
        itg = at(50700, 2)
        zer = at(50712, NE)
        ones_b = at(50784, P, dt=BF16)
        upper_b = at(50848, P, dt=BF16)

        tp = [ctx.enter_context(nc.psum_tensor(f"turn{i}", [P, 512], F32)) for i in range(2)]
        lg = [ctx.enter_context(nc.psum_tensor(f"logit{i}", [P, 1024], F32)) for i in range(2)]
        pa = [ctx.enter_context(nc.psum_tensor(f"acc{i}", [P, 512], F32)) for i in range(2)]

        def sem(name):
            return ctx.enter_context(nc.semaphore(name))

        consts = sem("consts")
        const_in = sem("const_in")
        x_in = [sem(f"x_in{t}") for t in range(NT)]
        step = sem("dve_step")
        var_rdy = sem("var_rdy")
        rstd_rdy = sem("rstd_rdy")
        ln_rdy = sem("ln_rdy")
        h_st = sem("h_stored")
        t_rdy = sem("turn_ready")
        t_out = sem("turn_out")
        ang_rdy = sem("angles_ready")
        rope_rdy = sem("rope_tables")
        w_in_s = [sem(f"w_in{i}") for i in range(2)]
        pj_rdy = sem("proj_ready")
        pj_out = sem("proj_out")
        rope_own = sem("rope_steps")
        rope_own2 = sem("rope_steps_pool")
        rot_rdy = sem("rotated")
        l_rdy = sem("logits_ready")
        l_act = sem("logits_read_act")
        l_dve = sem("logits_read_dve")
        rel_rdy = sem("relu_ready")
        rel_used = sem("relu_used")
        iw_rdy = sem("iw_ready")
        wo_in = sem("wo_in")
        rows_in = sem("rows_in")
        mx_rdy = sem("max_ready")
        e_rdy = sem("exp_ready")
        cmb_rdy = sem("combined")
        pv_done = sem("pv_done")
        mix_rdy = sem("mix_ready")
        hin_s = sem("h_in")
        h1_rdy = sem("h1_ready")
        h1_st = sem("h1_stored")
        sq_rdy = sem("mean_square")
        rms_rdy = sem("rms_ready")
        lam_in = sem("lambda_sums")
        lam_out = sem("lambda_exps")
        y_fill = sem("unused_blocks_filled")
        rb_in = sem("router_bias_in")
        rc = sem("routing_consts")
        g8_rdy = sem("gates_by_slot_ready")
        sig_rdy = sem("sigmoid_ready")
        sel_rdy = sem("chosen_ready")
        pos_rdy = sem("places_ready")
        eob_rdy = sem("block_experts_ready")
        eob_row = sem("block_experts_row")
        tab_rdy = sem("tables_ready")
        w_slot = [sem(f"weights_in{i}") for i in range(NW)]
        w_rdy = sem("weights_ready")
        oh_rdy = sem("onehot_ready")
        tok_rdy = sem("tokens_psum")
        idx_rdy = sem("indices_ready")
        gb_own = sem("block_base")
        x_got = sem("rows_gathered")
        go = sem("gather_may_start")
        x_trn = sem("rows_transposed")
        xT_rdy = sem("rowsT_ready")
        up_done = sem("up_done")
        silu_rdy = sem("silu_ready")
        hid_rdy = sem("hidden_ready")
        hT_trn = sem("hidden_transposed")
        hT_rdy = sem("hiddenT_ready")
        down_done = sem("down_done")
        y_out = sem("y_read")
        y_st = sem("y_stored")
        ple_in = sem("ple_weights_in")
        row_in = [sem(f"tile_in{i}") for i in range(2)]
        y_in = [sem(f"y_in{i}") for i in range(TOPK)]
        y_used = sem("y_used")
        h2_rdy = sem("h2_ready")
        g_mm = sem("gate_products")
        z_rdy = sem("gate_argument")
        s_rdy = sem("gate_ready")
        o_rdy = sem("out_ready")
        o_st = [sem(f"out_stored{i}") for i in range(2)]

        block = ctx.enter_context(nc.Block())

        TASKS = [(t, k) for t in range(NT) for k in range(AH + BH)]
        NTK = len(TASKS)
        l_uses = []
        n_free = {"act": 0, "dve": 0, "exp": 0}

        def use_l(who):
            n_free[who] += 1
            l_uses.append((who, n_free[who]))

        for t in range(2, NT):
            for h in range(8):
                use_l("act")
        FINISH_AT = {1: "mix", 5: "rows"}
        order = []
        for i, (t, k) in enumerate(TASKS):
            order.append(("task", i))
            if t > 0 and k in FINISH_AT:
                order.append((FINISH_AT[k], t - 1))
        order += [("task", NTK), ("task", NTK + 1), ("mix", NT - 1), ("rows", NT - 1)]
        for what, i in order:
            if what == "task" and i < NTK:
                if TASKS[i][1] < AH:
                    use_l("dve")
                    n_free["exp"] += 1
                else:
                    use_l("exp")
                    use_l("exp")
            if what == "mix":
                use_l("dve")
        N_IDX = 6 * 8
        N_RC = 12
        T_LN = 2 * NT
        T_PROJ = NT * len(ROPED)

        def banks(t):
            return (t + 4) // 4

        prob_at, n = [], 0
        for t, k in TASKS:
            w = 1 if k < AH else 2
            prob_at.append([(n + j) % 4 for j in range(w)])
            n += w
        prob_owner = {}
        prob_prev = []
        for i, places in enumerate(prob_at):
            prob_prev.append(max([prob_owner.get(q, -1) for q in places]))
            for q in places:
                prob_owner[q] = i
        turned_at, u = {}, T_LN + T_PROJ
        for what, i in order:
            if what == "task" and 1 <= i <= NTK:
                u += banks(TASKS[i - 1][0])
                turned_at["task", i - 1] = u
            if what == "mix":
                u += 2
                turned_at["mix", i] = u
            if what == "rows":
                u += 3
                turned_at["rows", i] = u
        T_ALL = u

        def count_exp(i):
            t, k = TASKS[i] if i < NTK else (NT, 0)
            return t * (AH + 2 * BH) + (k if k < AH else AH + 2 * (k - AH))

        @block.sync
        def _(sp):
            for i, (dst, src) in enumerate([(g_emb, ln_emb_g), (b_emb, ln_emb_b), (inv, inv_freq)]):
                sp.dma_start(dst, src.rearrange("(a n) -> a n", a=1).broadcast_to([P, src.shape[0]])).then_inc(const_in, 16)
            sp.dma_start(posi, positions.rearrange("a (t q) -> q (a t)", q=P),
                         allow_slow_non_contiguous=True).then_inc(const_in, 16)
            for i, v in enumerate((lq1, lk1, lq2, lk2)):
                sp.dma_start(lam4[:, i, :], v.broadcast_to([P, HD])).then_inc(const_in, 16)
            sp.dma_start(subg, subln_g.broadcast_to([P, P])).then_inc(const_in, 16)
            for t in range(NT):
                sp.dma_start(h0[:, t, :], x_t[t]).then_inc(x_in[t], 16)
            for g, (_, c0, n) in enumerate(GROUPS):
                if g >= 2:
                    sp.wait_ge(pj_rdy, NT * (g - 1))
                sp.dma_start(w_sl[g % 2][:, :, 0:n], w_in_k[:, :, c0:c0 + n]).then_inc(w_in_s[g % 2], 16)
                if g == 0:
                    for t in range(NT):
                        sp.wait_ge(ln_rdy, t + 1)
                        sp.dma_start(h_d[t * P:(t + 1) * P, :], h0[:, t, :]).then_inc(h_st, 16)
            sp.wait_ge(pj_rdy, NT * NGR)
            sp.dma_start(wo, w_o_k).then_inc(wo_in, 16)
            sp.wait_ge(rel_used, N_IDX)
            sp.wait_ge(t_out, T_LN + T_PROJ)
            sp.wait_ge(h_st, 16 * NT)
            sp.dma_start(g1, ln1_g.broadcast_to([P, D])).then_inc(rows_in, 16)
            sp.dma_start(b1, ln1_b.broadcast_to([P, D])).then_inc(rows_in, 16)
            sp.dma_start(wr, w_r_k).then_inc(rows_in, 16)
            for t in range(NT):
                if t:
                    sp.wait_ge(h1_rdy, t)
                sp.dma_start(h_in, h_d[t * P:(t + 1) * P, :]).then_inc(hin_s, 16)
                b = SHB + NE + NT * t
                sp.dma_start(y_d[b * P:(b + NT) * P, :], x.rearrange("a s d -> (a s) d")).then_inc(y_fill, 16)
                sp.wait_ge(h1_rdy, t + 1)
                sp.dma_start(h1_d[t * P:(t + 1) * P, :], h1).then_inc(h1_st, 16)
            sp.wait_ge(h1_st, 16 * NT)
            sp.wait_ge(t_out, T_ALL)
            sp.wait_ge(pv_done, NTK)
            sp.dma_start(rbias, router_bias.broadcast_to([P, NE])).then_inc(rb_in, 16)

            def load_expert(e, slot):
                if isinstance(e, int) and e == 0:
                    srcs = (w_sg, w_su, w_sd)
                else:
                    srcs = (w_g_e[e - 1], w_u_e[e - 1], w_d_e[e - 1])
                for m, src in enumerate(srcs):
                    sp.dma_start(w_e[:, slot, 2048 * m:2048 * (m + 1)], src).then_inc(w_slot[slot], 16)

            for e in range(NW):
                load_expert(e, e)
            for dst, src in ((wpg, w_pg_k), (wpp, w_pp_k), (g2, ln2_g.broadcast_to([P, D])),
                             (b2, ln2_b.broadcast_to([P, D])), (bp, b_ple_gate.broadcast_to([P, D]))):
                sp.dma_start(dst, src).then_inc(ple_in, 16)
            sp.wait_ge(w_slot[0], 48)
            sp.sem_inc(w_rdy, 1)
            sp.wait_ge(tab_rdy, 3)

            def next_expert(n, j):
                sp.wait_ge(w_slot[(j + 1) % NW], 48 * (n + 1 + (j + 1) // NW))
                sp.sem_inc(w_rdy, 1)
                last = sp.value_load(bend_i[0:1, bass.ds(n * NW + j, 1)], min_val=SHB, max_val=MAXB)
                sp.wait_ge(down_done, last)
                load_expert(n * NW + j + NW, j)

            with sp.Fori(0, (NE - NW) // NW) as n:
                for j in range(NW):
                    next_expert(n, j)
            next_expert((NE - NW) // NW, 0)
            for e in range(NE - 2, NE + 1):
                sp.wait_ge(w_slot[e % NW], 48 * (e // NW + 1))
                sp.sem_inc(w_rdy, 1)
            n_blocks = sp.value_load(bend_i[0:1, NE:NE + 1], min_val=SHB, max_val=MAXB)
            sp.wait_ge(down_done, n_blocks)
            sp.wait_ge(y_st, n_blocks * 16 + 16)
            for t in range(NT + 2):
                if t < NT:
                    if t >= 2:
                        sp.wait_ge(o_rdy, t - 1)
                    ts = slice(t * P, (t + 1) * P)
                    for dst, src in ((acc[t % 2], h1_d[ts, :]), (ysh[t % 2], y_d[ts, :]), (pt_sb[t % 2], p_t[t])):
                        sp.dma_start(dst, src).then_inc(row_in[t % 2], 16)
                if t >= 2:
                    sp.wait_ge(o_rdy, t - 1)
                    sp.dma_start(out_t[t - 2], ot[t % 2]).then_inc(o_st[t % 2], 16)
            for i in range(2):
                sp.wait_ge(o_st[i], 16 * NT // 2)

        @block.gpsimd
        def _(pool):
            pool.memset(ident, 0.0).then_inc(consts, 1)
            pool.memset(rowneg, MASK).then_inc(consts, 1)
            pool.memset(colq[:, 0:CH], 1.0).then_inc(consts, 1)
            pool.memset(colq[:, CH:P], 0.0).then_inc(consts, 1)
            pool.memset(mhalf, -0.5).then_inc(consts, 1)
            pool.wait_ge(consts, 5)
            pool.affine_select(out=ident, in_=ident, compare_op=ALU.not_equal, fill=1.0, base=0,
                               pattern=[[-1, P]], channel_multiplier=1).then_inc(consts, 1)

            def rsqrt(n, src, dst, done):
                pool.wait_ge(src[1], n)
                pool.tensor_tensor(dst, src[0], mhalf[:, 0:dst.shape[1]], ALU.pow).then_inc(done, 1)

            pool.wait_ge(consts, 6)
            for t in range(NT):
                rsqrt(t + 1, (vareps[:, t % 2, :], var_rdy), rs[:, t % 2, :], rstd_rdy)
            n_rot = 2 * NT
            for g in ROPED[2:]:
                for t in range(NT):
                    u = (ROPED.index(g)) * NT + t
                    src, dst = raw[u % 2].rearrange("p (h j c) -> p h j c", j=2, c=HALF), rot[u % 2].rearrange("p (h j c) -> p h j c", j=2, c=HALF)
                    tmp = rot2.rearrange("p (h j c) -> p h j c", j=2, c=HALF)
                    pool.wait_ge(pj_out, g * NT + t + 1)
                    pool.wait_ge(t_rdy, T_LN + u - 1)
                    pool.wait_ge(rot_rdy, u)
                    if u == n_rot:
                        pool.wait_ge(rope_rdy, 2)
                    cb = cosd[:, t, :].rearrange("p (j c) -> p j c", j=2).unsqueeze(1).broadcast_to([P, 8, 2, HALF])
                    sb_ = sind[:, t, :].rearrange("p (j c) -> p j c", j=2).unsqueeze(1).broadcast_to([P, 8, 2, HALF])
                    pool.tensor_tensor(dst, src, cb, ALU.mult).then_inc(rope_own2, 1)
                    pool.tensor_tensor(tmp, src[:, :, ::-1, :], sb_, ALU.mult).then_inc(rope_own2, 1)
                    pool.wait_ge(rope_own2, 2 * (u - n_rot + 1))
                    pool.tensor_tensor(dst, dst, tmp, ALU.add).then_inc(rot_rdy, 1)
            for t in range(NT):
                rsqrt(t + 1, (ms, sq_rdy), rms, rms_rdy)
                rsqrt(NT + t + 1, (vareps[:, 0, :], var_rdy), rs[:, 0, :], rstd_rdy)

            pool.wait_ge(h1_rdy, NT)
            n_rc = [0]

            def const(ins):
                ins.then_inc(rc, 1)
                n_rc[0] += 1

            const(pool.iota(iota_s, [[1, P]], base=0, channel_multiplier=0, allow_small_or_imprecise_dtypes=True))
            const(pool.iota(slotm[:, :, 0], [[P, NT]], base=0, channel_multiplier=1, allow_small_or_imprecise_dtypes=True))
            const(pool.iota(thr, [[P, 7]], base=P, channel_multiplier=0, allow_small_or_imprecise_dtypes=True))
            const(pool.iota(itg, [[P, 2]], base=0, channel_multiplier=1, allow_small_or_imprecise_dtypes=True))
            const(pool.iota(tokpair[:, :, 0], [[P, NT]], base=0, channel_multiplier=0, allow_small_or_imprecise_dtypes=True))
            const(pool.iota(tokpair[:, :, 1], [[0, NT]], base=0, channel_multiplier=1, allow_small_or_imprecise_dtypes=True))
            const(pool.memset(zer, 0.0))
            const(pool.memset(ones_b, 1.0))
            const(pool.memset(upper_b, 1.0))
            const(pool.memset(tri, 1.0))
            pool.wait_ge(rc, n_rc[0])
            const(pool.affine_select(out=upper_b, in_=upper_b, compare_op=ALU.is_gt, fill=0.0, base=0,
                                     pattern=[[1, P]], channel_multiplier=-1))
            const(pool.affine_select(out=tri, in_=tri, compare_op=ALU.is_gt, fill=0.0, base=0,
                                     pattern=[[1, NG], [-1, NG]], channel_multiplier=0))
            assert n_rc[0] == N_RC

            def gather():
                pool.indirect_dma_start(out=xg, out_offset=None, in_=h1_d,
                                        in_offset=bass.IndirectOffsetOnAxis(ap=idx, axis=0)).then_inc(x_got, 16)

            pool.wait_ge(h1_st, 16 * NT)
            pool.wait_ge(idx_rdy, 1)
            gather()
            pool.wait_ge(idx_rdy, 2)
            pool.wait_ge(x_trn, 2)
            gather()
            pool.wait_ge(tab_rdy, 3)
            n_blocks = pool.value_load(bend_i[0:1, NE:NE + 1], min_val=SHB, max_val=MAXB)
            with pool.Fori(0, n_blocks) as g:
                pool.wait_ge(idx_rdy, g + 3)
                pool.wait_ge(x_trn, g * 2 + 4)
                pool.sem_inc(go, 1)
                gather()
            pool.wait_ge(y_st, n_blocks * 16 + 16)
            pool.wait_ge(x_got, n_blocks * 16 + 32)
            pool.sem_inc(go, 1)
            pool.wait_ge(g8_rdy, 1)

            def gather_y(t, ks):
                for k in ks:
                    if t:
                        pool.wait_ge(y_used, 8 * (t - 1) + k + 1)
                    pool.indirect_dma_start(out=yk[k], out_offset=None, in_=y_d,
                                            in_offset=bass.IndirectOffsetOnAxis(ap=slot8i[:, t, k:k + 1], axis=0)
                                            ).then_inc(y_in[k], 16)

            gather_y(0, range(TOPK))
            for t in range(NT):
                if t + 1 < NT:
                    gather_y(t + 1, range(4))
                rsqrt(2 * NT + t + 1, (vareps[:, 0, :], var_rdy), rs[:, 0, :], rstd_rdy)
                if t + 1 < NT:
                    gather_y(t + 1, range(4, TOPK))

        @block.scalar
        def _(act):
            act.wait_ge(ang_rdy, 1)
            act.activation(sind[:, :, HALF:HD], tr, ACT.Sin).then_inc(rope_rdy, 1)
            act.activation(cosd[:, :, 0:HALF], tc, ACT.Sin).then_inc(rope_rdy, 1)
            act.wait_ge(rope_rdy, 2)
            act.mul(sind[:, :, 0:HALF], sind[:, :, HALF:HD], -1.0).then_inc(rope_rdy, 1)
            act.copy(cosd[:, :, HALF:HD], cosd[:, :, 0:HALF]).then_inc(rope_rdy, 1)
            act.wait_ge(lam_in, 1)
            act.activation(lam2[:, 2:4], lam2[:, 0:2], ACT.Exp).then_inc(lam_out, 1)
            tu = [0]

            def turn_out(dst):
                act.wait_ge(t_rdy, tu[0] + 1)
                n = dst.free_size()
                src = tp[tu[0] % 2][:, 0:n]
                if len(dst.shape) == 3:
                    src = src.rearrange("p (a b) -> p a b", a=dst.shape[1])
                act.activation(dst, src, ACT.Copy).then_inc(t_out, 1)
                tu[0] += 1

            for t in range(NT):
                for b in range(2):
                    turn_out(hT[:, 4 * b:4 * b + 4, t * P:(t + 1) * P])
            dstT = {"qi": qiT, "qa": qaT, "ka": kaT, "qb": qbT, "kb": kbT}

            def group(g):
                name, c0, n = GROUPS[g]

                def turned(t):
                    ts = slice(t * P, (t + 1) * P)
                    turn_out(kiT[:, ts] if name == "ki" else dstT[name][:, :, ts])

                for t in range(NT):
                    u = g * NT + t
                    act.wait_ge(pj_rdy, u + 1)
                    if name[0] == "v":
                        dst = (va if name == "va" else vb)[:, t, :]
                    else:
                        r = ROPED.index(g) * NT + t
                        dst = raw[r % 2][:, 0:n]
                        if r >= 2:
                            act.wait_ge(rot_rdy, r - 1)
                    if name == "va" and t == 0:
                        act.wait_ge(h_st, 16 * NT)
                    act.activation(dst, pa[u % 2][:, 0:n], ACT.Copy).then_inc(pj_out, 1)
                    if name[0] != "v" and t >= 1:
                        turned(t - 1)
                if name[0] != "v":
                    turned(NT - 1)

            group(0)
            group(1)
            for u in range(N_IDX):
                t = 2 + u // 8
                n = P * (t + 1)
                act.wait_ge(l_rdy, u + 1)
                if u >= 2:
                    act.wait_ge(rel_used, u - 1)
                act.activation(rel[u % 2][:, 0:n], lg[u % 2][:, 0:n], ACT.Relu).then_inc(l_act, 1)
            for g in range(2, NGR):
                group(g)

            lu = N_IDX
            n_max = 0
            for what, i in order:
                if what == "task" and i < NTK:
                    t, k = TASKS[i]
                    n = P * (t + 1)
                    for j, q in enumerate(prob_at[i]):
                        n_max += 1
                        act.wait_ge(mx_rdy, n_max)
                        c = k if k < AH else AH + 2 * (k - AH) + j
                        if k < AH:
                            act.activation(prob[q][:, 0:n], prob[q][:, 0:n], ACT.Exp, bias=nmx[:, c:c + 1], scale=SCALE,
                                           accum_out=ssum[t % 2][:, c:c + 1]).then_inc(e_rdy, 1)
                        else:
                            if j == 0 and prob_prev[i] >= 0:
                                act.wait_ge(t_rdy, turned_at["task", prob_prev[i]])
                            act.activation(prob[q][:, 0:n], lg[lu % 2][:, 0:n], ACT.Exp, bias=nmx[:, c:c + 1], scale=SCALE,
                                           accum_out=ssum[t % 2][:, c:c + 1]).then_inc(e_rdy, 1)
                        lu += 1
                if what == "task" and 1 <= i <= NTK:
                    t, k = TASKS[i - 1]
                    if i - 1 >= 2:
                        act.wait_ge(pv_done, i - 2)
                    for b in range(banks(t)):
                        turn_out(pT[(i - 1) % 2][:, 4 * b:min(4 * b + 4, t + 1), :])
                if what == "mix":
                    turn_out(mixT[:, 0:4, :])
                    turn_out(mixT[:, 4:8, :])
                    lu += 1
                if what == "rows":
                    turn_out(mixT[:, 0:4, :])
                    turn_out(mixT[:, 4:8, :])
                    turn_out(rl[:, i, :])

            act.wait_ge(t_out, T_ALL)
            act.activation(sig, rl, ACT.Sigmoid).then_inc(sig_rdy, 1)

            def rows_out(first):
                for b in range(2):
                    act.wait_ge(x_trn, first + b)
                    act.activation(xT[:, 4 * b:4 * b + 4, :], tp[b].rearrange("p (a b) -> p a b", b=P), ACT.Copy).then_inc(xT_rdy, 1)

            rows_out(1)
            act.wait_ge(tab_rdy, 3)
            n_blocks = act.value_load(bend_i[0:1, NE:NE + 1], min_val=SHB, max_val=MAXB)
            act.wait_ge(y_fill, 16 * (MAXB - SHB - NE) // NT)
            act.sem_inc(y_st, 16)
            with act.Fori(0, n_blocks) as g:
                act.wait_ge(up_done, g + 1)
                act.activation(sg, lg[0][:, 0:ED], ACT.Silu).then_inc(silu_rdy, 1)
                rows_out(g * 2 + 3)
                act.wait_ge(y_out, g + 2)
                act.dma_start(y_d[bass.ds(g * P, P), :], y_sb).then_inc(y_st, 16)

            tu[0] = 0
            base = n_blocks * 2 + 2

            def turn_out2(dst):
                act.wait_ge(x_trn, base + tu[0] + 1)
                n = dst.free_size()
                act.activation(dst, tp[tu[0] % 2][:, 0:n].rearrange("p (a b) -> p a b", b=P), ACT.Copy).then_inc(xT_rdy, 1)
                tu[0] += 1

            for t in range(NT):
                if t:
                    act.wait_ge(g_mm, t)
                turn_out2(ppT)
                turn_out2(h2T[:, 0:4, :])
                turn_out2(h2T[:, 4:8, :])
                act.wait_ge(z_rdy, t + 1)
                act.activation(zt, zt, ACT.Sigmoid).then_inc(s_rdy, 1)

        @block.tensor
        def _(pe):
            tu = [0]

            def turn(srcs, idn, done=True):
                if tu[0] >= 2:
                    pe.wait_ge(t_out, tu[0] - 1)
                for j, s_ in enumerate(srcs):
                    m = pe.transpose(tp[tu[0] % 2][0:s_.shape[1], j * P:j * P + P], s_, idn)
                m.then_inc(t_rdy, 1)
                tu[0] += 1

            pe.wait_ge(consts, 6)
            for t in range(NT):
                pe.wait_ge(ln_rdy, t + 1)
                for b in range(2):
                    turn([h0[:, t, (4 * b + j) * P:(4 * b + j + 1) * P] for j in range(4)], ident)

            def turn_rot(r):
                pe.wait_ge(rot_rdy, r + 1)
                if GROUPS[ROPED[r // NT]][0] == "ki":
                    turn([rot[r % 2][:, 0:P]], ident)
                else:
                    turn([rot[r % 2][:, j * P:(j + 1) * P] for j in range(4)], ident)

            def group(g):
                name, c0, n = GROUPS[g]
                pe.wait_ge(w_in_s[g % 2], 16 * (g // 2 + 1))
                for t in range(NT):
                    u = g * NT + t
                    if g == 0:
                        pe.wait_ge(t_out, 2 * t + 2)
                    if u >= 2:
                        pe.wait_ge(pj_out, u - 1)
                    for k in range(KC):
                        m = pe.matmul(pa[u % 2][:, 0:n], hT[:, k, t * P:(t + 1) * P], w_sl[g % 2][:, k, 0:n],
                                      start=(k == 0), stop=(k == KC - 1))
                    m.then_inc(pj_rdy, 1)
                    if g in ROPED and t >= 1:
                        turn_rot(ROPED.index(g) * NT + t - 1)
                if g in ROPED:
                    turn_rot(ROPED.index(g) * NT + NT - 1)

            lu = [0]

            def next_l():
                u = lu[0]
                lu[0] += 1
                if u >= 2:
                    who, c = l_uses[u - 2]
                    pe.wait_ge({"act": l_act, "dve": l_dve, "exp": e_rdy}[who], c)
                return lg[u % 2]

            group(0)
            group(1)
            pe.wait_ge(t_out, T_LN + 2 * NT)
            for t in range(2, NT):
                for h in range(8):
                    o, n = next_l(), P * (t + 1)
                    r = slice(HD * (h % 2), HD * (h % 2) + HD)
                    for c in range(0, n, 512):
                        e = min(c + 512, n)
                        m = pe.matmul(o[:, c:e], qiT[r, h // 2, t * P:(t + 1) * P], kiT[r, c:e], start=True, stop=True)
                    m.then_inc(l_rdy, 1)
            for g in range(2, NGR):
                group(g)
            pe.wait_ge(t_out, T_LN + T_PROJ)

            def logits(i):
                t, k = TASKS[i]
                n = P * (t + 1)
                ts = slice(t * P, (t + 1) * P)
                for j in range(1 if k < AH else 2):
                    o = next_l()
                    if k < AH:
                        r, c, qT, kT = slice(HD * (k % 2), HD * (k % 2) + HD), k // 2, qaT, kaT
                    else:
                        r, c, qT, kT = slice(HD * j, HD * j + HD), k - AH, qbT, kbT
                    full = n if k < AH else n - CH
                    for a in range(0, full, 512):
                        e = min(a + 512, full)
                        m = pe.matmul(o[:, a:e], qT[r, c, ts], kT[r, c, a:e], start=True, stop=True)
                    if k >= AH:
                        pe.matmul(o[:, full:n], qT[r, c, ts], kT[r, c, full:n], start=True, stop=False)
                        m = pe.matmul(o[:, full:n], colq[0:1, :], rowneg[0:1, :], start=False, stop=True)
                    m.then_inc(l_rdy, 1)

            def values(i):
                t, k = TASKS[i]
                pe.wait_ge(t_out, turned_at["task", i])
                if k == 0 and t > 0:
                    pe.wait_ge(mix_rdy, t)
                for b in range(t + 1):
                    if k < AH:
                        o, v = pa[0][:, k * HD:(k + 1) * HD], va[:, b, k * HD:(k + 1) * HD]
                    else:
                        o, v = pa[1][:, (k - AH) * P:(k - AH + 1) * P], vb[:, b, (k - AH) * P:(k - AH + 1) * P]
                    m = pe.matmul(o, pT[i % 2][:, b, :], v, start=(b == 0), stop=(b == t))
                m.then_inc(pv_done, 1)

            def turn_prob(i):
                t, k = TASKS[i]
                if k < AH:
                    pe.wait_ge(e_rdy, count_exp(i) + 1)
                else:
                    pe.wait_ge(cmb_rdy, BH * t + k - AH + 1)
                q = prob[prob_at[i][0]]
                for b in range(banks(t)):
                    turn([q[:, c * P:(c + 1) * P] for c in range(4 * b, min(4 * b + 4, t + 1))], ident)

            for what, i in order:
                if what == "task":
                    if i < NTK:
                        logits(i)
                    if 2 <= i:
                        values(i - 2)
                    if 1 <= i <= NTK:
                        turn_prob(i - 1)
                if what == "mix":
                    pe.wait_ge(mix_rdy, i + 1)
                    for b in range(2):
                        turn([mix[:, (4 * b + j) * P:(4 * b + j + 1) * P] for j in range(4)], ident)
                    pe.wait_ge(t_out, turned_at["mix", i])
                    if i == 0:
                        pe.wait_ge(wo_in, 16)
                    o = next_l()
                    for c in range(2):
                        for k in range(KC):
                            m = pe.matmul(o[:, c * 512:(c + 1) * 512], mixT[:, k, :], wo[:, k, c * 512:(c + 1) * 512],
                                          start=(k == 0), stop=(k == KC - 1))
                    m.then_inc(l_rdy, 1)
                if what == "rows":
                    pe.wait_ge(h1_rdy, i + 1)
                    for b in range(2):
                        turn([h1[:, (4 * b + j) * P:(4 * b + j + 1) * P] for j in range(4)], ident)
                    pe.wait_ge(t_out, turned_at["rows", i] - 1)
                    if i == 0:
                        pe.wait_ge(rows_in, 48)
                    for k in range(KC):
                        m = pe.matmul(tp[tu[0] % 2][:, 0:NE], mixT[:, k, :], wr[:, k, :], start=(k == 0), stop=(k == KC - 1))
                    m.then_inc(t_rdy, 1)
                    tu[0] += 1

            pe.wait_ge(sel_rdy, 1)
            pe.wait_ge(rc, N_RC)
            for t in range(NT):
                for s_ in range(t + 1):
                    pe.matmul(lg[0][:, t * NE:(t + 1) * NE], (upper_b if s_ == t else ones_b), sel_b[:, s_, :],
                              start=(s_ == 0), stop=(s_ == t))
            for t in range(NT):
                m = pe.matmul(lg[1][:, 0:NE], ones_b, sel_b[:, t, :], start=(t == 0), stop=(t == NT - 1))
            m.then_inc(pos_rdy, 1)
            pe.wait_ge(eob_rdy, 1)
            for c in range(2):
                m = pe.transpose(lg[1][0:1, 512 + c * P:512 + (c + 1) * P], eobc[:, c:c + 1], ident)
            m.then_inc(eob_row, 1)

            def tokens(j):
                pe.wait_ge(oh_rdy, j)
                for t in range(NT):
                    m = pe.matmul(pa[0][:, 0:2], onehot[:, t, :], tokpair[:, t, :], start=(t == 0), stop=(t == NT - 1))
                m.then_inc(tok_rdy, 1)

            def turn_rows(n):
                pe.wait_ge(x_got, 16 * n)
                for b in range(2):
                    for k in range(4):
                        m = pe.transpose(tp[b][:, k * P:(k + 1) * P], xg_v[:, 4 * b + k, :], ident)
                    m.then_inc(x_trn, 1)

            tokens(1)
            pe.wait_ge(t_out, T_ALL)
            turn_rows(1)
            tokens(2)
            pe.wait_ge(tab_rdy, 3)
            n_blocks = pe.value_load(bend_i[0:1, NE:NE + 1], min_val=SHB, max_val=MAXB)
            with pe.Fori(0, n_blocks) as g:
                e = pe.value_load(tab[0:1, 0, bass.ds(g, 1)], min_val=0, max_val=NE)
                place = pe.value_load(tab[0:1, 1, bass.ds(g, 1)], min_val=0, max_val=NW - 1)
                pe.wait_ge(w_rdy, e + 1)
                pe.wait_ge(xT_rdy, g * 2 + 2)
                for k in range(KC):
                    m = pe.matmul(lg[0][:, 0:2 * ED].rearrange("p (j f) -> p j f", j=2), xT[:, k, :], w_up_v[:, place, :, k, :],
                                  start=(k == 0), stop=(k == KC - 1))
                m.then_inc(up_done, 1)
                tokens(g + 3)
                pe.wait_ge(xT_rdy, g * 2 + 2)
                turn_rows(g + 2)
                pe.wait_ge(hid_rdy, g + 1)
                for j in range(2):
                    m = pe.transpose(pa[1][:, j * P:(j + 1) * P], hid_v[:, j, :], ident)
                m.then_inc(hT_trn, 1)
                pe.wait_ge(hT_rdy, g + 1)
                pe.wait_ge(y_out, g + 1)
                for c in range(2):
                    for j in range(2):
                        m = pe.matmul(lg[1][:, c * 512:(c + 1) * 512], hidT[:, j, :], w_dn_v[:, place, j, c * 512:(c + 1) * 512],
                                      start=(j == 0), stop=(j == 1))
                m.then_inc(down_done, 1)

            tu[0] = 0
            base = n_blocks * 2 + 2

            def turn2(srcs):
                pe.wait_ge(xT_rdy, base + max(tu[0] - 1, 0))
                for j, s_ in enumerate(srcs):
                    m = pe.transpose(tp[tu[0] % 2][:, j * P:(j + 1) * P], s_, ident)
                m.then_inc(x_trn, 1)
                tu[0] += 1

            pe.wait_ge(ple_in, 16 * 5)
            pe.wait_ge(y_out, n_blocks + 1)
            for t in range(NT):
                pe.wait_ge(row_in[t % 2], 48 * (t // 2 + 1))
                turn2([pt_sb[t % 2][:, j * P:(j + 1) * P] for j in range(2)])
                pe.wait_ge(h2_rdy, t + 1)
                for b in range(2):
                    turn2([acc[t % 2][:, (4 * b + j) * P:(4 * b + j + 1) * P] for j in range(4)])
                if t:
                    pe.wait_ge(o_rdy, t)
                pe.wait_ge(xT_rdy, base + tu[0])
                for dst, a_T, w, n in ((lg[0], h2T, wpg, KC), (lg[1], ppT, wpp, 2)):
                    for c in range(2):
                        for k in range(n):
                            m = pe.matmul(dst[:, c * 512:(c + 1) * 512], a_T[:, k, :], w[:, k, c * 512:(c + 1) * 512],
                                          start=(k == 0), stop=(k == n - 1))
                m.then_inc(g_mm, 1)

        @block.vector
        def _(dve):
            n_step = [0]

            def link(ins):
                ins.then_inc(step, 1)
                n_step[0] += 1
                dve.wait_ge(step, n_step[0])

            n_var = [0]

            def layer_norm(src, dst, g, b, slot, done, middle=lambda: None):
                dve.bn_stats(stats[:, 0, :], src[:, 0:512]).then_inc(step, 1)
                n_step[0] += 1
                link(dve.bn_stats(stats[:, 1, :], src[:, 512:1024]))
                link(dve.bn_aggr(mv, stats))
                dve.tensor_scalar(vareps[:, slot, :], mv[:, 1:2], EPS, None, ALU.add).then_inc(var_rdy, 1)
                n_var[0] += 1
                dve.wait_ge(rstd_rdy, n_var[0])
                link(dve.tensor_scalar(dst, src, mv[:, 0:1], rs[:, slot, :], ALU.subtract, ALU.mult))
                link(dve.tensor_tensor(dst, dst, g, ALU.mult))
                dve.tensor_tensor(dst, dst, b, ALU.add).then_inc(done, 1)

            dve.wait_ge(const_in, 16 * 9)
            link(dve.tensor_copy(posf, posi))
            link(dve.tensor_tensor(ang, posf.unsqueeze(2).broadcast_to([P, NT, HALF]),
                                   inv.unsqueeze(1).broadcast_to([P, NT, HALF]), ALU.mult))
            MAGIC = 1.5 * 2.0 ** 23
            TWO_PI = 6.283185307179586
            parts = [6.28125, 0.00193500518798828125, 3.0199159819567e-07]
            link(dve.tensor_scalar(tn, ang, 1.0 / TWO_PI, MAGIC, ALU.mult, ALU.add))
            link(dve.tensor_scalar(tn, tn, -MAGIC, None, ALU.add))
            src = ang
            for c in parts:
                link(dve.scalar_tensor_tensor(tr, tn, -c, src, ALU.mult, ALU.add))
                src = tr
            link(dve.tensor_scalar(tc, tr, TWO_PI / 4, None, ALU.add))
            link(dve.tensor_scalar(tw, tc, TWO_PI / 2, -TWO_PI, ALU.is_gt, ALU.mult))
            link(dve.tensor_tensor(tc, tc, tw, ALU.add))
            PI_IN = 3.1415925
            link(dve.tensor_scalar(tr, tr, PI_IN, -PI_IN, ALU.min, ALU.max))
            dve.tensor_scalar(tc, tc, PI_IN, -PI_IN, ALU.min, ALU.max).then_inc(ang_rdy, 1)
            link(dve.tensor_tensor(lam4[:, 0, :], lam4[:, 0, :], lam4[:, 1, :], ALU.mult))
            link(dve.tensor_tensor(lam4[:, 1, :], lam4[:, 2, :], lam4[:, 3, :], ALU.mult))
            dve.tensor_reduce(lam2[:, 0:2], lam4[:, 0:2, :], AX.X, ALU.add).then_inc(lam_in, 1)
            dve.wait_ge(lam_out, 1)
            link(dve.tensor_tensor(neglam, lam2[:, 3:4], lam2[:, 2:3], ALU.subtract))
            link(dve.tensor_scalar(neglam, neglam, -LAMBDA_INIT, None, ALU.add))
            link(dve.tensor_scalar(subg, subg, 1.0 - LAMBDA_INIT, None, ALU.mult))
            for t in range(NT):
                dve.wait_ge(x_in[t], 16)
                layer_norm(h0[:, t, :], h0[:, t, :], g_emb, b_emb, t % 2, ln_rdy)
            dve.wait_ge(rope_rdy, 4)
            n_own = 0
            for g in ROPED[:2]:
                for t in range(NT):
                    r = ROPED.index(g) * NT + t
                    nh = 8 if g == 0 else 1
                    src = raw[r % 2][:, 0:nh * HD].rearrange("p (h j c) -> p h j c", j=2, c=HALF)
                    dst = rot[r % 2][:, 0:nh * HD].rearrange("p (h j c) -> p h j c", j=2, c=HALF)
                    tmp = rot2[:, 0:nh * HD].rearrange("p (h j c) -> p h j c", j=2, c=HALF)
                    dve.wait_ge(pj_out, g * NT + t + 1)
                    if r >= 2:
                        dve.wait_ge(t_rdy, T_LN + r - 1)
                    if r >= 1:
                        dve.wait_ge(rot_rdy, r)
                    cb = cosd[:, t, :].rearrange("p (j c) -> p j c", j=2).unsqueeze(1).broadcast_to([P, nh, 2, HALF])
                    sb_ = sind[:, t, :].rearrange("p (j c) -> p j c", j=2).unsqueeze(1).broadcast_to([P, nh, 2, HALF])
                    dve.tensor_tensor(dst, src, cb, ALU.mult).then_inc(rope_own, 1)
                    dve.tensor_tensor(tmp, src[:, :, ::-1, :], sb_, ALU.mult).then_inc(rope_own, 1)
                    n_own += 2
                    dve.wait_ge(rope_own, n_own)
                    if g == 0:
                        dve.tensor_tensor(dst, dst, tmp, ALU.add).then_inc(rot_rdy, 1)
                    else:
                        dve.tensor_scalar(iws[:, t, :], raw[r % 2][:, HD:HD + 8], WSCALE, None, ALU.mult).then_inc(iw_rdy, 1)
                        link(dve.tensor_tensor(dst, dst, tmp, ALU.add))
                        dve.tensor_copy(rot[r % 2][:, HD:2 * HD], rot[r % 2][:, 0:HD]).then_inc(rot_rdy, 1)
            dve.wait_ge(iw_rdy, NT)
            for u in range(N_IDX):
                t, h = 2 + u // 8, u % 8
                n = P * (t + 1)
                dve.wait_ge(l_act, u + 1)
                if u:
                    dve.wait_ge(rel_used, u)
                if h == 0:
                    dve.tensor_scalar(score[t], rel[u % 2][:, 0:n], iws[:, t, h:h + 1], None, ALU.mult).then_inc(rel_used, 1)
                else:
                    dve.scalar_tensor_tensor(score[t], rel[u % 2][:, 0:n], iws[:, t, h:h + 1], score[t], ALU.mult,
                                             ALU.add).then_inc(rel_used, 1)
            dve.wait_ge(rel_used, N_IDX)
            for t in range(NT):
                n = P * (t + 1)
                if t < 2:
                    link(dve.memset(score[t], 0.0))
                    link(dve.memset(score[t][0:CH, n - CH:n], MASK))
                    continue
                link(dve.memset(score[t][0:CH, n - CH:n], FILL))
                for _ in range(NKEEP // 8):
                    link(dve.max(m8, score[t]))
                    link(dve.match_replace(score[t], m8, score[t], TAKEN))
                link(dve.tensor_scalar(score[t], score[t], 0.5 * (FILL + TAKEN), MASK, ALU.is_gt, ALU.mult))

            lu = N_IDX
            n_exp = 0
            n_dl = [0]
            for what, i in order:
                if what == "task" and i < NTK:
                    t, k = TASKS[i]
                    n = P * (t + 1)
                    if k < AH:
                        q = prob[prob_at[i][0]]
                        dve.wait_ge(l_rdy, lu + 1)
                        if prob_prev[i] >= 0:
                            dve.wait_ge(t_rdy, turned_at["task", prob_prev[i]])
                        dve.tensor_tensor_reduce(out=q[:, 0:n], in0=lg[lu % 2][:, 0:n], in1=score[t], scale=1.0,
                                                 scalar=-3.0e38, op0=ALU.add, op1=ALU.max,
                                                 accum_out=mx[:, k:k + 1]).then_inc(l_dve, 1)
                        n_dl[0] += 1
                        dve.wait_ge(l_dve, n_dl[0])
                        dve.tensor_scalar(nmx[:, k:k + 1], mx[:, k:k + 1], -SCALE, None, ALU.mult).then_inc(mx_rdy, 1)
                        lu += 1
                        n_exp += 1
                    else:
                        for j in range(2):
                            c = AH + 2 * (k - AH) + j
                            dve.wait_ge(l_rdy, lu + 1)
                            link(dve.tensor_reduce(mx[:, c:c + 1], lg[lu % 2][:, 0:n], AX.X, ALU.max))
                            dve.tensor_scalar(nmx[:, c:c + 1], mx[:, c:c + 1], -SCALE, None, ALU.mult).then_inc(mx_rdy, 1)
                            lu += 1
                        n_exp += 2
                        dve.wait_ge(e_rdy, n_exp)
                        s = ssum[t % 2]
                        p0, p1 = (prob[q][:, 0:n] for q in prob_at[i])
                        link(dve.reciprocal(rsum[:, c:c + 1], s[:, c:c + 1]))
                        link(dve.scalar_tensor_tensor(cB[:, 0:1], s[:, c - 1:c], neglam, rsum[:, c:c + 1], ALU.mult, ALU.mult))
                        dve.scalar_tensor_tensor(p0, p1, cB[:, 0:1], p0, ALU.mult, ALU.add).then_inc(cmb_rdy, 1)
                        dve.wait_ge(cmb_rdy, BH * t + k - AH + 1)
                if what == "task" and i >= 2 and TASKS[i - 2][1] == AH + BH - 1:
                    t = TASKS[i - 2][0]
                    s = ssum[t % 2]
                    dve.wait_ge(pv_done, i - 1)
                    dve.wait_ge(e_rdy, (t + 1) * 16)
                    link(dve.reciprocal(rsum, s))
                    link(dve.tensor_tensor(mix[:, 0:512].rearrange("p (h c) -> p h c", h=AH),
                                           pa[0][:, :].rearrange("p (h c) -> p h c", h=AH),
                                           rsum[:, 0:AH].unsqueeze(2).broadcast_to([P, AH, HD]), ALU.mult))
                    mb = mix[:, 512:1024].rearrange("p (h c) -> p h c", h=BH)
                    link(dve.tensor_tensor(mb, pa[1][:, :].rearrange("p (h c) -> p h c", h=BH),
                                           rsum[:, AH:AH + 2 * BH:2].unsqueeze(2).broadcast_to([P, BH, P]), ALU.mult))
                    link(dve.tensor_tensor(sq, mb, mb, ALU.mult))
                    link(dve.tensor_reduce(ms, sq, AX.X, ALU.add))
                    dve.tensor_scalar(ms, ms, 1.0 / P, EPS, ALU.mult, ALU.add).then_inc(sq_rdy, 1)
                    dve.wait_ge(rms_rdy, t + 1)
                    link(dve.tensor_tensor(mb, mb, rms.unsqueeze(2).broadcast_to([P, BH, P]), ALU.mult))
                    dve.tensor_tensor(mb, mb, subg.unsqueeze(1).broadcast_to([P, BH, P]), ALU.mult).then_inc(mix_rdy, 1)
                if what == "mix":
                    dve.wait_ge(l_rdy, lu + 1)
                    dve.wait_ge(hin_s, 16 * (i + 1))
                    if i:
                        dve.wait_ge(h1_st, 16 * i)
                        dve.wait_ge(t_rdy, turned_at["rows", i - 1])
                    else:
                        dve.wait_ge(rows_in, 48)
                    dve.scalar_tensor_tensor(h1, h_in, ALPHA, lg[lu % 2][:, :], ALU.mult, ALU.add).then_inc(l_dve, 1)
                    n_dl[0] += 1
                    dve.wait_ge(l_dve, n_dl[0])
                    lu += 1
                    layer_norm(h1, h1, g1, b1, 0, h1_rdy)

            def bc(v, dims, *axes):
                for ax in axes:
                    v = v.unsqueeze(ax)
                return v.broadcast_to([P, *dims])

            dve.wait_ge(sig_rdy, 1)
            dve.wait_ge(rb_in, 16)
            dve.wait_ge(rc, N_RC)
            link(dve.tensor_tensor(biased, sig, bc(rbias, (NT, NE), 1), ALU.add))
            b_g = biased.rearrange("p t (g e) -> p (t g) e", g=NG)
            for i in range(NT * NG):
                m = dve.max(g8[:, i, :], b_g[:, i, :])
            link(m)
            gs_f = gs.rearrange("p t g -> p (t g)")
            link(dve.tensor_tensor(gs_f, g8[:, :, 0], g8[:, :, 1], ALU.add))
            shape4 = dict(t=NT, g=NG)
            t1, t2 = (v.rearrange("p (t g e) -> p t g e", **shape4) for v in (tmp1, tmp2))
            other, own = bc(gs, (NT, NG, NG), 2), bc(gs, (NT, NG, NG), 3)
            link(dve.tensor_tensor(t1, other, own, ALU.is_gt))
            link(dve.tensor_tensor(t2, other, own, ALU.is_equal))
            link(dve.tensor_tensor(t2, t2, bc(tri, (NT, NG, NG), 1), ALU.mult))
            link(dve.tensor_tensor(t1, t1, t2, ALU.add))
            link(dve.tensor_reduce(gpen, t1, AX.X, ALU.add))
            link(dve.tensor_scalar(gpen, gpen, float(TOPG), -MASK, ALU.is_lt, ALU.mult))
            link(dve.tensor_scalar(gpen, gpen, MASK, None, ALU.add))
            b4 = biased.rearrange("p t (g e) -> p t g e", g=NG)
            link(dve.tensor_tensor(b4, b4, bc(gpen, (NT, NG, NG), 3), ALU.add))
            for t in range(NT):
                m = dve.max(g8[:, t, :], biased[:, t, :])
            link(m)
            for t in range(NT):
                m = dve.match_replace(biased[:, t, :], g8[:, t, :], biased[:, t, :], FILL)
            link(m)
            chosen = tmp1.rearrange("p (t e) -> p t e", t=NT)
            link(dve.tensor_scalar(chosen, biased, 0.1 * FILL, None, ALU.is_lt))
            dve.tensor_copy(sel_b, chosen).then_inc(sel_rdy, 1)
            link(dve.tensor_tensor(gate, sig, chosen, ALU.mult))
            link(dve.tensor_reduce(den8, gate, AX.X, ALU.add))
            link(dve.reciprocal(den8, den8))
            link(dve.tensor_scalar(den8, den8, ROUTED, None, ALU.mult))
            link(dve.tensor_tensor(gate, gate, bc(den8, (NT, NE), 2), ALU.mult))
            dve.wait_ge(pos_rdy, 1)
            over = tmp2[:, 0:NE * 7].rearrange("p (e k) -> p e k", k=7)
            link(dve.tensor_tensor(over, bc(lg[1][:, 0:NE], (NE, 7), 2), bc(thr, (NE, 7), 1), ALU.is_gt))
            link(dve.tensor_reduce(nblk, over, AX.X, ALU.add))
            link(dve.tensor_scalar(nblk, nblk, 1.0, None, ALU.add))
            link(dve.memset(bend[:, 0:1], float(SHB)))
            link(dve.tensor_tensor_scan(bend[:, 1:NE + 1], nblk, zer, float(SHB), ALU.add, ALU.add))
            ends = tmp3[:, 0:2 * (NE + 1)].rearrange("p (c e) -> p c e", c=2)
            link(dve.tensor_tensor(ends, bc(bend, (2, NE + 1), 1), bc(itg, (2, NE + 1), 2), ALU.is_le))
            link(dve.tensor_reduce(eobc, ends, AX.X, ALU.add))
            dve.tensor_scalar(eobc, eobc, float(NE), None, ALU.min).then_inc(eob_rdy, 1)
            link(dve.tensor_tensor(nblk, bend[:, 1:NE + 1], nblk, ALU.subtract))
            link(dve.tensor_scalar(nblk, nblk, float(P), 1.0, ALU.mult, ALU.add))
            pos = tmp2.rearrange("p (t e) -> p t e", t=NT)
            link(dve.tensor_tensor(pos, lg[0][:, 0:512].rearrange("p (t e) -> p t e", t=NT), bc(nblk, (NT, NE), 1), ALU.add))
            link(dve.tensor_tensor(pos, pos, chosen, ALU.mult))
            link(dve.tensor_scalar(slotm[:, :, 1:NE + 1], pos, -1.0, None, ALU.add))
            dve.wait_ge(eob_row, 1)
            dve.tensor_copy(bend_i[0:1, :], bend[0:1, :]).then_inc(tab_rdy, 1)
            dve.tensor_copy(tab[0:1, 0, :], lg[1][0:1, 512:512 + 2 * P]).then_inc(tab_rdy, 1)
            dve.wait_ge(tab_rdy, 2)
            dve.tensor_scalar(tab[0:1, 1, :], tab[0:1, 0, :], NW - 1, None, ALU.bitwise_and).then_inc(tab_rdy, 1)
            dve.wait_ge(tab_rdy, 3)

            def one_hot(j, e):
                dve.scalar_tensor_tensor(onehot, bc(slotm[:, :, e], (NT, P), *(() if isinstance(e, int) else ()), 2) if isinstance(e, int)
                                         else slotm[:, :, bass.ds(e, 1)].broadcast_to([P, NT, P]), gbase,
                                         bc(iota_s, (NT, P), 1), ALU.subtract, ALU.is_equal).then_inc(oh_rdy, 1)
                dve.wait_ge(oh_rdy, j)
                dve.tensor_scalar(gbase, gbase, float(P), None, ALU.add).then_inc(gb_own, 1)

            def indices(j):
                dve.wait_ge(tok_rdy, j)
                dve.tensor_scalar(idx, pa[0][:, 0:1], pa[0][:, 1:2], None, ALU.add).then_inc(idx_rdy, 1)

            dve.memset(gbase, 0.0).then_inc(gb_own, 1)
            dve.wait_ge(gb_own, 1)
            one_hot(1, 0)
            indices(1)
            dve.wait_ge(gb_own, 2)
            one_hot(2, 0)
            dve.wait_ge(x_got, 16)
            indices(2)
            for t in range(NT):
                m = dve.max(slot8[:, t, :], slotm[:, t, 1:NE + 1])
            link(m)
            link(dve.tensor_copy(slot8i, slot8))
            hit = tmp1.rearrange("p (k e) -> p k e", k=TOPK)
            for t in range(NT):
                link(dve.tensor_tensor(hit, bc(slotm[:, t, 1:NE + 1], (TOPK, NE), 1), bc(slot8[:, t, :], (TOPK, NE), 2), ALU.is_equal))
                link(dve.tensor_tensor(hit, hit, bc(gate[:, t, :], (TOPK, NE), 1), ALU.mult))
                m = dve.tensor_reduce(gate8[:, t, :], hit, AX.X, ALU.add)
                if t < NT - 1:
                    link(m)
            m.then_inc(g8_rdy, 1)
            n_blocks = dve.value_load(bend_i[0:1, NE:NE + 1], min_val=SHB, max_val=MAXB)
            dve.sem_inc(y_out, 1)
            with dve.Fori(0, n_blocks) as g:
                e2 = dve.value_load(tab[0:1, 0, bass.ds(g + 2, 1)], min_val=0, max_val=NE)
                dve.wait_ge(tok_rdy, g + 2)
                dve.wait_ge(gb_own, g + 3)
                one_hot(g + 3, e2)
                dve.wait_ge(x_got, g * 16 + 32)
                indices(g + 3)
                dve.wait_ge(silu_rdy, g + 1)
                dve.tensor_tensor(hid, sg, lg[0][:, ED:2 * ED], ALU.mult).then_inc(hid_rdy, 1)
                dve.wait_ge(hT_trn, g + 1)
                dve.tensor_copy(hidT, pa[1][:, 0:2 * P].rearrange("p (j q) -> p j q", j=2)).then_inc(hT_rdy, 1)
                dve.wait_ge(down_done, g + 1)
                dve.wait_ge(y_st, g * 16 + 16)
                dve.tensor_copy(y_sb, lg[1][:, :]).then_inc(y_out, 1)

            dve.wait_ge(ple_in, 16 * 5)

            def finish(t):
                a = acc[t % 2]
                dve.wait_ge(g_mm, t + 1)
                if t:
                    dve.wait_ge(o_rdy, t)
                dve.tensor_tensor(zt, lg[0][:, :], bp, ALU.add).then_inc(z_rdy, 1)
                dve.wait_ge(s_rdy, t + 1)
                if t >= 2:
                    dve.wait_ge(o_st[t % 2], 16 * (t // 2))
                link(dve.tensor_tensor(ot[t % 2], zt, lg[1][:, :], ALU.mult))
                dve.tensor_tensor(ot[t % 2], ot[t % 2], a, ALU.add).then_inc(o_rdy, 1)

            for t in range(NT):
                a = acc[t % 2]
                dve.wait_ge(row_in[t % 2], 48 * (t // 2 + 1))
                link(dve.scalar_tensor_tensor(a, a, ALPHA, ysh[t % 2], ALU.mult, ALU.add))
                for k in range(TOPK):
                    dve.wait_ge(y_in[k], 16 * (t + 1))
                    dve.scalar_tensor_tensor(a, yk[k], gate8[:, t, k:k + 1], a, ALU.mult, ALU.add).then_inc(y_used, 1)
                    dve.wait_ge(y_used, 8 * t + k + 1)
                layer_norm(a, a, g2, b2, 0, h2_rdy)
                if t:
                    finish(t - 1)
            finish(NT - 1)


_INS = ["x", "p", "positions", "ln_emb_g", "ln_emb_b", "w_in", "w_o", "diff_lq1", "diff_lk1", "diff_lq2", "diff_lk2",
        "diff_subln_g", "ln1_g", "ln1_b", "w_router", "router_bias", "w_exp_gate", "w_exp_up", "w_exp_down",
        "w_sh_gate", "w_sh_up", "w_sh_down", "ln2_g", "ln2_b", "w_ple_gate", "b_ple_gate", "w_ple_proj"]


def kernel(**inputs):
    import numpy as np
    import concourse.bacc as bacc
    from concourse.bass_utils import run_bass_kernel_spmd as run

    nc = bacc.Bacc("TRN2", target_bir_lowering=False, num_devices=1)
    arrays, args = {}, []
    host = {n: np.ascontiguousarray(inputs[n]) for n in _INS}
    host["inv_freq"] = np.float32(10000.0) ** (-np.arange(0, HD, 2, dtype=np.float32) / np.float32(HD))
    for name, a in host.items():
        arrays[f"in_{name}"] = a
        args.append(nc.dram_tensor(f"in_{name}", a.shape, mybir.dt.from_np(a.dtype), kind="ExternalInput").ap())
    args.append(nc.dram_tensor("out_0", (1, S, D), F32, kind="ExternalOutput").ap())
    build(nc, *args)
    return run(nc, [arrays], core_ids=[0]).results[0]["out_0"]
```

```python
from contextlib import ExitStack

import concourse.bass as bass
from concourse import mybir

F32 = mybir.dt.float32
F32R = mybir.dt.float32r
BF16 = mybir.dt.bfloat16
I32 = mybir.dt.int32
U32 = mybir.dt.uint32
ALU = mybir.AluOpType
ACT = mybir.ActivationFunctionType
AX = mybir.AxisListType

P = 128
D = 1024
S = 1024
NT = S // P
KC = D // P
HD = 64
HALF = HD // 2
AH = 8
BH = 4
CH = 64
NKEEP = 256
ALPHA = 2.0 ** 0.25
EPS = 1e-5
LAMBDA_INIT = 0.8 - 0.6
SCALE = HD ** -0.5
WSCALE = (8 ** -0.5) * (64 ** -0.5)
NE = 64
NG = 8
TOPG = 4
TOPK = 8
ED = 256
ROUTED = 2.5
PLE = 256
MASK = -1e30
FILL = -3.0e38
TAKEN = -3.4e38
SHB = NT
MAXB = SHB + (S * TOPK + NE * P) // P
UW, DW = KC * 2 * ED, 2 * D
EW = UW + DW
CUT = (0, 1536, 3072, UW)

C_QA, C_KA, C_VA, C_QI, C_KI, C_QB, C_KB, C_VB = 0, 512, 1024, 1536, 2048, 2120, 2632, 3144
GROUPS = [("qi", C_QI, 512), ("ki", C_KI, 72), ("va", C_VA, 512), ("vb", C_VB, 512),
          ("qa", C_QA, 512), ("ka", C_KA, 512), ("qb", C_QB, 512), ("kb", C_KB, 512)]
NGR = len(GROUPS)
ROPED = [g for g, (n, _, _) in enumerate(GROUPS) if n[0] in "qk"]


def build(nc, x, p, positions, ln_emb_g, ln_emb_b, w_in, w_o, lq1, lk1, lq2, lk2, subln_g, ln1_g, ln1_b,
          w_router, router_bias, w_gate, w_up, w_down, w_sh_gate, w_sh_up, w_sh_down, ln2_g, ln2_b,
          w_ple_gate, b_ple_gate, w_ple_proj, inv_freq, out):
    x_t = x.rearrange("a (t q) d -> t (a q) d", q=P)
    out_t = out.rearrange("a (t q) d -> t (a q) d", q=P)
    p_t = p.rearrange("l a (t q) d -> t (l a q) d", q=P)
    w_in_k = w_in.rearrange("l (k q) n -> q (l k) n", q=P)
    w_o_k = w_o.rearrange("l (k q) n -> q (l k) n", q=P)
    w_r_k = w_router.rearrange("l (k q) n -> q (l k) n", q=P)
    w_pg_k = w_ple_gate.rearrange("l (k q) n -> q (l k) n", q=P)
    w_pp_k = w_ple_proj.rearrange("l (k q) n -> q (l k) n", q=P)
    w_g_e = w_gate.rearrange("l e (q k) f -> (l e) q (k f)", q=P)
    w_u_e = w_up.rearrange("l e (q k) f -> (l e) q (k f)", q=P)
    w_d_e = w_down.rearrange("l e (q k) f -> (l e) q (k f)", q=P)
    w_sg = w_sh_gate.rearrange("l (q k) f -> q (l k f)", q=P)
    w_su = w_sh_up.rearrange("l (q k) f -> q (l k f)", q=P)
    w_sd = w_sh_down.rearrange("l (q k) f -> q (l k f)", q=P)

    h_d = nc.dram_tensor("h_emb", (S, D), F32).ap()
    h1_d = nc.dram_tensor("h_mix", (S, D), F32).ap()
    y_d = nc.dram_tensor("y_slots", (MAXB * P, D), F32).ap()

    ctx = ExitStack()
    with ctx:
        arena = ctx.enter_context(nc.sbuf_tensor("arena", [P, 53200], F32))
        base = nc.sbuf_base - 53200 * 4
        n_at = [0]

        def at(off, *dims, dt=F32):
            n = 1
            for d in dims:
                n *= d
            n_at[0] += 1
            v = nc.alloc_sbuf_tensor_at(f"at{off}_{n_at[0]}", [P, n], dt, offset=base + 4 * off, align_bytes=4)[:, :]
            if len(dims) == 1:
                return v
            names = "abcd"[:len(dims)]
            return v.rearrange(f"p ({' '.join(names)}) -> p {' '.join(names)}", **dict(zip(names[1:], dims[1:])))

        hT = at(0, KC, S)
        w_sl = [at(8192, KC, 512), at(12288, KC, 512)]
        raw = [at(16384, 512), at(16896, 512)]
        rot = [at(17408, 512), at(17920, 512)]
        rot2 = at(18432, 512)
        rel = [at(18944, 1024), at(19968, 1024)]
        qiT = qbT = at(20992, 4, S)
        kiT = at(25088, S)
        qaT, kaT, kbT = at(26112, 4, S), at(30208, 4, S), at(34304, 4, S)
        va, vb = at(38400, NT, 512), at(42496, NT, 512)
        h0 = at(26112, NT, D)
        g_emb, b_emb = at(34304, D), at(35328, D)
        off_sc = [46592 + 64 * t * (t + 1) for t in range(NT)]
        score = [at(off_sc[t], P * (t + 1)) for t in range(NT)]
        wo = at(0, KC, D)
        prob = [at(8192 + 1024 * i, 1024) for i in range(4)]
        pT = [at(12288 + 1024 * i, NT, P) for i in range(2)]
        mix = at(14336, D)
        mixT = at(15360, KC, P)
        h_in = at(16384, D)
        h1 = at(17408, D)
        g1, b1 = at(18432, D), at(19456, D)
        sq = at(20480, BH, P)
        wr = at(25088, KC, NE)
        rl = at(25600, NT, NE)
        w_ru = [at(i * EW, UW) for i in range(2)]
        w_rd = [at(i * EW + UW, DW) for i in range(2)]
        w_uh = [at(12288 + 8192 * i, UW, dt=F32R) for i in range(2)]
        w_ul = [at(16384 + 8192 * i, UW, dt=F32R) for i in range(2)]
        w_dh = [at(o, DW, dt=F32R) for o in (32768, 28672)]
        w_dl = [at(o, DW, dt=F32R) for o in (34816, 30720)]
        y_sb = at(46160, D)
        hidTh, hidTl = at(40448, 2, P, dt=F32R), at(36864, 2, P, dt=F32R)
        xTh, xTl = at(38400, KC, P, dt=F32R), at(42768, KC, P, dt=F32R)
        xg = [at(o, D) for o in (37376, 44304)]
        xT = at(38400, KC, P)
        onehot = at(39424, NT, P, dt=BF16)
        sg, hid, hidT = at(39936, ED), at(40192, ED), at(40448, 2, P)
        slotm = at(40704, NT, NE + 1)
        gate = at(41224, NT, NE)
        iota_s = at(41736, P)
        slot8 = at(41864, NT, TOPK)
        slot8i = at(41928, NT, TOPK, dt=U32)
        gate8 = at(41992, NT, TOPK)
        tab = at(42056, 2 * P, dt=I32)
        bend_i = at(42568, NE + 1, dt=I32)
        bend = at(42636, NE + 1)
        nblk = at(42704, NE)
        sig, biased = at(42768, NT, NE), at(43280, NT, NE)
        tmp1, tmp2, tmp3 = at(43792, 512), at(44304, 512), at(44816, 512)
        sel_b = at(45328, NT, NE, dt=BF16)
        g8 = at(45584, NT * NG, 8)
        rbias = at(46096, NE)

        def up_v(w):
            return w.rearrange("p (j k f) -> p j k f", j=2, k=KC)

        def dn_v(w):
            return w.rearrange("p (j n) -> p j n", j=2)

        w_sh = at(26112, EW)
        sh_up_v, sh_dn_v = up_v(w_sh[:, 0:UW]), dn_v(w_sh[:, UW:EW])
        xg_v = [v.rearrange("p (q k) -> p k q", k=KC) for v in xg]
        hid_v = hid.rearrange("p (q j) -> p j q", j=2)
        wpg, wpp = at(0, KC, D), at(8192, 2, D)
        g2, b2, bp = at(47184, D), at(48208, D), at(49232, D)
        acc = [at(12288 + 1024 * i, D) for i in range(2)]
        ysh = [at(14336 + 1024 * i, D) for i in range(2)]
        yk = [at(16384 + 1024 * i, D) for i in range(8)]
        h2T = at(24576, KC, P)
        zt, ot = at(25600, D), [at(26624 + 1024 * i, D) for i in range(2)]
        pt_sb = [at(28672 + 256 * i, PLE) for i in range(2)]
        ppT = at(29184, 2, P)
        ident = at(51200, P)
        cosd, sind = at(51328, NT, HD), at(51840, NT, HD)
        used = [52352]

        def small(*dims, dt=F32):
            n = 1
            for d in dims:
                n *= d
            o = used[0]
            used[0] += (n + 1) // 2 if dt == BF16 else n
            assert used[0] <= 53200, used
            return at(o, *dims, dt=dt)

        iws = small(NT, 8)
        stats, mv = small(2, 6), small(2)
        rs, nmr = small(2, 1), small(2, 1)
        vareps = small(2, 1)
        mhalf = small(8)
        m8 = small(8)
        mx, nmx = small(12 + BH), small(12 + BH)
        ssum = [small(12 + BH) for _ in range(2)]
        rsum = small(12 + BH)
        cB = small(2)
        ms = small(BH)
        rms = small(BH)
        subg = small(P)
        lam2 = small(4)
        neglam = small(1)
        posi, posf = small(NT, dt=I32), small(NT)
        rowneg = small(HD)
        colq = small(P)
        tokpair = small(NT, 2, dt=BF16)
        gbase = small(1)
        idx = small(2, dt=U32)
        parity = at(37120, 2 * P, dt=I32)
        ang = at(46592, NT, HALF)
        tn, tr, tc, tw = (at(46592 + 256 * i, NT, HALF) for i in range(1, 5))
        inv = at(48128, HALF)
        lam4 = at(48192, 4, HD)
        gsub = at(50304, P)
        thr = at(50432, 7)
        tri = at(50496, NG, NG)
        gs = at(50560, NT, NG)
        gpen = at(50624, NT, NG)
        den8 = at(50688, NT)
        eobc = at(50696, 2)
        itg = at(50700, 2)
        zer = at(50712, NE)
        ones_b = at(50784, P, dt=BF16)
        upper_b = at(50848, P, dt=BF16)

        tp = [ctx.enter_context(nc.psum_tensor(f"turn{i}", [P, 512], F32)) for i in range(2)]
        lg = [ctx.enter_context(nc.psum_tensor(f"logit{i}", [P, 1024], F32)) for i in range(2)]
        pa = [ctx.enter_context(nc.psum_tensor(f"acc{i}", [P, 512], F32)) for i in range(2)]

        def sem(name):
            return ctx.enter_context(nc.semaphore(name))

        consts = sem("consts")
        const_in = sem("const_in")
        x_in = [sem(f"x_in{t}") for t in range(NT)]
        step = sem("dve_step")
        var_rdy = sem("var_rdy")
        rstd_rdy = sem("rstd_rdy")
        ln_rdy = sem("ln_rdy")
        h_st = sem("h_stored")
        t_rdy = sem("turn_ready")
        t_out = sem("turn_out")
        ang_rdy = sem("angles_ready")
        rope_rdy = sem("rope_tables")
        w_in_s = [sem(f"w_in{i}") for i in range(2)]
        pj_rdy = sem("proj_ready")
        pj_out = sem("proj_out")
        rope_own = sem("rope_steps")
        rope_own2 = sem("rope_steps_pool")
        rot_rdy = sem("rotated")
        l_rdy = sem("logits_ready")
        l_act = sem("logits_read_act")
        l_dve = sem("logits_read_dve")
        rel_rdy = sem("relu_ready")
        rel_used = sem("relu_used")
        iw_rdy = sem("iw_ready")
        wo_in = sem("wo_in")
        rows_in = sem("rows_in")
        mx_rdy = sem("max_ready")
        e_rdy = sem("exp_ready")
        cmb_rdy = sem("combined")
        pv_done = sem("pv_done")
        mix_rdy = sem("mix_ready")
        hin_s = sem("h_in")
        h1_rdy = sem("h1_ready")
        h1_st = sem("h1_stored")
        sq_rdy = sem("mean_square")
        rms_rdy = sem("rms_ready")
        lam_in = sem("lambda_sums")
        lam_out = sem("lambda_exps")
        y_fill = sem("unused_blocks_filled")
        rb_in = sem("router_bias_in")
        rc = sem("routing_consts")
        g8_rdy = sem("gates_by_slot_ready")
        sig_rdy = sem("sigmoid_ready")
        sel_rdy = sem("chosen_ready")
        pos_rdy = sem("places_ready")
        eob_rdy = sem("block_experts_ready")
        eob_row = sem("block_experts_row")
        tab_rdy = sem("tables_ready")
        sh_in = sem("shared_weights_in")
        xs_got = sem("shared_rows_in")
        ru_in = [sem(f"gate_up_in{i}") for i in range(2)]
        rd_in = [sem(f"down_in{i}") for i in range(2)]
        uh_rdy = sem("gate_up_rounded")
        ul_rdy = sem("gate_up_remainders")
        ud_rdy = sem("gate_up_last_remainders")
        dh_rdy = sem("down_rounded")
        dl_rdy = sem("down_remainders")
        xh_rdy = sem("rows_rounded")
        hh_rdy = sem("hidden_rounded")
        oh_rdy = sem("onehot_ready")
        tok_rdy = sem("tokens_psum")
        idx_rdy = sem("indices_ready")
        gb_own = sem("block_base")
        x_got = [sem(f"rows_gathered{i}") for i in range(2)]
        go = sem("gather_may_start")
        up_done = sem("up_done")
        silu_rdy = sem("silu_ready")
        hid_rdy = sem("hidden_ready")
        hT_trn = sem("hidden_transposed")
        hT_rdy = sem("hiddenT_ready")
        down_done = sem("down_done")
        y_out = sem("y_read")
        y_st = sem("y_stored")
        ple_in = sem("ple_weights_in")
        row_in = [sem(f"tile_in{i}") for i in range(2)]
        y_in = [sem(f"y_in{i}") for i in range(TOPK)]
        y_used = sem("y_used")
        h2_rdy = sem("h2_ready")
        g_mm = sem("gate_products")
        z_rdy = sem("gate_argument")
        s_rdy = sem("gate_ready")
        o_rdy = sem("out_ready")
        o_st = [sem(f"out_stored{i}") for i in range(2)]

        def for_experts(eng, first, more):
            def pair(n):
                for j in range(2):
                    r = eng.value_load(bend_i[0:1, bass.ds(n * 2 + j, 1)], min_val=0, max_val=MAXB - SHB)
                    end = eng.value_load(bend_i[0:1, bass.ds(n * 2 + (j + 1), 1)], min_val=1, max_val=MAXB - SHB)
                    first(n, j, r)
                    with eng.If(r + 1 < end):
                        with eng.Fori(r + 1, end) as r2:
                            more(n, j, r2)

            pair(0)
            with eng.Fori(1, NE // 2 - 1) as n:
                pair(n)
            pair(NE // 2 - 1)

        block = ctx.enter_context(nc.Block())

        TASKS = [(t, k) for t in range(NT) for k in range(AH + BH)]
        NTK = len(TASKS)
        l_uses = []
        n_free = {"act": 0, "dve": 0, "exp": 0}

        def use_l(who):
            n_free[who] += 1
            l_uses.append((who, n_free[who]))

        for t in range(2, NT):
            for h in range(8):
                use_l("act")
        FINISH_AT = {1: "mix", 5: "rows"}
        order = []
        for i, (t, k) in enumerate(TASKS):
            order.append(("task", i))
            if t > 0 and k in FINISH_AT:
                order.append((FINISH_AT[k], t - 1))
        order += [("task", NTK), ("task", NTK + 1), ("mix", NT - 1)]
        order += [("turn", 0), ("shared", 0), ("shared", 1), ("rows", NT - 1)] + [("shared", b) for b in range(2, SHB)]
        logits_at = {}
        for what, i in order:
            if what == "task" and i < NTK:
                if TASKS[i][1] < AH:
                    use_l("dve")
                    n_free["exp"] += 1
                else:
                    use_l("exp")
                    use_l("exp")
            if what == "mix":
                use_l("dve")
            if what in ("task", "mix"):
                logits_at[what, i] = len(l_uses)
        N_IDX = 6 * 8
        N_RC = 13
        T_LN = 2 * NT
        T_PROJ = NT * len(ROPED)

        def banks(t):
            return (t + 4) // 4

        prob_at, n = [], 0
        for t, k in TASKS:
            w = 1 if k < AH else 2
            prob_at.append([(n + j) % 4 for j in range(w)])
            n += w
        prob_owner = {}
        prob_prev = []
        for i, places in enumerate(prob_at):
            prob_prev.append(max([prob_owner.get(q, -1) for q in places]))
            for q in places:
                prob_owner[q] = i
        turned_at, u = {}, T_LN + T_PROJ
        for what, i in order:
            if what == "task" and 1 <= i <= NTK:
                u += banks(TASKS[i - 1][0])
                turned_at["task", i - 1] = u
            if what == "mix":
                u += 2
                turned_at["mix", i] = u
            if what == "rows":
                u += 3
                turned_at["rows", i] = u
            if what == "turn" or (what == "shared" and i < SHB - 1):
                u += 2
                turned_at["xT", 0 if what == "turn" else i + 1] = u
        T_ALL = u

        def count_exp(i):
            t, k = TASKS[i] if i < NTK else (NT, 0)
            return t * (AH + 2 * BH) + (k if k < AH else AH + 2 * (k - AH))

        @block.sync
        def _(sp):
            for i, (dst, src) in enumerate([(g_emb, ln_emb_g), (b_emb, ln_emb_b), (inv, inv_freq)]):
                sp.dma_start(dst, src.rearrange("(a n) -> a n", a=1).broadcast_to([P, src.shape[0]])).then_inc(const_in, 16)
            sp.dma_start(posi, positions.rearrange("a (t q) -> q (a t)", q=P),
                         allow_slow_non_contiguous=True).then_inc(const_in, 16)
            for i, v in enumerate((lq1, lk1, lq2, lk2)):
                sp.dma_start(lam4[:, i, :], v.broadcast_to([P, HD])).then_inc(const_in, 16)
            sp.dma_start(subg, subln_g.broadcast_to([P, P])).then_inc(const_in, 16)
            for t in range(NT):
                sp.dma_start(h0[:, t, :], x_t[t]).then_inc(x_in[t], 16)
            for g, (_, c0, n) in enumerate(GROUPS):
                if g >= 2:
                    sp.wait_ge(pj_rdy, NT * (g - 1))
                sp.dma_start(w_sl[g % 2][:, :, 0:n], w_in_k[:, :, c0:c0 + n]).then_inc(w_in_s[g % 2], 16)
                if g == 0:
                    for t in range(NT):
                        sp.wait_ge(ln_rdy, t + 1)
                        sp.dma_start(h_d[t * P:(t + 1) * P, :], h0[:, t, :]).then_inc(h_st, 16)
            sp.wait_ge(pj_rdy, NT * NGR)
            sp.dma_start(wo, w_o_k).then_inc(wo_in, 16)
            sp.wait_ge(rel_used, N_IDX)
            sp.wait_ge(t_out, T_LN + T_PROJ)
            sp.wait_ge(h_st, 16 * NT)
            sp.dma_start(g1, ln1_g.broadcast_to([P, D])).then_inc(rows_in, 16)
            sp.dma_start(b1, ln1_b.broadcast_to([P, D])).then_inc(rows_in, 16)
            sp.dma_start(wr, w_r_k).then_inc(rows_in, 16)
            for t in range(NT):
                if t:
                    sp.wait_ge(h1_rdy, t)
                sp.dma_start(h_in, h_d[t * P:(t + 1) * P, :]).then_inc(hin_s, 16)
                b = SHB + NE + NT * t
                sp.dma_start(y_d[b * P:(b + NT) * P, :], x.rearrange("a s d -> (a s) d")).then_inc(y_fill, 16)
                if t < NT - 1:
                    sp.wait_ge(h1_rdy, t + 1)
                    sp.dma_start(h1_d[t * P:(t + 1) * P, :], h1).then_inc(h1_st, 16)
            sp.wait_ge(l_rdy, logits_at["task", NTK - BH - 1])
            for m, src in enumerate((w_sg, w_su, w_sd)):
                sp.dma_start(w_sh[:, 2048 * m:2048 * (m + 1)], src).then_inc(sh_in, 16)
            sp.wait_ge(pv_done, NTK)
            sp.dma_start(rbias, router_bias.broadcast_to([P, NE])).then_inc(rb_in, 16)

            def shared_rows(b):
                if b:
                    sp.wait_ge(t_rdy, turned_at["xT", b - 1])
                sp.dma_start(xg[0], h1_d[b * P:(b + 1) * P, :]).then_inc(xs_got, 16)

            def load_up(r, place):
                for m, src in enumerate((w_g_e, w_u_e)):
                    sp.dma_start(w_ru[place][:, 2048 * m:2048 * (m + 1)], src[r]).then_inc(ru_in[place], 16)

            def load_down(r, place):
                sp.dma_start(w_rd[place], w_d_e[r]).then_inc(rd_in[place], 16)

            sp.wait_ge(h1_st, 16 * (NT - 1))
            shared_rows(0)
            sp.wait_ge(l_rdy, logits_at["mix", NT - 1])
            load_up(0, 0)
            load_down(0, 0)
            shared_rows(1)
            sp.wait_ge(h1_rdy, NT)
            sp.dma_start(h1_d[(NT - 1) * P:S, :], h1).then_inc(h1_st, 16)
            shared_rows(2)
            sp.wait_ge(t_out, turned_at["rows", NT - 1])
            sp.wait_ge(h1_st, 16 * NT)
            load_up(1, 1)
            load_down(1, 1)
            for b in range(3, SHB):
                shared_rows(b)
            sp.wait_ge(ul_rdy, 2)
            sp.wait_ge(ud_rdy, 1)
            load_up(2, 0)
            sp.wait_ge(down_done, SHB)
            for dst, src in ((g2, ln2_g), (b2, ln2_b), (bp, b_ple_gate)):
                sp.dma_start(dst, src.broadcast_to([P, D])).then_inc(ple_in, 16)
            sp.wait_ge(tab_rdy, 2)

            with sp.Fori(0, (NE - 4) // 2) as n:
                for j in range(2):
                    sp.wait_ge(ul_rdy, n * 4 + (2 * j + 4))
                    sp.wait_ge(ud_rdy, n * 2 + (j + 2))
                    load_up(n * 2 + (j + 3), 1 - j)
                    sp.wait_ge(dl_rdy, n * 2 + (j + 1))
                    load_down(n * 2 + (j + 2), j)
            sp.wait_ge(ul_rdy, 2 * (NE - 2))
            sp.wait_ge(ud_rdy, NE - 2)
            load_up(NE - 1, 1)
            sp.wait_ge(dl_rdy, NE - 3)
            load_down(NE - 2, 0)
            sp.wait_ge(dl_rdy, NE - 2)
            load_down(NE - 1, 1)
            sp.wait_ge(ul_rdy, 2 * NE)
            sp.wait_ge(ud_rdy, NE)
            sp.wait_ge(dl_rdy, NE - 1)
            for dst, src in ((wpg, w_pg_k), (wpp, w_pp_k)):
                sp.dma_start(dst, src).then_inc(ple_in, 16)
            n_routed = sp.value_load(bend_i[0:1, NE:NE + 1], min_val=NE, max_val=MAXB - SHB)
            sp.wait_ge(down_done, n_routed + SHB)
            sp.wait_ge(y_st, n_routed * 16 + SHB * 16)
            for t in range(NT + 2):
                if t < NT:
                    if t >= 2:
                        sp.wait_ge(o_rdy, t - 1)
                    ts = slice(t * P, (t + 1) * P)
                    for dst, src in ((acc[t % 2], h1_d[ts, :]), (ysh[t % 2], y_d[ts, :]), (pt_sb[t % 2], p_t[t])):
                        sp.dma_start(dst, src).then_inc(row_in[t % 2], 16)
                if t >= 2:
                    sp.wait_ge(o_rdy, t - 1)
                    sp.dma_start(out_t[t - 2], ot[t % 2]).then_inc(o_st[t % 2], 16)
            for i in range(2):
                sp.wait_ge(o_st[i], 16 * NT // 2)

        @block.gpsimd
        def _(pool):
            pool.memset(ident, 0.0).then_inc(consts, 1)
            pool.memset(rowneg, MASK).then_inc(consts, 1)
            pool.memset(colq[:, 0:CH], 1.0).then_inc(consts, 1)
            pool.memset(colq[:, CH:P], 0.0).then_inc(consts, 1)
            pool.memset(mhalf, -0.5).then_inc(consts, 1)
            pool.wait_ge(consts, 5)
            pool.affine_select(out=ident, in_=ident, compare_op=ALU.not_equal, fill=1.0, base=0,
                               pattern=[[-1, P]], channel_multiplier=1).then_inc(consts, 1)

            def rsqrt(n, src, dst, done):
                pool.wait_ge(src[1], n)
                pool.tensor_tensor(dst, src[0], mhalf[:, 0:dst.shape[1]], ALU.pow).then_inc(done, 1)

            pool.wait_ge(consts, 6)
            for t in range(NT):
                rsqrt(t + 1, (vareps[:, t % 2, :], var_rdy), rs[:, t % 2, :], rstd_rdy)
            n_rot = 2 * NT
            for g in ROPED[2:]:
                for t in range(NT):
                    u = (ROPED.index(g)) * NT + t
                    src, dst = raw[u % 2].rearrange("p (h j c) -> p h j c", j=2, c=HALF), rot[u % 2].rearrange("p (h j c) -> p h j c", j=2, c=HALF)
                    tmp = rot2.rearrange("p (h j c) -> p h j c", j=2, c=HALF)
                    pool.wait_ge(pj_out, g * NT + t + 1)
                    pool.wait_ge(t_rdy, T_LN + u - 1)
                    pool.wait_ge(rot_rdy, u)
                    if u == n_rot:
                        pool.wait_ge(rope_rdy, 2)
                    cb = cosd[:, t, :].rearrange("p (j c) -> p j c", j=2).unsqueeze(1).broadcast_to([P, 8, 2, HALF])
                    sb_ = sind[:, t, :].rearrange("p (j c) -> p j c", j=2).unsqueeze(1).broadcast_to([P, 8, 2, HALF])
                    pool.tensor_tensor(dst, src, cb, ALU.mult).then_inc(rope_own2, 1)
                    pool.tensor_tensor(tmp, src[:, :, ::-1, :], sb_, ALU.mult).then_inc(rope_own2, 1)
                    pool.wait_ge(rope_own2, 2 * (u - n_rot + 1))
                    pool.tensor_tensor(dst, dst, tmp, ALU.add).then_inc(rot_rdy, 1)
            for t in range(NT):
                rsqrt(t + 1, (ms, sq_rdy), rms, rms_rdy)
                rsqrt(NT + t + 1, (vareps[:, 0, :], var_rdy), rs[:, 0, :], rstd_rdy)

            pool.wait_ge(h1_rdy, NT)
            n_rc = [0]

            def const(ins):
                ins.then_inc(rc, 1)
                n_rc[0] += 1

            const(pool.iota(iota_s, [[1, P]], base=0, channel_multiplier=0, allow_small_or_imprecise_dtypes=True))
            const(pool.iota(slotm[:, :, 0], [[P, NT]], base=0, channel_multiplier=1, allow_small_or_imprecise_dtypes=True))
            const(pool.iota(thr, [[P, 7]], base=P, channel_multiplier=0, allow_small_or_imprecise_dtypes=True))
            const(pool.iota(itg, [[P, 2]], base=0, channel_multiplier=1, allow_small_or_imprecise_dtypes=True))
            const(pool.iota(tokpair[:, :, 0], [[P, NT]], base=0, channel_multiplier=0, allow_small_or_imprecise_dtypes=True))
            const(pool.iota(tokpair[:, :, 1], [[0, NT]], base=0, channel_multiplier=1, allow_small_or_imprecise_dtypes=True))
            const(pool.iota(parity, [[0, P], [1, 2]], base=0, channel_multiplier=0))
            const(pool.memset(zer, 0.0))
            const(pool.memset(ones_b, 1.0))
            const(pool.memset(upper_b, 1.0))
            const(pool.memset(tri, 1.0))
            pool.wait_ge(rc, n_rc[0])
            const(pool.affine_select(out=upper_b, in_=upper_b, compare_op=ALU.is_gt, fill=0.0, base=0,
                                     pattern=[[1, P]], channel_multiplier=-1))
            const(pool.affine_select(out=tri, in_=tri, compare_op=ALU.is_gt, fill=0.0, base=0,
                                     pattern=[[1, NG], [-1, NG]], channel_multiplier=0))
            assert n_rc[0] == N_RC

            def gather(i):
                pool.indirect_dma_start(out=xg[i], out_offset=None, in_=h1_d,
                                        in_offset=bass.IndirectOffsetOnAxis(ap=idx[:, i:i + 1], axis=0)).then_inc(x_got[i], 16)

            def remainders(n, j):
                for c in range(2):
                    pool.wait_ge(uh_rdy, n * 6 + (3 * j + c + 1))
                    h = slice(CUT[c], CUT[c + 1])
                    pool.tensor_tensor(w_ul[j][:, h], w_ru[j][:, h], w_uh[j][:, h], ALU.subtract).then_inc(ul_rdy, 1)

            pool.wait_ge(h1_st, 16 * NT)
            remainders(0, 0)
            pool.wait_ge(idx_rdy, 1)
            gather(1)
            pool.wait_ge(idx_rdy, 2)
            pool.wait_ge(t_rdy, turned_at["xT", SHB - 1])
            gather(0)
            pool.wait_ge(idx_rdy, 3)
            pool.wait_ge(t_rdy, T_ALL + 2)
            gather(1)
            n_routed = pool.value_load(bend_i[0:1, NE:NE + 1], min_val=NE, max_val=MAXB - SHB)

            def rows_ahead(r):
                odd = pool.value_load(parity[0:1, bass.ds(r, 1)], min_val=0, max_val=1)
                pool.wait_ge(idx_rdy, r + 4)
                pool.wait_ge(t_rdy, r * 2 + (T_ALL + 4))
                pool.sem_inc(go, 1)
                with pool.If(odd < 1):
                    gather(0)
                with pool.Else():
                    gather(1)

            def first(n, j, r):
                if j == 0:
                    remainders(n, 1)
                elif not isinstance(n, int) or n < NE // 2 - 1:
                    remainders(n + 1, 0)
                rows_ahead(r)

            for_experts(pool, first, lambda n, j, r: rows_ahead(r))
            pool.wait_ge(y_st, n_routed * 16 + SHB * 16)
            odd = pool.value_load(parity[0:1, bass.ds(n_routed, 1)], min_val=0, max_val=1)
            with pool.If(odd < 1):
                pool.wait_ge(x_got[0], n_routed * 8 + 16)
                pool.wait_ge(x_got[1], n_routed * 8 + 32)
            with pool.Else():
                pool.wait_ge(x_got[0], n_routed * 8 + 24)
                pool.wait_ge(x_got[1], n_routed * 8 + 24)
            pool.sem_inc(go, 1)
            pool.wait_ge(g8_rdy, 1)

            def gather_y(t, ks):
                for k in ks:
                    if t:
                        pool.wait_ge(y_used, 8 * (t - 1) + k + 1)
                    pool.indirect_dma_start(out=yk[k], out_offset=None, in_=y_d,
                                            in_offset=bass.IndirectOffsetOnAxis(ap=slot8i[:, t, k:k + 1], axis=0)
                                            ).then_inc(y_in[k], 16)

            gather_y(0, range(TOPK))
            for t in range(NT):
                if t + 1 < NT:
                    gather_y(t + 1, range(4))
                rsqrt(2 * NT + t + 1, (vareps[:, 0, :], var_rdy), rs[:, 0, :], rstd_rdy)
                if t + 1 < NT:
                    gather_y(t + 1, range(4, TOPK))

        @block.scalar
        def _(act):
            act.wait_ge(ang_rdy, 1)
            act.activation(sind[:, :, HALF:HD], tr, ACT.Sin).then_inc(rope_rdy, 1)
            act.activation(cosd[:, :, 0:HALF], tc, ACT.Sin).then_inc(rope_rdy, 1)
            act.wait_ge(rope_rdy, 2)
            act.mul(sind[:, :, 0:HALF], sind[:, :, HALF:HD], -1.0).then_inc(rope_rdy, 1)
            act.copy(cosd[:, :, HALF:HD], cosd[:, :, 0:HALF]).then_inc(rope_rdy, 1)
            act.wait_ge(lam_in, 1)
            act.activation(lam2[:, 2:4], lam2[:, 0:2], ACT.Exp).then_inc(lam_out, 1)
            tu = [0]

            def turn_out(dst):
                act.wait_ge(t_rdy, tu[0] + 1)
                n = dst.free_size()
                src = tp[tu[0] % 2][:, 0:n]
                if len(dst.shape) == 3:
                    src = src.rearrange("p (a b) -> p a b", a=dst.shape[1])
                act.activation(dst, src, ACT.Copy).then_inc(t_out, 1)
                tu[0] += 1

            for t in range(NT):
                for b in range(2):
                    turn_out(hT[:, 4 * b:4 * b + 4, t * P:(t + 1) * P])
            dstT = {"qi": qiT, "qa": qaT, "ka": kaT, "qb": qbT, "kb": kbT}

            def group(g):
                name, c0, n = GROUPS[g]

                def turned(t):
                    ts = slice(t * P, (t + 1) * P)
                    turn_out(kiT[:, ts] if name == "ki" else dstT[name][:, :, ts])

                for t in range(NT):
                    u = g * NT + t
                    act.wait_ge(pj_rdy, u + 1)
                    if name[0] == "v":
                        dst = (va if name == "va" else vb)[:, t, :]
                    else:
                        r = ROPED.index(g) * NT + t
                        dst = raw[r % 2][:, 0:n]
                        if r >= 2:
                            act.wait_ge(rot_rdy, r - 1)
                    if name == "va" and t == 0:
                        act.wait_ge(h_st, 16 * NT)
                    act.activation(dst, pa[u % 2][:, 0:n], ACT.Copy).then_inc(pj_out, 1)
                    if name[0] != "v" and t >= 1:
                        turned(t - 1)
                if name[0] != "v":
                    turned(NT - 1)

            def silu(g):
                act.wait_ge(up_done, g + 1)
                act.activation(sg, lg[0][:, 0:ED], ACT.Silu).then_inc(silu_rdy, 1)

            def round_up(n, j):
                act.wait_ge(ru_in[j], n * 32 + 32)
                for c in range(3):
                    h = slice(CUT[c], CUT[c + 1])
                    act.activation(w_uh[j][:, h], w_ru[j][:, h], ACT.Copy).then_inc(uh_rdy, 1)

            def round_rows(r):
                for b in range(2):
                    act.wait_ge(t_rdy, r * 2 + (T_ALL + 1 + b))
                    act.activation(xTh[:, 4 * b:4 * b + 4, :], tp[b].rearrange("p (a b) -> p a b", b=P), ACT.Copy).then_inc(xh_rdy, 1)

            def store(g):
                act.wait_ge(y_out, g + 1)
                rows = y_d[g * P:(g + 1) * P, :] if isinstance(g, int) else y_d[bass.ds(g * P, P), :]
                act.dma_start(rows, y_sb).then_inc(y_st, 16)

            group(0)
            group(1)
            for u in range(N_IDX):
                t = 2 + u // 8
                n = P * (t + 1)
                act.wait_ge(l_rdy, u + 1)
                if u >= 2:
                    act.wait_ge(rel_used, u - 1)
                act.activation(rel[u % 2][:, 0:n], lg[u % 2][:, 0:n], ACT.Relu).then_inc(l_act, 1)
            for g in range(2, NGR):
                group(g)

            lu = N_IDX
            n_max = 0
            for what, i in order:
                if what == "task" and i < NTK:
                    t, k = TASKS[i]
                    n = P * (t + 1)
                    for j, q in enumerate(prob_at[i]):
                        n_max += 1
                        act.wait_ge(mx_rdy, n_max)
                        c = k if k < AH else AH + 2 * (k - AH) + j
                        if k < AH:
                            act.activation(prob[q][:, 0:n], prob[q][:, 0:n], ACT.Exp, bias=nmx[:, c:c + 1], scale=SCALE,
                                           accum_out=ssum[t % 2][:, c:c + 1]).then_inc(e_rdy, 1)
                        else:
                            if j == 0 and prob_prev[i] >= 0:
                                act.wait_ge(t_rdy, turned_at["task", prob_prev[i]])
                            act.activation(prob[q][:, 0:n], lg[lu % 2][:, 0:n], ACT.Exp, bias=nmx[:, c:c + 1], scale=SCALE,
                                           accum_out=ssum[t % 2][:, c:c + 1]).then_inc(e_rdy, 1)
                        lu += 1
                if what == "task" and 1 <= i <= NTK:
                    t, k = TASKS[i - 1]
                    if i - 1 >= 2:
                        act.wait_ge(pv_done, i - 2)
                    for b in range(banks(t)):
                        turn_out(pT[(i - 1) % 2][:, 4 * b:min(4 * b + 4, t + 1), :])
                if what == "mix":
                    turn_out(mixT[:, 0:4, :])
                    turn_out(mixT[:, 4:8, :])
                    lu += 1
                if what == "rows":
                    turn_out(mixT[:, 0:4, :])
                    turn_out(mixT[:, 4:8, :])
                    turn_out(rl[:, i, :])
                    if i == NT - 1:
                        act.wait_ge(t_out, turned_at["rows", i])
                        act.activation(sig, rl, ACT.Sigmoid).then_inc(sig_rdy, 1)
                if what == "shared":
                    silu(i)
                if what == "shared" and i == SHB - 2:
                    act.wait_ge(h1_st, 16 * NT)
                    round_up(0, 0)
                if what == "shared" and i == SHB - 1:
                    round_rows(0)
                elif what == "turn" or what == "shared":
                    turn_out(xT[:, 0:4, :])
                    turn_out(xT[:, 4:8, :])
                if what == "shared" and 0 < i < SHB - 1:
                    store(i - 1)


            n_routed = act.value_load(bend_i[0:1, NE:NE + 1], min_val=NE, max_val=MAXB - SHB)

            def y_read(g):
                act.wait_ge(down_done, g + 1)
                act.wait_ge(y_st, g * 16)
                act.activation(y_sb, lg[1][:, :], ACT.Copy).then_inc(y_out, 1)
                store(g)

            def routed(r):
                silu(r + SHB)
                round_rows(r + 1)

            def first(n, j, r):
                act.wait_ge(up_done, r + SHB)
                if j == 0:
                    round_up(n, 1)
                elif not isinstance(n, int) or n < NE // 2 - 1:
                    round_up(n + 1, 0)
                act.wait_ge(rd_in[j], n * 16 + 16)
                act.wait_ge(down_done, r + (SHB - 1))
                if not (isinstance(n, int) and n == 0 and j == 0):
                    y_read(r + (SHB - 2))
                act.activation(w_dh[j], w_rd[j], ACT.Copy).then_inc(dh_rdy, 1)
                routed(r)

            def more(n, j, r):
                y_read(r + (SHB - 2))
                routed(r)

            store(SHB - 2)
            for_experts(act, first, more)
            y_read(n_routed + (SHB - 2))
            y_read(n_routed + (SHB - 1))

            tu[0] = 0
            base = n_routed * 2 + (T_ALL + 2)

            def turn_out2(dst):
                act.wait_ge(t_rdy, base + tu[0] + 1)
                n = dst.free_size()
                act.activation(dst, tp[tu[0] % 2][:, 0:n].rearrange("p (a b) -> p a b", b=P), ACT.Copy).then_inc(t_out, 1)
                tu[0] += 1

            for t in range(NT):
                if t:
                    act.wait_ge(g_mm, t)
                turn_out2(ppT)
                turn_out2(h2T[:, 0:4, :])
                turn_out2(h2T[:, 4:8, :])
                act.wait_ge(z_rdy, t + 1)
                act.activation(zt, zt, ACT.Sigmoid).then_inc(s_rdy, 1)

        @block.tensor
        def _(pe):
            tu = [0]

            def turn(srcs, idn, done=True):
                if tu[0] >= 2:
                    pe.wait_ge(t_out, tu[0] - 1)
                for j, s_ in enumerate(srcs):
                    m = pe.transpose(tp[tu[0] % 2][0:s_.shape[1], j * P:j * P + P], s_, idn)
                m.then_inc(t_rdy, 1)
                tu[0] += 1

            pe.wait_ge(consts, 6)
            for t in range(NT):
                pe.wait_ge(ln_rdy, t + 1)
                for b in range(2):
                    turn([h0[:, t, (4 * b + j) * P:(4 * b + j + 1) * P] for j in range(4)], ident)

            def turn_rot(r):
                pe.wait_ge(rot_rdy, r + 1)
                if GROUPS[ROPED[r // NT]][0] == "ki":
                    turn([rot[r % 2][:, 0:P]], ident)
                else:
                    turn([rot[r % 2][:, j * P:(j + 1) * P] for j in range(4)], ident)

            def group(g):
                name, c0, n = GROUPS[g]
                pe.wait_ge(w_in_s[g % 2], 16 * (g // 2 + 1))
                for t in range(NT):
                    u = g * NT + t
                    if g == 0:
                        pe.wait_ge(t_out, 2 * t + 2)
                    if u >= 2:
                        pe.wait_ge(pj_out, u - 1)
                    for k in range(KC):
                        m = pe.matmul(pa[u % 2][:, 0:n], hT[:, k, t * P:(t + 1) * P], w_sl[g % 2][:, k, 0:n],
                                      start=(k == 0), stop=(k == KC - 1))
                    m.then_inc(pj_rdy, 1)
                    if g in ROPED and t >= 1:
                        turn_rot(ROPED.index(g) * NT + t - 1)
                if g in ROPED:
                    turn_rot(ROPED.index(g) * NT + NT - 1)

            lu = [0]

            def next_l():
                u = lu[0]
                lu[0] += 1
                if u >= 2:
                    who, c = l_uses[u - 2]
                    pe.wait_ge({"act": l_act, "dve": l_dve, "exp": e_rdy}[who], c)
                return lg[u % 2]

            group(0)
            group(1)
            pe.wait_ge(t_out, T_LN + 2 * NT)
            for t in range(2, NT):
                for h in range(8):
                    o, n = next_l(), P * (t + 1)
                    r = slice(HD * (h % 2), HD * (h % 2) + HD)
                    for c in range(0, n, 512):
                        e = min(c + 512, n)
                        m = pe.matmul(o[:, c:e], qiT[r, h // 2, t * P:(t + 1) * P], kiT[r, c:e], start=True, stop=True)
                    m.then_inc(l_rdy, 1)
            for g in range(2, NGR):
                group(g)
            pe.wait_ge(t_out, T_LN + T_PROJ)

            def logits(i):
                t, k = TASKS[i]
                n = P * (t + 1)
                ts = slice(t * P, (t + 1) * P)
                for j in range(1 if k < AH else 2):
                    o = next_l()
                    if k < AH:
                        r, c, qT, kT = slice(HD * (k % 2), HD * (k % 2) + HD), k // 2, qaT, kaT
                    else:
                        r, c, qT, kT = slice(HD * j, HD * j + HD), k - AH, qbT, kbT
                    full = n if k < AH else n - CH
                    for a in range(0, full, 512):
                        e = min(a + 512, full)
                        m = pe.matmul(o[:, a:e], qT[r, c, ts], kT[r, c, a:e], start=True, stop=True)
                    if k >= AH:
                        pe.matmul(o[:, full:n], qT[r, c, ts], kT[r, c, full:n], start=True, stop=False)
                        m = pe.matmul(o[:, full:n], colq[0:1, :], rowneg[0:1, :], start=False, stop=True)
                    m.then_inc(l_rdy, 1)

            def values(i):
                t, k = TASKS[i]
                pe.wait_ge(t_out, turned_at["task", i])
                if k == 0 and t > 0:
                    pe.wait_ge(mix_rdy, t)
                for b in range(t + 1):
                    if k < AH:
                        o, v = pa[0][:, k * HD:(k + 1) * HD], va[:, b, k * HD:(k + 1) * HD]
                    else:
                        o, v = pa[1][:, (k - AH) * P:(k - AH + 1) * P], vb[:, b, (k - AH) * P:(k - AH + 1) * P]
                    m = pe.matmul(o, pT[i % 2][:, b, :], v, start=(b == 0), stop=(b == t))
                m.then_inc(pv_done, 1)

            def turn_prob(i):
                t, k = TASKS[i]
                if k < AH:
                    pe.wait_ge(e_rdy, count_exp(i) + 1)
                else:
                    pe.wait_ge(cmb_rdy, BH * t + k - AH + 1)
                q = prob[prob_at[i][0]]
                for b in range(banks(t)):
                    turn([q[:, c * P:(c + 1) * P] for c in range(4 * b, min(4 * b + 4, t + 1))], ident)

            def up(w):
                for k in range(KC):
                    m = pe.matmul(lg[0][:, 0:2 * ED].rearrange("p (j f) -> p j f", j=2), xT[:, k, :], w[:, :, k, :],
                                  start=(k == 0), stop=(k == KC - 1))
                m.then_inc(up_done, 1)

            def down(g, w):
                pe.wait_ge(hT_rdy, g + 1)
                if not isinstance(g, int) or g > 0:
                    pe.wait_ge(y_out, g)
                for c in range(2):
                    for j in range(2):
                        m = pe.matmul(lg[1][:, c * 512:(c + 1) * 512], hidT[:, j, :], w[:, j, c * 512:(c + 1) * 512],
                                      start=(j == 0), stop=(j == 1))
                m.then_inc(down_done, 1)

            def turn_hidden(g):
                pe.wait_ge(hid_rdy, g + 1)
                for j in range(2):
                    m = pe.transpose(pa[1][:, j * P:(j + 1) * P], hid_v[:, j, :], ident)
                m.then_inc(hT_trn, 1)

            def shared_turn(b):
                pe.wait_ge(xs_got, 16 * (b + 1))
                for c in range(2):
                    turn([xg_v[0][:, 4 * c + j, :] for j in range(4)], ident)

            def turn_rows(i, gathered):
                pe.wait_ge(x_got[i], gathered)
                for b in range(2):
                    for k in range(4):
                        m = pe.transpose(tp[b][:, k * P:(k + 1) * P], xg_v[i][:, 4 * b + k, :], ident)
                    m.then_inc(t_rdy, 1)

            def tokens(n):
                pe.wait_ge(oh_rdy, n)
                for t in range(NT):
                    m = pe.matmul(pa[0][:, 0:2], onehot[:, t, :], tokpair[:, t, :], start=(t == 0), stop=(t == NT - 1))
                m.then_inc(tok_rdy, 1)

            def places():
                pe.wait_ge(sel_rdy, 1)
                pe.wait_ge(rc, N_RC)
                for t in range(NT):
                    for s_ in range(t + 1):
                        pe.matmul(lg[0][:, 512 + t * NE:512 + (t + 1) * NE], (upper_b if s_ == t else ones_b), sel_b[:, s_, :],
                                  start=(s_ == 0), stop=(s_ == t))
                for t in range(NT):
                    m = pe.matmul(pa[0][:, NE:2 * NE], ones_b, sel_b[:, t, :], start=(t == 0), stop=(t == NT - 1))
                m.then_inc(pos_rdy, 1)

            def block_experts():
                pe.wait_ge(eob_rdy, 1)
                for c in range(2):
                    m = pe.transpose(pa[1][0:1, 256 + c * P:256 + (c + 1) * P], eobc[:, c:c + 1], ident)
                m.then_inc(eob_row, 1)

            assert T_ALL % 2 == 0
            for what, i in order:
                if what == "task":
                    if i < NTK:
                        logits(i)
                    if 2 <= i:
                        values(i - 2)
                    if 1 <= i <= NTK:
                        turn_prob(i - 1)
                if what == "mix":
                    pe.wait_ge(mix_rdy, i + 1)
                    for b in range(2):
                        turn([mix[:, (4 * b + j) * P:(4 * b + j + 1) * P] for j in range(4)], ident)
                    pe.wait_ge(t_out, turned_at["mix", i])
                    if i == 0:
                        pe.wait_ge(wo_in, 16)
                    o = next_l()
                    for c in range(2):
                        for k in range(KC):
                            m = pe.matmul(o[:, c * 512:(c + 1) * 512], mixT[:, k, :], wo[:, k, c * 512:(c + 1) * 512],
                                          start=(k == 0), stop=(k == KC - 1))
                    m.then_inc(l_rdy, 1)
                if what == "rows":
                    pe.wait_ge(h1_rdy, i + 1)
                    for b in range(2):
                        turn([h1[:, (4 * b + j) * P:(4 * b + j + 1) * P] for j in range(4)], ident)
                    pe.wait_ge(t_out, turned_at["rows", i] - 1)
                    if i == 0:
                        pe.wait_ge(rows_in, 48)
                    for k in range(KC):
                        m = pe.matmul(tp[tu[0] % 2][:, 0:NE], mixT[:, k, :], wr[:, k, :], start=(k == 0), stop=(k == KC - 1))
                    m.then_inc(t_rdy, 1)
                    tu[0] += 1
                if what == "turn":
                    shared_turn(0)
                if what == "shared":
                    if i == 0:
                        pe.wait_ge(sh_in, 48)
                        pe.wait_ge(l_dve, n_free["dve"])
                    pe.wait_ge(t_out, turned_at["xT", i])
                    up(sh_up_v)
                    if i == 4:
                        places()
                    if i == 5:
                        block_experts()
                    if i >= 6:
                        tokens(i - 5)
                    if i < SHB - 1:
                        shared_turn(i + 1)
                    else:
                        turn_rows(1, 16)
                    if i:
                        down(i - 1, sh_dn_v)
                    turn_hidden(i)
            tokens(3)

            n_routed = pe.value_load(bend_i[0:1, NE:NE + 1], min_val=NE, max_val=MAXB - SHB)


            def up_split(n, j, r):
                pe.wait_ge(ul_rdy, n * 4 + (2 * j + 2))
                pe.wait_ge(ud_rdy, n * 2 + (j + 1))
                pe.wait_ge(xh_rdy, r * 2 + 2)
                xs = [(xTh, w_uh, k) for k in range(KC)] + [(xTh, w_ul, k) for k in range(KC)] + [(xTl, w_uh, k) for k in range(KC)]
                for c, (x_, w, k) in enumerate(xs):
                    if c == 2 * KC:
                        pe.wait_ge(t_out, r * 2 + (T_ALL + 2))
                    m = pe.matmul(lg[0][:, 0:2 * ED].rearrange("p (j f) -> p j f", j=2), x_[:, k, :], up_v(w[j])[:, :, k, :],
                                  start=(c == 0), stop=(c == 3 * KC - 1))
                m.then_inc(up_done, 1)

            def down_split(g, place):
                pe.wait_ge(hT_rdy, g + 1)
                pe.wait_ge(y_out, g)
                for c in range(2):
                    for i, (h_, w, j) in enumerate((h_, w, j) for h_, w in ((hidTh, w_dh), (hidTh, w_dl), (hidTl, w_dh))
                                                   for j in range(2)):
                        m = pe.matmul(lg[1][:, c * 512:(c + 1) * 512], h_[:, j, :], dn_v(w[place])[:, j, c * 512:(c + 1) * 512],
                                      start=(i == 0), stop=(i == 5))
                m.then_inc(down_done, 1)

            def between(r):
                odd = pe.value_load(parity[0:1, bass.ds(r, 1)], min_val=0, max_val=1)
                tokens(r + 4)
                with pe.If(odd < 1):
                    turn_rows(0, r * 8 + 16)
                with pe.Else():
                    turn_rows(1, r * 8 + 24)

            def first(n, j, r):
                up_split(n, j, r)
                between(r)
                if isinstance(n, int) and n == 0 and j == 0:
                    down(SHB - 1, sh_dn_v)
                else:
                    pe.wait_ge(dl_rdy, n * 2 + j)
                    down_split(r + (SHB - 1), 1 - j)
                turn_hidden(r + SHB)

            def more(n, j, r):
                up_split(n, j, r)
                between(r)
                pe.wait_ge(dl_rdy, n * 2 + (j + 1))
                down_split(r + (SHB - 1), j)
                turn_hidden(r + SHB)

            for_experts(pe, first, more)
            pe.wait_ge(dl_rdy, NE)
            down_split(n_routed + (SHB - 1), (NE - 1) % 2)

            tu[0] = 0
            base = n_routed * 2 + (T_ALL + 2)

            def turn2(srcs):
                pe.wait_ge(t_out, base + max(tu[0] - 1, 0))
                for j, s_ in enumerate(srcs):
                    m = pe.transpose(tp[tu[0] % 2][:, j * P:(j + 1) * P], s_, ident)
                m.then_inc(t_rdy, 1)
                tu[0] += 1

            pe.wait_ge(ple_in, 16 * 5)
            pe.wait_ge(y_out, n_routed + SHB)
            for t in range(NT):
                pe.wait_ge(row_in[t % 2], 48 * (t // 2 + 1))
                turn2([pt_sb[t % 2][:, j * P:(j + 1) * P] for j in range(2)])
                pe.wait_ge(h2_rdy, t + 1)
                for b in range(2):
                    turn2([acc[t % 2][:, (4 * b + j) * P:(4 * b + j + 1) * P] for j in range(4)])
                if t:
                    pe.wait_ge(o_rdy, t)
                pe.wait_ge(t_out, base + tu[0])
                for dst, a_T, w, n in ((lg[0], h2T, wpg, KC), (lg[1], ppT, wpp, 2)):
                    for c in range(2):
                        for k in range(n):
                            m = pe.matmul(dst[:, c * 512:(c + 1) * 512], a_T[:, k, :], w[:, k, c * 512:(c + 1) * 512],
                                          start=(k == 0), stop=(k == n - 1))
                m.then_inc(g_mm, 1)

        @block.vector
        def _(dve):
            n_step = [0]

            def link(ins):
                ins.then_inc(step, 1)
                n_step[0] += 1
                dve.wait_ge(step, n_step[0])

            n_var = [0]

            def layer_norm(src, dst, g, b, slot, done, middle=lambda: None):
                dve.bn_stats(stats[:, 0, :], src[:, 0:512]).then_inc(step, 1)
                n_step[0] += 1
                link(dve.bn_stats(stats[:, 1, :], src[:, 512:1024]))
                link(dve.bn_aggr(mv, stats))
                dve.tensor_scalar(vareps[:, slot, :], mv[:, 1:2], EPS, None, ALU.add).then_inc(var_rdy, 1)
                n_var[0] += 1
                dve.wait_ge(rstd_rdy, n_var[0])
                link(dve.tensor_scalar(dst, src, mv[:, 0:1], rs[:, slot, :], ALU.subtract, ALU.mult))
                link(dve.tensor_tensor(dst, dst, g, ALU.mult))
                dve.tensor_tensor(dst, dst, b, ALU.add).then_inc(done, 1)

            dve.wait_ge(const_in, 16 * 9)
            link(dve.tensor_copy(posf, posi))
            link(dve.tensor_tensor(ang, posf.unsqueeze(2).broadcast_to([P, NT, HALF]),
                                   inv.unsqueeze(1).broadcast_to([P, NT, HALF]), ALU.mult))
            MAGIC = 1.5 * 2.0 ** 23
            TWO_PI = 6.283185307179586
            parts = [6.28125, 0.00193500518798828125, 3.0199159819567e-07]
            link(dve.tensor_scalar(tn, ang, 1.0 / TWO_PI, MAGIC, ALU.mult, ALU.add))
            link(dve.tensor_scalar(tn, tn, -MAGIC, None, ALU.add))
            src = ang
            for c in parts:
                link(dve.scalar_tensor_tensor(tr, tn, -c, src, ALU.mult, ALU.add))
                src = tr
            link(dve.tensor_scalar(tc, tr, TWO_PI / 4, None, ALU.add))
            link(dve.tensor_scalar(tw, tc, TWO_PI / 2, -TWO_PI, ALU.is_gt, ALU.mult))
            link(dve.tensor_tensor(tc, tc, tw, ALU.add))
            PI_IN = 3.1415925
            link(dve.tensor_scalar(tr, tr, PI_IN, -PI_IN, ALU.min, ALU.max))
            dve.tensor_scalar(tc, tc, PI_IN, -PI_IN, ALU.min, ALU.max).then_inc(ang_rdy, 1)
            link(dve.tensor_tensor(lam4[:, 0, :], lam4[:, 0, :], lam4[:, 1, :], ALU.mult))
            link(dve.tensor_tensor(lam4[:, 1, :], lam4[:, 2, :], lam4[:, 3, :], ALU.mult))
            dve.tensor_reduce(lam2[:, 0:2], lam4[:, 0:2, :], AX.X, ALU.add).then_inc(lam_in, 1)
            dve.wait_ge(lam_out, 1)
            link(dve.tensor_tensor(neglam, lam2[:, 3:4], lam2[:, 2:3], ALU.subtract))
            link(dve.tensor_scalar(neglam, neglam, -LAMBDA_INIT, None, ALU.add))
            link(dve.tensor_scalar(subg, subg, 1.0 - LAMBDA_INIT, None, ALU.mult))
            for t in range(NT):
                dve.wait_ge(x_in[t], 16)
                layer_norm(h0[:, t, :], h0[:, t, :], g_emb, b_emb, t % 2, ln_rdy)
            dve.wait_ge(rope_rdy, 4)
            n_own = 0
            for g in ROPED[:2]:
                for t in range(NT):
                    r = ROPED.index(g) * NT + t
                    nh = 8 if g == 0 else 1
                    src = raw[r % 2][:, 0:nh * HD].rearrange("p (h j c) -> p h j c", j=2, c=HALF)
                    dst = rot[r % 2][:, 0:nh * HD].rearrange("p (h j c) -> p h j c", j=2, c=HALF)
                    tmp = rot2[:, 0:nh * HD].rearrange("p (h j c) -> p h j c", j=2, c=HALF)
                    dve.wait_ge(pj_out, g * NT + t + 1)
                    if r >= 2:
                        dve.wait_ge(t_rdy, T_LN + r - 1)
                    if r >= 1:
                        dve.wait_ge(rot_rdy, r)
                    cb = cosd[:, t, :].rearrange("p (j c) -> p j c", j=2).unsqueeze(1).broadcast_to([P, nh, 2, HALF])
                    sb_ = sind[:, t, :].rearrange("p (j c) -> p j c", j=2).unsqueeze(1).broadcast_to([P, nh, 2, HALF])
                    dve.tensor_tensor(dst, src, cb, ALU.mult).then_inc(rope_own, 1)
                    dve.tensor_tensor(tmp, src[:, :, ::-1, :], sb_, ALU.mult).then_inc(rope_own, 1)
                    n_own += 2
                    dve.wait_ge(rope_own, n_own)
                    if g == 0:
                        dve.tensor_tensor(dst, dst, tmp, ALU.add).then_inc(rot_rdy, 1)
                    else:
                        dve.tensor_scalar(iws[:, t, :], raw[r % 2][:, HD:HD + 8], WSCALE, None, ALU.mult).then_inc(iw_rdy, 1)
                        link(dve.tensor_tensor(dst, dst, tmp, ALU.add))
                        dve.tensor_copy(rot[r % 2][:, HD:2 * HD], rot[r % 2][:, 0:HD]).then_inc(rot_rdy, 1)
            dve.wait_ge(iw_rdy, NT)
            for u in range(N_IDX):
                t, h = 2 + u // 8, u % 8
                n = P * (t + 1)
                dve.wait_ge(l_act, u + 1)
                if u:
                    dve.wait_ge(rel_used, u)
                if h == 0:
                    dve.tensor_scalar(score[t], rel[u % 2][:, 0:n], iws[:, t, h:h + 1], None, ALU.mult).then_inc(rel_used, 1)
                else:
                    dve.scalar_tensor_tensor(score[t], rel[u % 2][:, 0:n], iws[:, t, h:h + 1], score[t], ALU.mult,
                                             ALU.add).then_inc(rel_used, 1)
            dve.wait_ge(rel_used, N_IDX)
            for t in range(NT):
                n = P * (t + 1)
                if t < 2:
                    link(dve.memset(score[t], 0.0))
                    link(dve.memset(score[t][0:CH, n - CH:n], MASK))
                    continue
                link(dve.memset(score[t][0:CH, n - CH:n], FILL))
                for _ in range(NKEEP // 8):
                    link(dve.max(m8, score[t]))
                    link(dve.match_replace(score[t], m8, score[t], TAKEN))
                link(dve.tensor_scalar(score[t], score[t], 0.5 * (FILL + TAKEN), MASK, ALU.is_gt, ALU.mult))

            def bc(v, dims, *axes):
                for ax in axes:
                    v = v.unsqueeze(ax)
                return v.broadcast_to([P, *dims])

            chosen = tmp1.rearrange("p (t e) -> p t e", t=NT)

            def rank_groups():
                dve.wait_ge(sig_rdy, 1)
                dve.wait_ge(rb_in, 16)
                dve.wait_ge(rc, N_RC)
                link(dve.tensor_tensor(biased, sig, bc(rbias, (NT, NE), 1), ALU.add))
                b_g = biased.rearrange("p t (g e) -> p (t g) e", g=NG)
                for i in range(NT * NG):
                    m = dve.max(g8[:, i, :], b_g[:, i, :])
                link(m)
                gs_f = gs.rearrange("p t g -> p (t g)")
                link(dve.tensor_tensor(gs_f, g8[:, :, 0], g8[:, :, 1], ALU.add))
                shape4 = dict(t=NT, g=NG)
                t1, t2 = (v.rearrange("p (t g e) -> p t g e", **shape4) for v in (tmp1, tmp2))
                other, own = bc(gs, (NT, NG, NG), 2), bc(gs, (NT, NG, NG), 3)
                link(dve.tensor_tensor(t1, other, own, ALU.is_gt))
                link(dve.tensor_tensor(t2, other, own, ALU.is_equal))
                link(dve.tensor_tensor(t2, t2, bc(tri, (NT, NG, NG), 1), ALU.mult))
                link(dve.tensor_tensor(t1, t1, t2, ALU.add))
                link(dve.tensor_reduce(gpen, t1, AX.X, ALU.add))
                link(dve.tensor_scalar(gpen, gpen, float(TOPG), -MASK, ALU.is_lt, ALU.mult))
                link(dve.tensor_scalar(gpen, gpen, MASK, None, ALU.add))
                b4 = biased.rearrange("p t (g e) -> p t g e", g=NG)
                link(dve.tensor_tensor(b4, b4, bc(gpen, (NT, NG, NG), 3), ALU.add))

            def choose_experts():
                for t in range(NT):
                    m = dve.max(g8[:, t, :], biased[:, t, :])
                link(m)
                for t in range(NT):
                    m = dve.match_replace(biased[:, t, :], g8[:, t, :], biased[:, t, :], FILL)
                link(m)
                link(dve.tensor_scalar(chosen, biased, 0.1 * FILL, None, ALU.is_lt))
                dve.tensor_copy(sel_b, chosen).then_inc(sel_rdy, 1)

            def weigh():
                link(dve.tensor_tensor(gate, sig, chosen, ALU.mult))
                link(dve.tensor_reduce(den8, gate, AX.X, ALU.add))
                link(dve.reciprocal(den8, den8))
                link(dve.tensor_scalar(den8, den8, ROUTED, None, ALU.mult))
                link(dve.tensor_tensor(gate, gate, bc(den8, (NT, NE), 2), ALU.mult))

            def count_blocks():
                dve.wait_ge(pos_rdy, 1)
                over = tmp2[:, 0:NE * 7].rearrange("p (e k) -> p e k", k=7)
                link(dve.tensor_tensor(over, bc(pa[0][:, NE:2 * NE], (NE, 7), 2), bc(thr, (NE, 7), 1), ALU.is_gt))
                link(dve.tensor_reduce(nblk, over, AX.X, ALU.add))
                link(dve.tensor_scalar(nblk, nblk, 1.0, None, ALU.add))
                link(dve.memset(bend[:, 0:1], float(SHB)))
                link(dve.tensor_tensor_scan(bend[:, 1:NE + 1], nblk, zer, float(SHB), ALU.add, ALU.add))
                ends = tmp3[:, 0:2 * (NE + 1)].rearrange("p (c e) -> p c e", c=2)
                link(dve.tensor_tensor(ends, bc(bend, (2, NE + 1), 1), bc(itg, (2, NE + 1), 2), ALU.is_le))
                link(dve.tensor_reduce(eobc, ends, AX.X, ALU.add))
                dve.tensor_scalar(eobc, eobc, float(NE), None, ALU.min).then_inc(eob_rdy, 1)

            def place_tokens():
                link(dve.tensor_tensor(nblk, bend[:, 1:NE + 1], nblk, ALU.subtract))
                link(dve.tensor_scalar(nblk, nblk, float(P), 1.0, ALU.mult, ALU.add))
                pos = tmp2.rearrange("p (t e) -> p t e", t=NT)
                link(dve.tensor_tensor(pos, lg[0][:, 512:1024].rearrange("p (t e) -> p t e", t=NT), bc(nblk, (NT, NE), 1), ALU.add))
                link(dve.tensor_tensor(pos, pos, chosen, ALU.mult))
                link(dve.tensor_scalar(slotm[:, :, 1:NE + 1], pos, -1.0, None, ALU.add))

            def write_tables():
                dve.wait_ge(eob_row, 1)
                dve.tensor_scalar(bend_i[0:1, :], bend[0:1, :], -float(SHB), None, ALU.add).then_inc(tab_rdy, 1)
                dve.tensor_copy(tab[0:1, :], pa[1][0:1, 256:256 + 2 * P]).then_inc(tab_rdy, 1)
                dve.wait_ge(tab_rdy, 2)

            def slots_of_tokens():
                for t in range(NT):
                    m = dve.max(slot8[:, t, :], slotm[:, t, 1:NE + 1])
                link(m)
                link(dve.tensor_copy(slot8i, slot8))

            def gates_by_slot(tiles):
                hit = tmp1.rearrange("p (k e) -> p k e", k=TOPK)
                for t in tiles:
                    link(dve.tensor_tensor(hit, bc(slotm[:, t, 1:NE + 1], (TOPK, NE), 1), bc(slot8[:, t, :], (TOPK, NE), 2), ALU.is_equal))
                    link(dve.tensor_tensor(hit, hit, bc(gate[:, t, :], (TOPK, NE), 1), ALU.mult))
                    m = dve.tensor_reduce(gate8[:, t, :], hit, AX.X, ALU.add)
                    if t < NT - 1:
                        link(m)
                    else:
                        m.then_inc(g8_rdy, 1)

            def one_hot(n, e):
                if isinstance(n, int) and n == 1:
                    dve.memset(gbase, float(SHB * P)).then_inc(gb_own, 1)
                else:
                    dve.wait_ge(tok_rdy, n - 1)
                dve.wait_ge(gb_own, n)
                column = slotm[:, :, bass.ds(e, 1)].broadcast_to([P, NT, P])
                dve.scalar_tensor_tensor(onehot, column, gbase, bc(iota_s, (NT, P), 1), ALU.subtract,
                                         ALU.is_equal).then_inc(oh_rdy, 1)
                dve.wait_ge(oh_rdy, n)
                dve.tensor_scalar(gbase, gbase, float(P), None, ALU.add).then_inc(gb_own, 1)

            def indices(n, i):
                dve.wait_ge(tok_rdy, n)
                dve.tensor_scalar(idx[:, i], pa[0][:, 0:1], pa[0][:, 1:2], None, ALU.add).then_inc(idx_rdy, 1)

            def hidden(g):
                dve.wait_ge(silu_rdy, g + 1)
                dve.tensor_tensor(hid, sg, lg[0][:, ED:2 * ED], ALU.mult).then_inc(hid_rdy, 1)

            def y_read(g):
                dve.wait_ge(down_done, g + 1)
                if not isinstance(g, int) or g > 0:
                    dve.wait_ge(y_st, g * 16)
                dve.tensor_copy(y_sb, lg[1][:, :]).then_inc(y_out, 1)

            def hidden_t(g):
                dve.wait_ge(hT_trn, g + 1)
                dve.tensor_copy(hidT, pa[1][:, 0:2 * P].rearrange("p (j q) -> p j q", j=2)).then_inc(hT_rdy, 1)

            def row_remainders(r):
                for b in range(2):
                    dve.wait_ge(xh_rdy, r * 2 + (b + 1))
                    dve.tensor_tensor(xTl[:, 4 * b:4 * b + 4, :], tp[b].rearrange("p (a b) -> p a b", b=P),
                                      xTh[:, 4 * b:4 * b + 4, :], ALU.subtract).then_inc(t_out, 1)

            def last_remainders(n, j):
                dve.wait_ge(uh_rdy, n * 6 + (3 * j + 3))
                dve.tensor_tensor(w_ul[j][:, CUT[2]:], w_ru[j][:, CUT[2]:], w_uh[j][:, CUT[2]:], ALU.subtract).then_inc(ud_rdy, 1)

            def shared(b):
                if b == 6:
                    indices(1, slice(1, 2))
                if b == 7:
                    indices(2, slice(0, 1))
                hidden(b)
                if b:
                    y_read(b - 1)
                hidden_t(b)
                if b == 2:
                    rank_groups()
                if b == 3:
                    choose_experts()
                    weigh()
                if b == 4:
                    count_blocks()
                    place_tokens()
                if b == 5:
                    write_tables()
                    one_hot(1, 1)
                    slots_of_tokens()
                if b == 6:
                    one_hot(2, dve.value_load(tab[0:1, SHB + 1:SHB + 2], min_val=0, max_val=NE))
                    gates_by_slot(range(NT // 2))
                if b == 7:
                    gates_by_slot(range(NT // 2, NT))
                    one_hot(3, dve.value_load(tab[0:1, SHB + 2:SHB + 3], min_val=0, max_val=NE))
                    row_remainders(0)
                    last_remainders(0, 0)
                    indices(3, slice(1, 2))

            lu = N_IDX
            n_exp = 0
            n_dl = [0]
            for what, i in order:
                if what == "task" and i < NTK:
                    t, k = TASKS[i]
                    n = P * (t + 1)
                    if k < AH:
                        q = prob[prob_at[i][0]]
                        dve.wait_ge(l_rdy, lu + 1)
                        if prob_prev[i] >= 0:
                            dve.wait_ge(t_rdy, turned_at["task", prob_prev[i]])
                        dve.tensor_tensor_reduce(out=q[:, 0:n], in0=lg[lu % 2][:, 0:n], in1=score[t], scale=1.0,
                                                 scalar=-3.0e38, op0=ALU.add, op1=ALU.max,
                                                 accum_out=mx[:, k:k + 1]).then_inc(l_dve, 1)
                        n_dl[0] += 1
                        dve.wait_ge(l_dve, n_dl[0])
                        dve.tensor_scalar(nmx[:, k:k + 1], mx[:, k:k + 1], -SCALE, None, ALU.mult).then_inc(mx_rdy, 1)
                        lu += 1
                        n_exp += 1
                    else:
                        for j in range(2):
                            c = AH + 2 * (k - AH) + j
                            dve.wait_ge(l_rdy, lu + 1)
                            link(dve.tensor_reduce(mx[:, c:c + 1], lg[lu % 2][:, 0:n], AX.X, ALU.max))
                            dve.tensor_scalar(nmx[:, c:c + 1], mx[:, c:c + 1], -SCALE, None, ALU.mult).then_inc(mx_rdy, 1)
                            lu += 1
                        n_exp += 2
                        dve.wait_ge(e_rdy, n_exp)
                        s = ssum[t % 2]
                        p0, p1 = (prob[q][:, 0:n] for q in prob_at[i])
                        link(dve.reciprocal(rsum[:, c:c + 1], s[:, c:c + 1]))
                        link(dve.scalar_tensor_tensor(cB[:, 0:1], s[:, c - 1:c], neglam, rsum[:, c:c + 1], ALU.mult, ALU.mult))
                        dve.scalar_tensor_tensor(p0, p1, cB[:, 0:1], p0, ALU.mult, ALU.add).then_inc(cmb_rdy, 1)
                        dve.wait_ge(cmb_rdy, BH * t + k - AH + 1)
                if what == "task" and i >= 2 and TASKS[i - 2][1] == AH + BH - 1:
                    t = TASKS[i - 2][0]
                    s = ssum[t % 2]
                    dve.wait_ge(pv_done, i - 1)
                    dve.wait_ge(e_rdy, (t + 1) * 16)
                    link(dve.reciprocal(rsum, s))
                    link(dve.tensor_tensor(mix[:, 0:512].rearrange("p (h c) -> p h c", h=AH),
                                           pa[0][:, :].rearrange("p (h c) -> p h c", h=AH),
                                           rsum[:, 0:AH].unsqueeze(2).broadcast_to([P, AH, HD]), ALU.mult))
                    mb = mix[:, 512:1024].rearrange("p (h c) -> p h c", h=BH)
                    link(dve.tensor_tensor(mb, pa[1][:, :].rearrange("p (h c) -> p h c", h=BH),
                                           rsum[:, AH:AH + 2 * BH:2].unsqueeze(2).broadcast_to([P, BH, P]), ALU.mult))
                    link(dve.tensor_tensor(sq, mb, mb, ALU.mult))
                    link(dve.tensor_reduce(ms, sq, AX.X, ALU.add))
                    dve.tensor_scalar(ms, ms, 1.0 / P, EPS, ALU.mult, ALU.add).then_inc(sq_rdy, 1)
                    dve.wait_ge(rms_rdy, t + 1)
                    link(dve.tensor_tensor(mb, mb, rms.unsqueeze(2).broadcast_to([P, BH, P]), ALU.mult))
                    dve.tensor_tensor(mb, mb, subg.unsqueeze(1).broadcast_to([P, BH, P]), ALU.mult).then_inc(mix_rdy, 1)
                if what == "mix":
                    dve.wait_ge(l_rdy, lu + 1)
                    dve.wait_ge(hin_s, 16 * (i + 1))
                    if i:
                        dve.wait_ge(h1_st, 16 * i)
                        dve.wait_ge(t_rdy, turned_at["rows", i - 1])
                    else:
                        dve.wait_ge(rows_in, 48)
                    dve.scalar_tensor_tensor(h1, h_in, ALPHA, lg[lu % 2][:, :], ALU.mult, ALU.add).then_inc(l_dve, 1)
                    n_dl[0] += 1
                    dve.wait_ge(l_dve, n_dl[0])
                    lu += 1
                    layer_norm(h1, h1, g1, b1, 0, h1_rdy)
                if what == "shared":
                    shared(i)

            n_routed = dve.value_load(bend_i[0:1, NE:NE + 1], min_val=NE, max_val=MAXB - SHB)

            def ahead(r):
                e3 = dve.value_load(tab[0:1, bass.ds(r + (SHB + 3), 1)], min_val=0, max_val=NE)
                one_hot(r + 4, e3)

            def routed(r):
                hidden(r + SHB)
                row_remainders(r + 1)
                indices(r + 4, bass.ds(dve.value_load(parity[0:1, bass.ds(r, 1)], min_val=0, max_val=1), 1))
                src = pa[1][:, 0:2 * P].rearrange("p (j q) -> p j q", j=2)
                dve.wait_ge(hT_trn, r + (SHB + 1))
                dve.tensor_copy(hidTh, src).then_inc(hh_rdy, 1)
                dve.wait_ge(hh_rdy, r + 1)
                dve.tensor_tensor(hidTl, src, hidTh, ALU.subtract).then_inc(hT_rdy, 1)

            def first(n, j, r):
                ahead(r)
                if j == 0:
                    last_remainders(n, 1)
                elif not isinstance(n, int) or n < NE // 2 - 1:
                    last_remainders(n + 1, 0)
                dve.wait_ge(dh_rdy, n * 2 + (j + 1))
                dve.tensor_tensor(w_dl[j], w_rd[j], w_dh[j], ALU.subtract).then_inc(dl_rdy, 1)
                routed(r)

            def more(n, j, r):
                ahead(r)
                routed(r)

            for_experts(dve, first, more)
            dve.wait_ge(ple_in, 16 * 5)

            def finish(t):
                a = acc[t % 2]
                dve.wait_ge(g_mm, t + 1)
                if t:
                    dve.wait_ge(o_rdy, t)
                dve.tensor_tensor(zt, lg[0][:, :], bp, ALU.add).then_inc(z_rdy, 1)
                dve.wait_ge(s_rdy, t + 1)
                if t >= 2:
                    dve.wait_ge(o_st[t % 2], 16 * (t // 2))
                link(dve.tensor_tensor(ot[t % 2], zt, lg[1][:, :], ALU.mult))
                dve.tensor_tensor(ot[t % 2], ot[t % 2], a, ALU.add).then_inc(o_rdy, 1)

            for t in range(NT):
                a = acc[t % 2]
                dve.wait_ge(row_in[t % 2], 48 * (t // 2 + 1))
                link(dve.scalar_tensor_tensor(a, a, ALPHA, ysh[t % 2], ALU.mult, ALU.add))
                for k in range(TOPK):
                    dve.wait_ge(y_in[k], 16 * (t + 1))
                    dve.scalar_tensor_tensor(a, yk[k], gate8[:, t, k:k + 1], a, ALU.mult, ALU.add).then_inc(y_used, 1)
                    dve.wait_ge(y_used, 8 * t + k + 1)
                layer_norm(a, a, g2, b2, 0, h2_rdy)
                if t:
                    finish(t - 1)
            finish(NT - 1)


_INS = ["x", "p", "positions", "ln_emb_g", "ln_emb_b", "w_in", "w_o", "diff_lq1", "diff_lk1", "diff_lq2", "diff_lk2",
        "diff_subln_g", "ln1_g", "ln1_b", "w_router", "router_bias", "w_exp_gate", "w_exp_up", "w_exp_down",
        "w_sh_gate", "w_sh_up", "w_sh_down", "ln2_g", "ln2_b", "w_ple_gate", "b_ple_gate", "w_ple_proj"]


def kernel(**inputs):
    import numpy as np
    import concourse.bacc as bacc
    from concourse.bass_utils import run_bass_kernel_spmd as run

    nc = bacc.Bacc("TRN2", target_bir_lowering=False, num_devices=1)
    arrays, args = {}, []
    host = {n: np.ascontiguousarray(inputs[n]) for n in _INS}
    host["inv_freq"] = np.float32(10000.0) ** (-np.arange(0, HD, 2, dtype=np.float32) / np.float32(HD))
    for name, a in host.items():
        arrays[f"in_{name}"] = a
        args.append(nc.dram_tensor(f"in_{name}", a.shape, mybir.dt.from_np(a.dtype), kind="ExternalInput").ap())
    args.append(nc.dram_tensor("out_0", (1, S, D), F32, kind="ExternalOutput").ap())
    build(nc, *args)
    return run(nc, [arrays], core_ids=[0]).results[0]["out_0"]
```

```python
from contextlib import ExitStack

import concourse.bass as bass
from concourse import mybir

F32 = mybir.dt.float32
F32R = mybir.dt.float32r
BF16 = mybir.dt.bfloat16
I32 = mybir.dt.int32
U32 = mybir.dt.uint32
ALU = mybir.AluOpType
ACT = mybir.ActivationFunctionType
AX = mybir.AxisListType

P = 128
D = 1024
S = 1024
NT = S // P
KC = D // P
HD = 64
HALF = HD // 2
AH = 8
BH = 4
CH = 64
NKEEP = 256
ALPHA = 2.0 ** 0.25
EPS = 1e-5
LAMBDA_INIT = 0.8 - 0.6
SCALE = HD ** -0.5
WSCALE = (8 ** -0.5) * (64 ** -0.5)
NE = 64
NG = 8
TOPG = 4
TOPK = 8
ED = 256
ROUTED = 2.5
PLE = 256
MASK = -1e30
FILL = -3.0e38
TAKEN = -3.4e38
SHB = NT
MAXB = SHB + (S * TOPK + NE * P) // P
UW, DW = KC * 2 * ED, 2 * D
EW = UW + DW
CUT = (0, 1280, 2560, UW)

C_QA, C_KA, C_VA, C_QI, C_KI, C_QB, C_KB, C_VB = 0, 512, 1024, 1536, 2048, 2120, 2632, 3144
GROUPS = [("qi", C_QI, 512), ("ki", C_KI, 72), ("va", C_VA, 512), ("vb", C_VB, 512),
          ("qa", C_QA, 512), ("ka", C_KA, 512), ("kb", C_KB, 512), ("qb", C_QB, 512)]
NGR = len(GROUPS)
ROPED = [g for g, (n, _, _) in enumerate(GROUPS) if n[0] in "qk"]


def build(nc, x, p, positions, ln_emb_g, ln_emb_b, w_in, w_o, lq1, lk1, lq2, lk2, subln_g, ln1_g, ln1_b,
          w_router, router_bias, w_gate, w_up, w_down, w_sh_gate, w_sh_up, w_sh_down, ln2_g, ln2_b,
          w_ple_gate, b_ple_gate, w_ple_proj, inv_freq, out):
    x_t = x.rearrange("a (t q) d -> t (a q) d", q=P)
    out_t = out.rearrange("a (t q) d -> t (a q) d", q=P)
    p_t = p.rearrange("l a (t q) d -> t (l a q) d", q=P)
    w_in_k = w_in.rearrange("l (k q) n -> q (l k) n", q=P)
    w_o_k = w_o.rearrange("l (k q) n -> q (l k) n", q=P)
    w_r_k = w_router.rearrange("l (k q) n -> q (l k) n", q=P)
    w_pg_k = w_ple_gate.rearrange("l (k q) n -> q (l k) n", q=P)
    w_pp_k = w_ple_proj.rearrange("l (k q) n -> q (l k) n", q=P)
    w_g_e = w_gate.rearrange("l e (q k) f -> (l e) q (k f)", q=P)
    w_u_e = w_up.rearrange("l e (q k) f -> (l e) q (k f)", q=P)
    w_d_e = w_down.rearrange("l e (q k) f -> (l e) q (k f)", q=P)
    w_sg = w_sh_gate.rearrange("l (q k) f -> q (l k f)", q=P)
    w_su = w_sh_up.rearrange("l (q k) f -> q (l k f)", q=P)
    w_sd = w_sh_down.rearrange("l (q k) f -> q (l k f)", q=P)

    h_d = nc.dram_tensor("h_emb", (S, D), F32).ap()
    h1_d = nc.dram_tensor("h_mix", (S, D), F32).ap()
    y_d = nc.dram_tensor("y_slots", (MAXB * P, D), F32).ap()

    ctx = ExitStack()
    with ctx:
        arena = ctx.enter_context(nc.sbuf_tensor("arena", [P, 53200], F32))
        base = nc.sbuf_base - 53200 * 4
        n_at = [0]

        def at(off, *dims, dt=F32):
            n = 1
            for d in dims:
                n *= d
            n_at[0] += 1
            v = nc.alloc_sbuf_tensor_at(f"at{off}_{n_at[0]}", [P, n], dt, offset=base + 4 * off, align_bytes=4)[:, :]
            if len(dims) == 1:
                return v
            names = "abcd"[:len(dims)]
            return v.rearrange(f"p ({' '.join(names)}) -> p {' '.join(names)}", **dict(zip(names[1:], dims[1:])))

        hT = at(0, KC, S)
        w_sl = [at(8192, KC, 512), at(12288, KC, 512)]
        raw = [at(16384, 512), at(16896, 512)]
        rot = [at(17408, 512), at(17920, 512)]
        rot2 = at(18432, 512)
        rel = [at(18944, 1024), at(19968, 1024)]
        qiT = qbT = at(20992, 4, S)
        kiT = at(25088, S)
        qaT, kaT, kbT = at(26112, 4, S), at(30208, 4, S), at(34304, 4, S)
        va, vb = at(38400, NT, 512), at(42496, NT, 512)
        h0 = at(26112, NT, D)
        g_emb, b_emb = at(34304, D), at(35328, D)
        off_sc = [46592 + 64 * t * (t + 1) for t in range(NT)]
        score = [at(off_sc[t], P * (t + 1)) for t in range(NT)]
        wo = at(0, KC, D)
        prob = [at(8192 + 1024 * i, 1024) for i in range(4)]
        pT = [at(12288 + 1024 * i, NT, P) for i in range(2)]
        mix = at(14336, D)
        mixT = at(15360, KC, P)
        h_in = at(16384, D)
        h1 = at(17408, D)
        g1, b1 = at(18432, D), at(19456, D)
        sq = at(20480, BH, P)
        wr = at(25088, KC, NE)
        rl = at(25600, NT, NE)
        w_ru = [at(i * EW, UW) for i in range(2)]
        w_rd = [at(i * EW + UW, DW) for i in range(2)]
        w_uh = [at(12288 + 8192 * i, UW, dt=F32R) for i in range(2)]
        w_ul = [at(16384 + 8192 * i, UW, dt=F32R) for i in range(2)]
        w_dh = [at(o, DW, dt=F32R) for o in (32768, 28672)]
        w_dl = [at(o, DW, dt=F32R) for o in (34816, 30720)]
        y_sb = at(46160, D)
        hidTh, hidTl = at(40448, 2, P, dt=F32R), at(36864, 2, P, dt=F32R)
        xTh, xTl = at(38400, KC, P, dt=F32R), at(42768, KC, P, dt=F32R)
        xg = [at(o, D) for o in (37376, 44304)]
        xT = at(38400, KC, P)
        onehot = at(39424, NT, P, dt=BF16)
        sg, hid, hidT = at(39936, ED), at(40192, ED), at(40448, 2, P)
        slotm = at(40704, NT, NE + 1)
        gate = at(41224, NT, NE)
        iota_s = at(41736, P)
        slot8 = at(41864, NT, TOPK)
        slot8i = at(41928, NT, TOPK, dt=U32)
        gate8 = at(41992, NT, TOPK)
        tab = at(42056, 2 * P, dt=I32)
        bend_i = at(42568, NE + 1, dt=I32)
        bend = at(42636, NE + 1)
        nblk = at(42704, NE)
        sig, biased = at(42768, NT, NE), at(43280, NT, NE)
        tmp1, tmp2, tmp3 = at(43792, 512), at(44304, 512), at(44816, 512)
        sel_b = at(45328, NT, NE, dt=BF16)
        g8 = at(45584, NT * NG, 8)
        rbias = at(46096, NE)

        def up_v(w):
            return w.rearrange("p (j k f) -> p j k f", j=2, k=KC)

        def dn_v(w):
            return w.rearrange("p (j n) -> p j n", j=2)

        w_sh = at(26112, EW)
        sh_up_v, sh_dn_v = up_v(w_sh[:, 0:UW]), dn_v(w_sh[:, UW:EW])
        xg_v = [v.rearrange("p (q k) -> p k q", k=KC) for v in xg]
        hid_v = hid.rearrange("p (q j) -> p j q", j=2)
        wpg, wpp = at(0, KC, D), at(8192, 2, D)
        g2, b2, bp = at(47184, D), at(48208, D), at(49232, D)
        acc = [at(o, D) for o in (12288, 13312, 29696)]
        ysh = [at(o, D) for o in (14336, 15360, 30720)]
        yk = [at(16384 + 1024 * i, D) for i in range(8)]
        h2T = at(24576, KC, P)
        zt, ot = at(25600, D), [at(26624 + 1024 * i, D) for i in range(2)]
        pt_sb = [at(28672 + 256 * i, PLE) for i in range(3)]
        ppT = at(29440, 2, P)
        ident = at(51200, P)
        cosd, sind = at(51328, NT, HD), at(51840, NT, HD)
        used = [52352]

        def small(*dims, dt=F32):
            n = 1
            for d in dims:
                n *= d
            o = used[0]
            used[0] += (n + 1) // 2 if dt == BF16 else n
            assert used[0] <= 53200, used
            return at(o, *dims, dt=dt)

        iws = small(NT, 8)
        stats, mv = small(2, 6), small(2)
        rs = small(2, 1)
        vareps = small(2, 1)
        mhalf = small(8)
        m8 = small(8)
        mx, nmx = small(12 + BH), small(12 + BH)
        ssum = [small(12 + BH) for _ in range(2)]
        rsum = small(12 + BH)
        cB = small(2)
        ms = small(BH)
        rms = small(BH)
        subg = small(P)
        lam2 = small(4)
        neglam = small(1)
        posi, posf = small(NT, dt=I32), small(NT)
        rowneg = small(HD)
        colq = small(P)
        tokpair = small(NT, 2, dt=BF16)
        gbase = small(1)
        idx = small(2, dt=U32)
        parity = at(37120, 2 * P, dt=I32)
        ang = at(46592, NT, HALF)
        tn, tr, tc, tw = (at(46592 + 256 * i, NT, HALF) for i in range(1, 5))
        inv = at(48128, HALF)
        lam4 = at(48192, 4, HD)
        thr = at(50432, 7)
        tri = at(50496, NG, NG)
        gs = at(50560, NT, NG)
        gpen = at(50624, NT, NG)
        den8 = at(50688, NT)
        eobc = at(50696, 2)
        itg = at(50700, 2)
        zer = at(50712, NE)
        ones_b = at(50784, P, dt=BF16)
        upper_b = at(50848, P, dt=BF16)

        tp = [ctx.enter_context(nc.psum_tensor(f"turn{i}", [P, 512], F32)) for i in range(2)]
        lg = [ctx.enter_context(nc.psum_tensor(f"logit{i}", [P, 1024], F32)) for i in range(2)]
        pa = [ctx.enter_context(nc.psum_tensor(f"acc{i}", [P, 512], F32)) for i in range(2)]

        def sem(name):
            return ctx.enter_context(nc.semaphore(name))

        consts = sem("consts")
        const_in = sem("const_in")
        emb_in = sem("embedding_norm_in")
        x_in = [sem(f"x_in{t}") for t in range(NT)]
        step = sem("dve_step")
        var_rdy = sem("var_rdy")
        rstd_rdy = sem("rstd_rdy")
        ln_rdy = sem("ln_rdy")
        h_st = sem("h_stored")
        t_rdy = sem("turn_ready")
        t_out = sem("turn_out")
        ang_rdy = sem("angles_ready")
        rope_rdy = sem("rope_tables")
        w_in_s = [sem(f"w_in{i}") for i in range(2)]
        pj_rdy = sem("proj_ready")
        pj_out = sem("proj_out")
        rope_own = sem("rope_steps")
        rope_own2 = sem("rope_steps_pool")
        rot_rdy = sem("rotated")
        l_rdy = sem("logits_ready")
        l_act = sem("logits_read_act")
        l_dve = sem("logits_read_dve")
        rel_used = sem("relu_used")
        iw_rdy = sem("iw_ready")
        wo_in = sem("wo_in")
        rows_in = sem("rows_in")
        mx_rdy = sem("max_ready")
        e_rdy = sem("exp_ready")
        cmb_rdy = sem("combined")
        pv_done = sem("pv_done")
        sums_read = sem("values_sums_read")
        mix_rdy = sem("mix_ready")
        hin_s = sem("h_in")
        h1_rdy = sem("h1_ready")
        h1_st = sem("h1_stored")
        sq_rdy = sem("mean_square")
        rms_rdy = sem("rms_ready")
        lam_in = sem("lambda_sums")
        lam_out = sem("lambda_exps")
        y_fill = sem("unused_blocks_filled")
        rb_in = sem("router_bias_in")
        rc = sem("routing_consts")
        sig_rdy = sem("sigmoid_ready")
        sel_rdy = sem("chosen_ready")
        pos_rdy = sem("places_ready")
        eob_rdy = sem("block_experts_ready")
        eob_row = sem("block_experts_row")
        tab_rdy = sem("tables_ready")
        sh_in = sem("shared_weights_in")
        xs_got = sem("shared_rows_in")
        ru_in = [sem(f"gate_up_in{i}") for i in range(2)]
        rd_in = [sem(f"down_in{i}") for i in range(2)]
        uh_rdy = sem("gate_up_rounded")
        ul_rdy = sem("gate_up_remainders")
        ud_rdy = sem("gate_up_last_remainders")
        dh_rdy = sem("down_rounded")
        dl_rdy = sem("down_remainders")
        xh_rdy = sem("rows_rounded")
        hh_rdy = sem("hidden_rounded")
        oh_rdy = sem("onehot_ready")
        tok_rdy = sem("tokens_psum")
        idx_rdy = sem("indices_ready")
        gb_own = sem("block_base")
        x_got = [sem(f"rows_gathered{i}") for i in range(2)]
        go = sem("gather_may_start")
        up_done = sem("up_done")
        silu_rdy = sem("silu_ready")
        hid_rdy = sem("hidden_ready")
        hT_trn = sem("hidden_transposed")
        hT_rdy = sem("hiddenT_ready")
        down_done = sem("down_done")
        y_out = sem("y_read")
        y_st = sem("y_stored")
        ple_in = sem("ple_weights_in")
        row_in = [sem(f"tile_in{i}") for i in range(3)]
        y_in = [sem(f"y_in{i}") for i in range(TOPK)]
        y_used = sem("y_used")
        h2_rdy = sem("h2_ready")
        g_mm = sem("gate_products")
        p_mm = sem("input_products")
        m_rdy = sem("gated_ready")
        z_rdy = sem("gate_argument")
        s_rdy = sem("gate_ready")
        o_rdy = sem("out_ready")
        o_st = [sem(f"out_stored{i}") for i in range(2)]

        def for_experts(eng, first, more):
            def pair(n):
                for j in range(2):
                    r = eng.value_load(bend_i[0:1, bass.ds(n * 2 + j, 1)], min_val=0, max_val=MAXB - SHB)
                    end = eng.value_load(bend_i[0:1, bass.ds(n * 2 + (j + 1), 1)], min_val=1, max_val=MAXB - SHB)
                    first(n, j, r)
                    with eng.If(r + 1 < end):
                        with eng.Fori(r + 1, end) as r2:
                            more(n, j, r2)

            pair(0)
            with eng.Fori(1, NE // 2 - 1) as n:
                pair(n)
            pair(NE // 2 - 1)

        block = ctx.enter_context(nc.Block())

        TASKS = [(t, k) for t in range(NT) for k in range(AH + BH)]
        NTK = len(TASKS)
        l_uses = []
        n_free = {"act": 0, "dve": 0, "exp": 0}

        def use_l(who):
            n_free[who] += 1
            l_uses.append((who, n_free[who]))

        for t in range(2, NT):
            for h in range(8):
                use_l("act")
        FINISH_AT = {3: "mix", 8: "rows"}
        order = []
        for i, (t, k) in enumerate(TASKS):
            order.append(("task", i))
            if t > 0 and k in FINISH_AT:
                order.append((FINISH_AT[k], t - 1))
        order += [("task", NTK), ("task", NTK + 1), ("turn", 0), ("shared", 0), ("mix", NT - 1), ("shared", 1)]
        order += [("rows", NT - 1)] + [("shared", b) for b in range(2, SHB)]
        logits_at = {}
        for what, i in order:
            if what == "task" and i < NTK:
                if TASKS[i][1] < AH:
                    use_l("dve")
                    n_free["exp"] += 1
                else:
                    use_l("exp")
                    use_l("exp")
            if what == "mix":
                use_l("dve")
            if what in ("task", "mix"):
                logits_at[what, i] = len(l_uses)
        N_IDX = 6 * 8
        N_RC = 13
        T_LN = 2 * NT
        T_PROJ = NT * len(ROPED)

        def rows_turned(t):
            return 2 * (t + 1) + 2 * max(0, t - 2)

        def rot_turned(r):
            return (2 * min(r // 2 + 3, NT) if r < 2 * NT else T_LN) + r + 1

        def product_of(g, t):
            return 2 * t + g if g < 2 else g * NT + t

        def rotated_of(g, t):
            return 2 * t + g if g < 2 else ROPED.index(g) * NT + t

        BETWEEN = (4, 6, 8, 9, 11)
        rest = [(g, t) for g in range(2, NGR) for t in range(NT)]
        mixed = []
        for t in range(2, NT):
            mixed.append(("index", t, None))
            m = BETWEEN[t - 2] if t < NT - 1 else len(rest)
            mixed += [("project", g, t_) for g, t_ in rest[:m]]
            rest = rest[m:]
        assert not rest and sum(BETWEEN) <= 5 * NT

        def banks(t):
            return (t + 4) // 4

        prob_at, n = [], 0
        for t, k in TASKS:
            w = 1 if k < AH else 2
            prob_at.append([(n + j) % 4 for j in range(w)])
            n += w
        prob_owner = {}
        prob_prev = []
        for i, places in enumerate(prob_at):
            prob_prev.append(max([prob_owner.get(q, -1) for q in places]))
            for q in places:
                prob_owner[q] = i
        turned_at, u = {}, T_LN + T_PROJ
        for what, i in order:
            if what == "task" and 1 <= i <= NTK:
                u += banks(TASKS[i - 1][0])
                turned_at["task", i - 1] = u
            if what == "mix":
                u += 2
                turned_at["mix", i] = u
            if what == "rows":
                u += 3
                turned_at["rows", i] = u
            if what == "turn" or (what == "shared" and i < SHB - 1):
                u += 2
                turned_at["xT", 0 if what == "turn" else i + 1] = u
        assert l_uses[-1][0] == "dve" and len(l_uses) % 2 == 0
        T_ALL = u

        def count_exp(i):
            t, k = TASKS[i] if i < NTK else (NT, 0)
            return t * (AH + 2 * BH) + (k if k < AH else AH + 2 * (k - AH))

        @block.sync
        def _(sp):
            def load_x(t):
                sp.dma_start(h0[:, t, :], x_t[t]).then_inc(x_in[t], 16)

            load_x(0)
            for dst, src in ((g_emb, ln_emb_g), (b_emb, ln_emb_b)):
                sp.dma_start(dst, src.rearrange("(a n) -> a n", a=1).broadcast_to([P, src.shape[0]])).then_inc(emb_in, 16)
            load_x(1)
            _, c0, n = GROUPS[0]
            sp.dma_start(w_sl[0][:, :, 0:n], w_in_k[:, :, c0:c0 + n]).then_inc(w_in_s[0], 16)
            sp.dma_start(inv, inv_freq.rearrange("(a n) -> a n", a=1).broadcast_to([P, HALF])).then_inc(const_in, 16)
            sp.dma_start(posi, positions.rearrange("a (t q) -> q (a t)", q=P),
                         allow_slow_non_contiguous=True).then_inc(const_in, 16)
            for i, v in enumerate((lq1, lk1, lq2, lk2)):
                sp.dma_start(lam4[:, i, :], v.broadcast_to([P, HD])).then_inc(const_in, 16)
            sp.dma_start(subg, subln_g.broadcast_to([P, P])).then_inc(const_in, 16)
            for t in range(2, NT):
                load_x(t)
            for g, (_, c0, n) in enumerate(GROUPS[1:], 1):
                if g >= 2:
                    sp.wait_ge(pj_rdy, NT * max(g - 1, 2))
                sp.dma_start(w_sl[g % 2][:, :, 0:n], w_in_k[:, :, c0:c0 + n]).then_inc(w_in_s[g % 2], 16)
                if g == 1:
                    for t in range(NT):
                        sp.wait_ge(ln_rdy, t + 1)
                        sp.dma_start(h_d[t * P:(t + 1) * P, :], h0[:, t, :]).then_inc(h_st, 16)
            sp.wait_ge(pj_rdy, NT * NGR)
            sp.dma_start(wo, w_o_k).then_inc(wo_in, 16)
            sp.wait_ge(rel_used, N_IDX)
            sp.wait_ge(t_out, T_LN + T_PROJ)
            sp.wait_ge(h_st, 16 * NT)
            sp.dma_start(g1, ln1_g.broadcast_to([P, D])).then_inc(rows_in, 16)
            sp.dma_start(b1, ln1_b.broadcast_to([P, D])).then_inc(rows_in, 16)
            sp.dma_start(wr, w_r_k).then_inc(rows_in, 16)
            for t in range(NT):
                if t:
                    sp.wait_ge(h1_rdy, t)
                sp.dma_start(h_in, h_d[t * P:(t + 1) * P, :]).then_inc(hin_s, 16)
                b = SHB + NE + NT * t
                sp.dma_start(y_d[b * P:(b + NT) * P, :], x.rearrange("a s d -> (a s) d")).then_inc(y_fill, 16)
                if t < NT - 1:
                    sp.wait_ge(h1_rdy, t + 1)
                    sp.dma_start(h1_d[t * P:(t + 1) * P, :], h1).then_inc(h1_st, 16)
            sp.wait_ge(l_rdy, logits_at["task", NTK - BH - 1])
            for m, src in enumerate((w_sg, w_su, w_sd)):
                sp.dma_start(w_sh[:, 2048 * m:2048 * (m + 1)], src).then_inc(sh_in, 16)
            sp.wait_ge(pv_done, NTK)
            sp.dma_start(rbias, router_bias.broadcast_to([P, NE])).then_inc(rb_in, 16)

            def shared_rows(b):
                if b:
                    sp.wait_ge(t_rdy, turned_at["xT", b - 1])
                sp.dma_start(xg[0], h1_d[b * P:(b + 1) * P, :]).then_inc(xs_got, 16)

            def load_up(r, place):
                for m, src in enumerate((w_g_e, w_u_e)):
                    sp.dma_start(w_ru[place][:, 2048 * m:2048 * (m + 1)], src[r]).then_inc(ru_in[place], 16)

            def load_down(r, place):
                sp.dma_start(w_rd[place], w_d_e[r]).then_inc(rd_in[place], 16)

            sp.wait_ge(h1_st, 16 * (NT - 1))
            for b in range(3):
                shared_rows(b)
            sp.wait_ge(l_rdy, logits_at["mix", NT - 1])
            load_up(0, 0)
            load_down(0, 0)
            sp.wait_ge(h1_rdy, NT)
            sp.dma_start(h1_d[(NT - 1) * P:S, :], h1).then_inc(h1_st, 16)
            shared_rows(3)
            sp.wait_ge(t_out, turned_at["rows", NT - 1])
            sp.wait_ge(h1_st, 16 * NT)
            load_up(1, 1)
            load_down(1, 1)
            for b in range(4, SHB):
                shared_rows(b)
            sp.wait_ge(ul_rdy, 2)
            sp.wait_ge(ud_rdy, 1)
            load_up(2, 0)
            sp.wait_ge(down_done, SHB)
            for dst, src in ((g2, ln2_g), (b2, ln2_b), (bp, b_ple_gate)):
                sp.dma_start(dst, src.broadcast_to([P, D])).then_inc(ple_in, 16)
            sp.wait_ge(tab_rdy, 2)

            with sp.Fori(0, (NE - 4) // 2) as n:
                for j in range(2):
                    sp.wait_ge(ul_rdy, n * 4 + (2 * j + 4))
                    sp.wait_ge(ud_rdy, n * 2 + (j + 2))
                    load_up(n * 2 + (j + 3), 1 - j)
                    sp.wait_ge(dl_rdy, n * 2 + (j + 1))
                    load_down(n * 2 + (j + 2), j)
            sp.wait_ge(ul_rdy, 2 * (NE - 2))
            sp.wait_ge(ud_rdy, NE - 2)
            load_up(NE - 1, 1)
            sp.wait_ge(dl_rdy, NE - 3)
            load_down(NE - 2, 0)
            sp.wait_ge(dl_rdy, NE - 2)
            load_down(NE - 1, 1)
            sp.wait_ge(ul_rdy, 2 * NE)
            sp.wait_ge(ud_rdy, NE)
            sp.wait_ge(dl_rdy, NE - 1)
            for dst, src in ((wpg, w_pg_k), (wpp, w_pp_k)):
                sp.dma_start(dst, src).then_inc(ple_in, 16)
            n_routed = sp.value_load(bend_i[0:1, NE:NE + 1], min_val=NE, max_val=MAXB - SHB)
            sp.wait_ge(down_done, n_routed + SHB)
            sp.wait_ge(y_st, n_routed * 16 + SHB * 16)
            for t in range(NT + 2):
                if t < NT:
                    if t >= 3:
                        sp.wait_ge(o_rdy, t - 2)
                    ts = slice(t * P, (t + 1) * P)
                    for dst, src in ((acc[t % 3], h1_d[ts, :]), (ysh[t % 3], y_d[ts, :]), (pt_sb[t % 3], p_t[t])):
                        sp.dma_start(dst, src).then_inc(row_in[t % 3], 16)
                if t >= 2:
                    sp.wait_ge(o_rdy, t - 1)
                    sp.dma_start(out_t[t - 2], ot[t % 2]).then_inc(o_st[t % 2], 16)
            for i in range(2):
                sp.wait_ge(o_st[i], 16 * NT // 2)

        @block.gpsimd
        def _(pool):
            pool.memset(ident, 0.0).then_inc(consts, 1)
            pool.memset(rowneg, MASK).then_inc(consts, 1)
            pool.memset(colq[:, 0:CH], 1.0).then_inc(consts, 1)
            pool.memset(colq[:, CH:P], 0.0).then_inc(consts, 1)
            pool.memset(mhalf, -0.5).then_inc(consts, 1)
            pool.wait_ge(consts, 5)
            pool.affine_select(out=ident, in_=ident, compare_op=ALU.not_equal, fill=1.0, base=0,
                               pattern=[[-1, P]], channel_multiplier=1).then_inc(consts, 1)

            def rsqrt(n, src, dst, done):
                pool.wait_ge(src[1], n)
                pool.tensor_tensor(dst, src[0], mhalf[:, 0:dst.shape[1]], ALU.pow).then_inc(done, 1)

            pool.wait_ge(consts, 6)
            for t in range(NT):
                rsqrt(t + 1, (vareps[:, t % 2, :], var_rdy), rs[:, t % 2, :], rstd_rdy)
            n_rot = 2 * NT
            for g in ROPED[2:]:
                for t in range(NT):
                    u = (ROPED.index(g)) * NT + t
                    src, dst = raw[u % 2].rearrange("p (h j c) -> p h j c", j=2, c=HALF), rot[u % 2].rearrange("p (h j c) -> p h j c", j=2, c=HALF)
                    tmp = rot2.rearrange("p (h j c) -> p h j c", j=2, c=HALF)
                    pool.wait_ge(pj_out, g * NT + t + 1)
                    pool.wait_ge(t_rdy, T_LN + u - 1)
                    pool.wait_ge(rot_rdy, u)
                    if u == n_rot:
                        pool.wait_ge(rope_rdy, 2)
                    cb = cosd[:, t, :].rearrange("p (j c) -> p j c", j=2).unsqueeze(1).broadcast_to([P, 8, 2, HALF])
                    sb_ = sind[:, t, :].rearrange("p (j c) -> p j c", j=2).unsqueeze(1).broadcast_to([P, 8, 2, HALF])
                    pool.tensor_tensor(dst, src, cb, ALU.mult).then_inc(rope_own2, 1)
                    pool.tensor_tensor(tmp, src[:, :, ::-1, :], sb_, ALU.mult).then_inc(rope_own2, 1)
                    pool.wait_ge(rope_own2, 2 * (u - n_rot + 1))
                    pool.tensor_tensor(dst, dst, tmp, ALU.add).then_inc(rot_rdy, 1)
            for t in range(NT):
                rsqrt(t + 1, (ms, sq_rdy), rms, rms_rdy)
                rsqrt(NT + t + 1, (vareps[:, 0, :], var_rdy), rs[:, 0, :], rstd_rdy)

            pool.wait_ge(h1_rdy, NT)
            n_rc = [0]

            def const(ins):
                ins.then_inc(rc, 1)
                n_rc[0] += 1

            const(pool.iota(iota_s, [[1, P]], base=0, channel_multiplier=0, allow_small_or_imprecise_dtypes=True))
            const(pool.iota(slotm[:, :, 0], [[P, NT]], base=0, channel_multiplier=1, allow_small_or_imprecise_dtypes=True))
            const(pool.iota(thr, [[P, 7]], base=P, channel_multiplier=0, allow_small_or_imprecise_dtypes=True))
            const(pool.iota(itg, [[P, 2]], base=0, channel_multiplier=1, allow_small_or_imprecise_dtypes=True))
            const(pool.iota(tokpair[:, :, 0], [[P, NT]], base=0, channel_multiplier=0, allow_small_or_imprecise_dtypes=True))
            const(pool.iota(tokpair[:, :, 1], [[0, NT]], base=0, channel_multiplier=1, allow_small_or_imprecise_dtypes=True))
            const(pool.iota(parity, [[0, P], [1, 2]], base=0, channel_multiplier=0))
            const(pool.memset(zer, 0.0))
            const(pool.memset(ones_b, 1.0))
            const(pool.memset(upper_b, 1.0))
            const(pool.memset(tri, 1.0))
            pool.wait_ge(rc, n_rc[0])
            const(pool.affine_select(out=upper_b, in_=upper_b, compare_op=ALU.is_gt, fill=0.0, base=0,
                                     pattern=[[1, P]], channel_multiplier=-1))
            const(pool.affine_select(out=tri, in_=tri, compare_op=ALU.is_gt, fill=0.0, base=0,
                                     pattern=[[1, NG], [-1, NG]], channel_multiplier=0))
            assert n_rc[0] == N_RC

            def gather(i):
                pool.indirect_dma_start(out=xg[i], out_offset=None, in_=h1_d,
                                        in_offset=bass.IndirectOffsetOnAxis(ap=idx[:, i:i + 1], axis=0)).then_inc(x_got[i], 16)

            def remainders(n, j):
                for c in range(2):
                    pool.wait_ge(uh_rdy, n * 6 + (3 * j + c + 1))
                    h = slice(CUT[c], CUT[c + 1])
                    pool.tensor_tensor(w_ul[j][:, h], w_ru[j][:, h], w_uh[j][:, h], ALU.subtract).then_inc(ul_rdy, 1)

            pool.wait_ge(h1_st, 16 * NT)
            remainders(0, 0)
            pool.wait_ge(idx_rdy, 1)
            gather(1)
            pool.wait_ge(idx_rdy, 2)
            pool.wait_ge(t_rdy, turned_at["xT", SHB - 1])
            gather(0)
            pool.wait_ge(idx_rdy, 3)
            pool.wait_ge(t_rdy, T_ALL + 2)
            gather(1)
            n_routed = pool.value_load(bend_i[0:1, NE:NE + 1], min_val=NE, max_val=MAXB - SHB)

            def rows_ahead(r):
                odd = pool.value_load(parity[0:1, bass.ds(r, 1)], min_val=0, max_val=1)
                pool.wait_ge(idx_rdy, r + 4)
                pool.wait_ge(t_rdy, r * 2 + (T_ALL + 4))
                pool.sem_inc(go, 1)
                with pool.If(odd < 1):
                    gather(0)
                with pool.Else():
                    gather(1)

            def first(n, j, r):
                if j == 0:
                    remainders(n, 1)
                elif not isinstance(n, int) or n < NE // 2 - 1:
                    remainders(n + 1, 0)
                rows_ahead(r)

            for_experts(pool, first, lambda n, j, r: rows_ahead(r))
            pool.wait_ge(y_st, n_routed * 16 + SHB * 16)
            odd = pool.value_load(parity[0:1, bass.ds(n_routed, 1)], min_val=0, max_val=1)
            with pool.If(odd < 1):
                pool.wait_ge(x_got[0], n_routed * 8 + 16)
                pool.wait_ge(x_got[1], n_routed * 8 + 32)
            with pool.Else():
                pool.wait_ge(x_got[0], n_routed * 8 + 24)
                pool.wait_ge(x_got[1], n_routed * 8 + 24)
            pool.sem_inc(go, 1)

            def gather_y(t, ks):
                for k in ks:
                    if t:
                        pool.wait_ge(y_used, 8 * (t - 1) + k + 1)
                    pool.indirect_dma_start(out=yk[k], out_offset=None, in_=y_d,
                                            in_offset=bass.IndirectOffsetOnAxis(ap=slot8i[:, t, k:k + 1], axis=0)
                                            ).then_inc(y_in[k], 16)

            def residual(t):
                pool.wait_ge(m_rdy, t + 1)
                pool.tensor_tensor(ot[t % 2], ot[t % 2], acc[t % 3], ALU.add).then_inc(o_rdy, 1)

            gather_y(0, range(TOPK))
            for t in range(NT):
                if t + 1 < NT:
                    gather_y(t + 1, range(4))
                if t >= 2:
                    residual(t - 2)
                rsqrt(2 * NT + t + 1, (vareps[:, 0, :], var_rdy), rs[:, 0, :], rstd_rdy)
                if t + 1 < NT:
                    gather_y(t + 1, range(4, TOPK))
            residual(NT - 2)
            residual(NT - 1)

        @block.scalar
        def _(act):
            tu = [0]

            def turn_out(dst):
                act.wait_ge(t_rdy, tu[0] + 1)
                n = dst.free_size()
                src = tp[tu[0] % 2][:, 0:n]
                if len(dst.shape) == 3:
                    src = src.rearrange("p (a b) -> p a b", a=dst.shape[1])
                act.activation(dst, src, ACT.Copy).then_inc(t_out, 1)
                tu[0] += 1

            def rows(t):
                for b in range(2):
                    turn_out(hT[:, 4 * b:4 * b + 4, t * P:(t + 1) * P])

            rows(0)
            act.wait_ge(ang_rdy, 1)
            act.activation(sind[:, :, HALF:HD], tr, ACT.Sin).then_inc(rope_rdy, 1)
            act.activation(cosd[:, :, 0:HALF], tc, ACT.Sin).then_inc(rope_rdy, 1)
            act.wait_ge(rope_rdy, 2)
            act.mul(sind[:, :, 0:HALF], sind[:, :, HALF:HD], -1.0).then_inc(rope_rdy, 1)
            act.copy(cosd[:, :, HALF:HD], cosd[:, :, 0:HALF]).then_inc(rope_rdy, 1)
            dstT = {"qi": qiT, "qa": qaT, "ka": kaT, "qb": qbT, "kb": kbT}

            def copy_out(g, t):
                name, c0, n = GROUPS[g]
                u = product_of(g, t)
                act.wait_ge(pj_rdy, u + 1)
                if name[0] == "v":
                    dst = (va if name == "va" else vb)[:, t, :]
                else:
                    r = rotated_of(g, t)
                    dst = raw[r % 2][:, 0:n]
                    if r >= 2:
                        act.wait_ge(rot_rdy, r - 1)
                if name == "va" and t == 0:
                    act.wait_ge(h_st, 16 * NT)
                act.activation(dst, pa[u % 2][:, 0:n], ACT.Copy).then_inc(pj_out, 1)

            def turned(g, t):
                name, ts = GROUPS[g][0], slice(t * P, (t + 1) * P)
                turn_out(kiT[:, ts] if name == "ki" else dstT[name][:, :, ts])

            def silu(g):
                act.wait_ge(up_done, g + 1)
                act.activation(sg, lg[0][:, 0:ED], ACT.Silu).then_inc(silu_rdy, 1)

            def round_up(n, j):
                act.wait_ge(ru_in[j], n * 32 + 32)
                for c in range(3):
                    h = slice(CUT[c], CUT[c + 1])
                    act.activation(w_uh[j][:, h], w_ru[j][:, h], ACT.Copy).then_inc(uh_rdy, 1)

            def round_rows(r):
                for b in range(2):
                    act.wait_ge(t_rdy, r * 2 + (T_ALL + 1 + b))
                    act.activation(xTh[:, 4 * b:4 * b + 4, :], tp[b].rearrange("p (a b) -> p a b", b=P), ACT.Copy).then_inc(xh_rdy, 1)

            def store(g):
                act.wait_ge(y_out, g + 1)
                rows = y_d[g * P:(g + 1) * P, :] if isinstance(g, int) else y_d[bass.ds(g * P, P), :]
                act.dma_start(rows, y_sb).then_inc(y_st, 16)

            for t in range(NT):
                if t + 1 < NT:
                    rows(t + 1)
                for g in range(2):
                    copy_out(g, t)
                    if t >= 1:
                        turned(g, t - 1)
            for g in range(2):
                turned(g, NT - 1)
            act.wait_ge(lam_in, 1)
            act.activation(lam2[:, 2:4], lam2[:, 0:2], ACT.Exp).then_inc(lam_out, 1)
            last = None
            for what, a, t in mixed:
                if what == "index":
                    n = P * (a + 1)
                    for u in range(8 * (a - 2), 8 * (a - 1)):
                        act.wait_ge(l_rdy, u + 1)
                        if u >= 2:
                            act.wait_ge(rel_used, u - 1)
                        act.activation(rel[u % 2][:, 0:n], lg[u % 2][:, 0:n], ACT.Relu).then_inc(l_act, 1)
                else:
                    copy_out(a, t)
                    if last:
                        turned(*last)
                    last = (a, t) if a in ROPED else None
            turned(*last)

            lu = N_IDX
            n_max = 0
            for what, i in order:
                if what == "task" and i < NTK:
                    t, k = TASKS[i]
                    n = P * (t + 1)
                    for j, q in enumerate(prob_at[i]):
                        n_max += 1
                        act.wait_ge(mx_rdy, n_max)
                        c = k if k < AH else AH + 2 * (k - AH) + j
                        if k < AH:
                            act.activation(prob[q][:, 0:n], prob[q][:, 0:n], ACT.Exp, bias=nmx[:, c:c + 1], scale=SCALE,
                                           accum_out=ssum[t % 2][:, c:c + 1]).then_inc(e_rdy, 1)
                        else:
                            if j == 0 and prob_prev[i] >= 0:
                                act.wait_ge(t_rdy, turned_at["task", prob_prev[i]])
                            act.activation(prob[q][:, 0:n], lg[lu % 2][:, 0:n], ACT.Exp, bias=nmx[:, c:c + 1], scale=SCALE,
                                           accum_out=ssum[t % 2][:, c:c + 1]).then_inc(e_rdy, 1)
                        lu += 1
                if what == "task" and 1 <= i <= NTK:
                    t, k = TASKS[i - 1]
                    if i - 1 >= 2:
                        act.wait_ge(pv_done, i - 2)
                    for b in range(banks(t)):
                        turn_out(pT[(i - 1) % 2][:, 4 * b:min(4 * b + 4, t + 1), :])
                if what == "mix":
                    turn_out(mixT[:, 0:4, :])
                    turn_out(mixT[:, 4:8, :])
                    lu += 1
                if what == "rows":
                    turn_out(mixT[:, 0:4, :])
                    turn_out(mixT[:, 4:8, :])
                    turn_out(rl[:, i, :])
                    if i == NT - 1:
                        act.wait_ge(t_out, turned_at["rows", i])
                        act.activation(sig, rl, ACT.Sigmoid).then_inc(sig_rdy, 1)
                if what == "shared":
                    silu(i)
                if what == "shared" and i == SHB - 2:
                    act.wait_ge(h1_st, 16 * NT)
                    round_up(0, 0)
                if what == "shared" and i == SHB - 1:
                    round_rows(0)
                elif what == "turn" or what == "shared":
                    turn_out(xT[:, 0:4, :])
                    turn_out(xT[:, 4:8, :])
                if what == "shared" and 0 < i < SHB - 1:
                    store(i - 1)


            n_routed = act.value_load(bend_i[0:1, NE:NE + 1], min_val=NE, max_val=MAXB - SHB)

            def y_read(g):
                act.wait_ge(down_done, g + 1)
                act.wait_ge(y_st, g * 16)
                act.activation(y_sb, lg[1][:, :], ACT.Copy).then_inc(y_out, 1)
                store(g)

            def routed(r):
                silu(r + SHB)
                round_rows(r + 1)

            def first(n, j, r):
                act.wait_ge(up_done, r + SHB)
                if j == 0:
                    round_up(n, 1)
                elif not isinstance(n, int) or n < NE // 2 - 1:
                    round_up(n + 1, 0)
                act.wait_ge(rd_in[j], n * 16 + 16)
                act.wait_ge(down_done, r + (SHB - 1))
                if not (isinstance(n, int) and n == 0 and j == 0):
                    y_read(r + (SHB - 2))
                act.activation(w_dh[j], w_rd[j], ACT.Copy).then_inc(dh_rdy, 1)
                routed(r)

            def more(n, j, r):
                y_read(r + (SHB - 2))
                routed(r)

            store(SHB - 2)
            for_experts(act, first, more)
            y_read(n_routed + (SHB - 2))
            y_read(n_routed + (SHB - 1))

            tu[0] = 0
            base = n_routed * 2 + (T_ALL + 2)

            def turn_out2(dst):
                act.wait_ge(t_rdy, base + tu[0] + 1)
                n = dst.free_size()
                act.activation(dst, tp[tu[0] % 2][:, 0:n].rearrange("p (a b) -> p a b", b=P), ACT.Copy).then_inc(t_out, 1)
                tu[0] += 1

            def gate_of(t):
                act.wait_ge(z_rdy, t + 1)
                act.activation(zt, zt, ACT.Sigmoid).then_inc(s_rdy, 1)

            for t in range(NT):
                if t:
                    act.wait_ge(p_mm, t)
                turn_out2(ppT)
                turn_out2(h2T[:, 0:4, :])
                turn_out2(h2T[:, 4:8, :])
                if t:
                    gate_of(t - 1)
            gate_of(NT - 1)

        @block.tensor
        def _(pe):
            tu = [0]

            def turn(srcs, idn):
                if tu[0] >= 2:
                    pe.wait_ge(t_out, tu[0] - 1)
                for j, s_ in enumerate(srcs):
                    m = pe.transpose(tp[tu[0] % 2][0:s_.shape[1], j * P:j * P + P], s_, idn)
                m.then_inc(t_rdy, 1)
                tu[0] += 1

            pe.wait_ge(consts, 6)

            def turn_h(t):
                pe.wait_ge(ln_rdy, t + 1)
                for b in range(2):
                    turn([h0[:, t, (4 * b + j) * P:(4 * b + j + 1) * P] for j in range(4)], ident)

            def turn_rot(g, t):
                r = rotated_of(g, t)
                pe.wait_ge(rot_rdy, r + 1)
                turn([rot[r % 2][:, j * P:(j + 1) * P] for j in range(1 if GROUPS[g][0] == "ki" else 4)], ident)

            def project(g, t):
                _, _, n = GROUPS[g]
                u = product_of(g, t)
                if t == 0:
                    pe.wait_ge(w_in_s[g % 2], 16 * (g // 2 + 1))
                if u >= 2:
                    pe.wait_ge(pj_out, u - 1)
                for k in range(KC):
                    m = pe.matmul(pa[u % 2][:, 0:n], hT[:, k, t * P:(t + 1) * P], w_sl[g % 2][:, k, 0:n],
                                  start=(k == 0), stop=(k == KC - 1))
                m.then_inc(pj_rdy, 1)

            turn_h(0)
            for t in range(NT):
                if t + 1 < NT:
                    turn_h(t + 1)
                pe.wait_ge(t_out, rows_turned(t))
                for g in range(2):
                    project(g, t)
                    if t >= 1:
                        turn_rot(g, t - 1)
            for g in range(2):
                turn_rot(g, NT - 1)

            lu = [0]

            def next_l():
                u = lu[0]
                lu[0] += 1
                if u >= 2:
                    who, c = l_uses[u - 2]
                    pe.wait_ge({"act": l_act, "dve": l_dve, "exp": e_rdy}[who], c)
                return lg[u % 2]

            pe.wait_ge(t_out, T_LN + 2 * NT)
            last = None
            for what, a, t in mixed:
                if what == "index":
                    for h in range(8):
                        o, n = next_l(), P * (a + 1)
                        r = slice(HD * (h % 2), HD * (h % 2) + HD)
                        for c in range(0, n, 512):
                            e = min(c + 512, n)
                            m = pe.matmul(o[:, c:e], qiT[r, h // 2, a * P:(a + 1) * P], kiT[r, c:e], start=True, stop=True)
                        m.then_inc(l_rdy, 1)
                else:
                    project(a, t)
                    if last:
                        turn_rot(*last)
                    last = (a, t) if a in ROPED else None
            turn_rot(*last)
            pe.wait_ge(t_out, T_LN + T_PROJ)

            def logits(i):
                t, k = TASKS[i]
                n = P * (t + 1)
                ts = slice(t * P, (t + 1) * P)
                for j in range(1 if k < AH else 2):
                    o = next_l()
                    if k < AH:
                        r, c, qT, kT = slice(HD * (k % 2), HD * (k % 2) + HD), k // 2, qaT, kaT
                    else:
                        r, c, qT, kT = slice(HD * j, HD * j + HD), k - AH, qbT, kbT
                    full = n if k < AH else n - CH
                    for a in range(0, full, 512):
                        e = min(a + 512, full)
                        m = pe.matmul(o[:, a:e], qT[r, c, ts], kT[r, c, a:e], start=True, stop=True)
                    if k >= AH:
                        pe.matmul(o[:, full:n], qT[r, c, ts], kT[r, c, full:n], start=True, stop=False)
                        m = pe.matmul(o[:, full:n], colq[0:1, :], rowneg[0:1, :], start=False, stop=True)
                    m.then_inc(l_rdy, 1)

            def values(i):
                t, k = TASKS[i]
                pe.wait_ge(t_out, turned_at["task", i])
                if k == 0 and t > 0:
                    pe.wait_ge(sums_read, t)
                for b in range(t + 1):
                    if k < AH:
                        o, v = pa[0][:, k * HD:(k + 1) * HD], va[:, b, k * HD:(k + 1) * HD]
                    else:
                        o, v = pa[1][:, (k - AH) * P:(k - AH + 1) * P], vb[:, b, (k - AH) * P:(k - AH + 1) * P]
                    m = pe.matmul(o, pT[i % 2][:, b, :], v, start=(b == 0), stop=(b == t))
                m.then_inc(pv_done, 1)

            def turn_prob(i):
                t, k = TASKS[i]
                if k < AH:
                    pe.wait_ge(e_rdy, count_exp(i) + 1)
                else:
                    pe.wait_ge(cmb_rdy, BH * t + k - AH + 1)
                q = prob[prob_at[i][0]]
                for b in range(banks(t)):
                    turn([q[:, c * P:(c + 1) * P] for c in range(4 * b, min(4 * b + 4, t + 1))], ident)

            def up(w):
                for k in range(KC):
                    m = pe.matmul(lg[0][:, 0:2 * ED].rearrange("p (j f) -> p j f", j=2), xT[:, k, :], w[:, :, k, :],
                                  start=(k == 0), stop=(k == KC - 1))
                m.then_inc(up_done, 1)

            def down(g, w):
                pe.wait_ge(hT_rdy, g + 1)
                if not isinstance(g, int) or g > 0:
                    pe.wait_ge(y_out, g)
                for c in range(2):
                    for j in range(2):
                        m = pe.matmul(lg[1][:, c * 512:(c + 1) * 512], hidT[:, j, :], w[:, j, c * 512:(c + 1) * 512],
                                      start=(j == 0), stop=(j == 1))
                m.then_inc(down_done, 1)

            def turn_hidden(g):
                pe.wait_ge(hid_rdy, g + 1)
                for j in range(2):
                    m = pe.transpose(pa[1][:, j * P:(j + 1) * P], hid_v[:, j, :], ident)
                m.then_inc(hT_trn, 1)

            def shared_turn(b):
                pe.wait_ge(xs_got, 16 * (b + 1))
                for c in range(2):
                    turn([xg_v[0][:, 4 * c + j, :] for j in range(4)], ident)

            def turn_rows(i, gathered):
                pe.wait_ge(x_got[i], gathered)
                for b in range(2):
                    for k in range(4):
                        m = pe.transpose(tp[b][:, k * P:(k + 1) * P], xg_v[i][:, 4 * b + k, :], ident)
                    m.then_inc(t_rdy, 1)

            def tokens(n):
                pe.wait_ge(oh_rdy, n)
                for t in range(NT):
                    m = pe.matmul(pa[0][:, 0:2], onehot[:, t, :], tokpair[:, t, :], start=(t == 0), stop=(t == NT - 1))
                m.then_inc(tok_rdy, 1)

            def places():
                pe.wait_ge(sel_rdy, 1)
                pe.wait_ge(rc, N_RC)
                for t in range(NT):
                    for s_ in range(t + 1):
                        pe.matmul(lg[0][:, 512 + t * NE:512 + (t + 1) * NE], (upper_b if s_ == t else ones_b), sel_b[:, s_, :],
                                  start=(s_ == 0), stop=(s_ == t))
                for t in range(NT):
                    m = pe.matmul(pa[0][:, NE:2 * NE], ones_b, sel_b[:, t, :], start=(t == 0), stop=(t == NT - 1))
                m.then_inc(pos_rdy, 1)

            def block_experts():
                pe.wait_ge(eob_rdy, 1)
                for c in range(2):
                    m = pe.transpose(pa[1][0:1, 256 + c * P:256 + (c + 1) * P], eobc[:, c:c + 1], ident)
                m.then_inc(eob_row, 1)

            assert T_ALL % 2 == 0
            for what, i in order:
                if what == "task":
                    if i < NTK:
                        logits(i)
                    if 2 <= i:
                        values(i - 2)
                    if 1 <= i <= NTK:
                        turn_prob(i - 1)
                if what == "mix":
                    pe.wait_ge(mix_rdy, i + 1)
                    for b in range(2):
                        turn([mix[:, (4 * b + j) * P:(4 * b + j + 1) * P] for j in range(4)], ident)
                    pe.wait_ge(t_out, turned_at["mix", i])
                    if i == 0:
                        pe.wait_ge(wo_in, 16)
                    o = next_l()
                    for c in range(2):
                        for k in range(KC):
                            m = pe.matmul(o[:, c * 512:(c + 1) * 512], mixT[:, k, :], wo[:, k, c * 512:(c + 1) * 512],
                                          start=(k == 0), stop=(k == KC - 1))
                    m.then_inc(l_rdy, 1)
                if what == "rows":
                    pe.wait_ge(h1_rdy, i + 1)
                    for b in range(2):
                        turn([h1[:, (4 * b + j) * P:(4 * b + j + 1) * P] for j in range(4)], ident)
                    pe.wait_ge(t_out, turned_at["rows", i] - 1)
                    if i == 0:
                        pe.wait_ge(rows_in, 48)
                    for k in range(KC):
                        m = pe.matmul(tp[tu[0] % 2][:, 0:NE], mixT[:, k, :], wr[:, k, :], start=(k == 0), stop=(k == KC - 1))
                    m.then_inc(t_rdy, 1)
                    tu[0] += 1
                if what == "turn":
                    shared_turn(0)
                if what == "shared":
                    if i == 0:
                        pe.wait_ge(sh_in, 48)
                        pe.wait_ge(l_dve, n_free["dve"] - 1)
                    pe.wait_ge(t_out, turned_at["xT", i])
                    up(sh_up_v)
                    if i == 4:
                        places()
                    if i == 5:
                        block_experts()
                    if i >= 6:
                        tokens(i - 5)
                    if i < SHB - 1:
                        shared_turn(i + 1)
                    else:
                        turn_rows(1, 16)
                    if i == 1:
                        pe.wait_ge(l_dve, n_free["dve"])
                    if i:
                        down(i - 1, sh_dn_v)
                    turn_hidden(i)
            tokens(3)

            n_routed = pe.value_load(bend_i[0:1, NE:NE + 1], min_val=NE, max_val=MAXB - SHB)


            def up_split(n, j, r):
                pe.wait_ge(ul_rdy, n * 4 + (2 * j + 2))
                pe.wait_ge(ud_rdy, n * 2 + (j + 1))
                pe.wait_ge(xh_rdy, r * 2 + 2)
                xs = [(xTh, w_uh, k) for k in range(KC)] + [(xTh, w_ul, k) for k in range(KC)] + [(xTl, w_uh, k) for k in range(KC)]
                for c, (x_, w, k) in enumerate(xs):
                    if c == 2 * KC:
                        pe.wait_ge(t_out, r * 2 + (T_ALL + 2))
                    m = pe.matmul(lg[0][:, 0:2 * ED].rearrange("p (j f) -> p j f", j=2), x_[:, k, :], up_v(w[j])[:, :, k, :],
                                  start=(c == 0), stop=(c == 3 * KC - 1))
                m.then_inc(up_done, 1)

            def down_split(g, place):
                pe.wait_ge(hT_rdy, g + 1)
                pe.wait_ge(y_out, g)
                for c in range(2):
                    for i, (h_, w, j) in enumerate((h_, w, j) for h_, w in ((hidTh, w_dh), (hidTh, w_dl), (hidTl, w_dh))
                                                   for j in range(2)):
                        m = pe.matmul(lg[1][:, c * 512:(c + 1) * 512], h_[:, j, :], dn_v(w[place])[:, j, c * 512:(c + 1) * 512],
                                      start=(i == 0), stop=(i == 5))
                m.then_inc(down_done, 1)

            def between(r):
                odd = pe.value_load(parity[0:1, bass.ds(r, 1)], min_val=0, max_val=1)
                tokens(r + 4)
                with pe.If(odd < 1):
                    turn_rows(0, r * 8 + 16)
                with pe.Else():
                    turn_rows(1, r * 8 + 24)

            def first(n, j, r):
                up_split(n, j, r)
                between(r)
                if isinstance(n, int) and n == 0 and j == 0:
                    down(SHB - 1, sh_dn_v)
                else:
                    pe.wait_ge(dl_rdy, n * 2 + j)
                    down_split(r + (SHB - 1), 1 - j)
                turn_hidden(r + SHB)

            def more(n, j, r):
                up_split(n, j, r)
                between(r)
                pe.wait_ge(dl_rdy, n * 2 + (j + 1))
                down_split(r + (SHB - 1), j)
                turn_hidden(r + SHB)

            for_experts(pe, first, more)
            pe.wait_ge(dl_rdy, NE)
            down_split(n_routed + (SHB - 1), (NE - 1) % 2)

            tu[0] = 0
            base = n_routed * 2 + (T_ALL + 2)

            def turn2(srcs):
                pe.wait_ge(t_out, base + max(tu[0] - 1, 0))
                for j, s_ in enumerate(srcs):
                    m = pe.transpose(tp[tu[0] % 2][:, j * P:(j + 1) * P], s_, ident)
                m.then_inc(t_rdy, 1)
                tu[0] += 1

            pe.wait_ge(ple_in, 16 * 5)
            pe.wait_ge(y_out, n_routed + SHB)
            for t in range(NT):
                pe.wait_ge(row_in[t % 3], 48 * (t // 3 + 1))
                turn2([pt_sb[t % 3][:, j * P:(j + 1) * P] for j in range(2)])
                pe.wait_ge(h2_rdy, t + 1)
                for b in range(2):
                    turn2([acc[t % 3][:, (4 * b + j) * P:(4 * b + j + 1) * P] for j in range(4)])
                if t >= 2:
                    pe.wait_ge(z_rdy, t - 1)
                pe.wait_ge(t_out, base + tu[0])
                for c in range(2):
                    for k in range(KC):
                        m = pe.matmul(lg[t % 2][:, c * 512:(c + 1) * 512], h2T[:, k, :], wpg[:, k, c * 512:(c + 1) * 512],
                                      start=(k == 0), stop=(k == KC - 1))
                m.then_inc(g_mm, 1)
                if t:
                    pe.wait_ge(m_rdy, t)
                for c in range(2):
                    for k in range(2):
                        m = pe.matmul(pa[c][:, :], ppT[:, k, :], wpp[:, k, c * 512:(c + 1) * 512],
                                      start=(k == 0), stop=(k == 1))
                m.then_inc(p_mm, 1)

        @block.vector
        def _(dve):
            n_step = [0]

            def link(ins):
                ins.then_inc(step, 1)
                n_step[0] += 1
                dve.wait_ge(step, n_step[0])

            n_var = [0]

            def norm_stats(src, slot):
                dve.bn_stats(stats[:, 0, :], src[:, 0:512]).then_inc(step, 1)
                n_step[0] += 1
                link(dve.bn_stats(stats[:, 1, :], src[:, 512:1024]))
                link(dve.bn_aggr(mv, stats))
                dve.tensor_scalar(vareps[:, slot, :], mv[:, 1:2], EPS, None, ALU.add).then_inc(var_rdy, 1)
                n_var[0] += 1

            def norm_scale(src, dst, g, slot):
                dve.wait_ge(rstd_rdy, n_var[0])
                link(dve.tensor_scalar(dst, src, mv[:, 0:1], rs[:, slot, :], ALU.subtract, ALU.mult))
                link(dve.tensor_tensor(dst, dst, g, ALU.mult))

            def layer_norm(src, dst, g, b, slot, done):
                norm_stats(src, slot)
                norm_scale(src, dst, g, slot)
                dve.tensor_tensor(dst, dst, b, ALU.add).then_inc(done, 1)

            def embed(t):
                dve.wait_ge(x_in[t], 16)
                layer_norm(h0[:, t, :], h0[:, t, :], g_emb, b_emb, t % 2, ln_rdy)

            dve.wait_ge(emb_in, 32)
            embed(0)
            embed(1)
            dve.wait_ge(const_in, 16 * 7)
            link(dve.tensor_copy(posf, posi))
            link(dve.tensor_tensor(ang, posf.unsqueeze(2).broadcast_to([P, NT, HALF]),
                                   inv.unsqueeze(1).broadcast_to([P, NT, HALF]), ALU.mult))
            MAGIC = 1.5 * 2.0 ** 23
            TWO_PI = 6.283185307179586
            parts = [6.28125, 0.00193500518798828125, 3.0199159819567e-07]
            link(dve.tensor_scalar(tn, ang, 1.0 / TWO_PI, MAGIC, ALU.mult, ALU.add))
            link(dve.tensor_scalar(tn, tn, -MAGIC, None, ALU.add))
            src = ang
            for c in parts:
                link(dve.scalar_tensor_tensor(tr, tn, -c, src, ALU.mult, ALU.add))
                src = tr
            link(dve.tensor_scalar(tc, tr, TWO_PI / 4, None, ALU.add))
            link(dve.tensor_scalar(tw, tc, TWO_PI / 2, -TWO_PI, ALU.is_gt, ALU.mult))
            link(dve.tensor_tensor(tc, tc, tw, ALU.add))
            PI_IN = 3.1415925
            link(dve.tensor_scalar(tr, tr, PI_IN, -PI_IN, ALU.min, ALU.max))
            dve.tensor_scalar(tc, tc, PI_IN, -PI_IN, ALU.min, ALU.max).then_inc(ang_rdy, 1)
            def lambdas():
                link(dve.tensor_tensor(lam4[:, 0, :], lam4[:, 0, :], lam4[:, 1, :], ALU.mult))
                link(dve.tensor_tensor(lam4[:, 1, :], lam4[:, 2, :], lam4[:, 3, :], ALU.mult))
                dve.tensor_reduce(lam2[:, 0:2], lam4[:, 0:2, :], AX.X, ALU.add).then_inc(lam_in, 1)
                dve.wait_ge(lam_out, 1)
                link(dve.tensor_tensor(neglam, lam2[:, 3:4], lam2[:, 2:3], ALU.subtract))
                link(dve.tensor_scalar(neglam, neglam, -LAMBDA_INIT, None, ALU.add))
                link(dve.tensor_scalar(subg, subg, 1.0 - LAMBDA_INIT, None, ALU.mult))

            n_own = 0
            for t in range(NT):
                if t + 2 < NT:
                    embed(t + 2)
                if t == 0:
                    dve.wait_ge(rope_rdy, 4)
                for g in range(2):
                    r = rotated_of(g, t)
                    nh = 8 if g == 0 else 1
                    src = raw[r % 2][:, 0:nh * HD].rearrange("p (h j c) -> p h j c", j=2, c=HALF)
                    dst = rot[r % 2][:, 0:nh * HD].rearrange("p (h j c) -> p h j c", j=2, c=HALF)
                    tmp = rot2[:, 0:nh * HD].rearrange("p (h j c) -> p h j c", j=2, c=HALF)
                    dve.wait_ge(pj_out, product_of(g, t) + 1)
                    if r >= 2:
                        dve.wait_ge(t_rdy, rot_turned(r - 2))
                    if r >= 1:
                        dve.wait_ge(rot_rdy, r)
                    cb = cosd[:, t, :].rearrange("p (j c) -> p j c", j=2).unsqueeze(1).broadcast_to([P, nh, 2, HALF])
                    sb_ = sind[:, t, :].rearrange("p (j c) -> p j c", j=2).unsqueeze(1).broadcast_to([P, nh, 2, HALF])
                    dve.tensor_tensor(dst, src, cb, ALU.mult).then_inc(rope_own, 1)
                    dve.tensor_tensor(tmp, src[:, :, ::-1, :], sb_, ALU.mult).then_inc(rope_own, 1)
                    n_own += 2
                    dve.wait_ge(rope_own, n_own)
                    if g == 0:
                        dve.tensor_tensor(dst, dst, tmp, ALU.add).then_inc(rot_rdy, 1)
                    else:
                        dve.tensor_scalar(iws[:, t, :], raw[r % 2][:, HD:HD + 8], WSCALE, None, ALU.mult).then_inc(iw_rdy, 1)
                        link(dve.tensor_tensor(dst, dst, tmp, ALU.add))
                        dve.tensor_copy(rot[r % 2][:, HD:2 * HD], rot[r % 2][:, 0:HD]).then_inc(rot_rdy, 1)
            lambdas()
            dve.wait_ge(iw_rdy, NT)
            for t in range(NT):
                n = P * (t + 1)
                if t < 2:
                    link(dve.memset(score[t], 0.0))
                    link(dve.memset(score[t][0:CH, n - CH:n], MASK))
                    continue
                for h in range(8):
                    u = 8 * (t - 2) + h
                    dve.wait_ge(l_act, u + 1)
                    if u:
                        dve.wait_ge(rel_used, u)
                    if h == 0:
                        dve.tensor_scalar(score[t], rel[u % 2][:, 0:n], iws[:, t, h:h + 1], None, ALU.mult).then_inc(rel_used, 1)
                    else:
                        dve.scalar_tensor_tensor(score[t], rel[u % 2][:, 0:n], iws[:, t, h:h + 1], score[t], ALU.mult,
                                                 ALU.add).then_inc(rel_used, 1)
                dve.wait_ge(rel_used, 8 * (t - 1))
                link(dve.memset(score[t][0:CH, n - CH:n], FILL))
                for _ in range(NKEEP // 8):
                    link(dve.max(m8, score[t]))
                    link(dve.match_replace(score[t], m8, score[t], TAKEN))
                link(dve.tensor_scalar(score[t], score[t], 0.5 * (FILL + TAKEN), MASK, ALU.is_gt, ALU.mult))

            def bc(v, dims, *axes):
                for ax in axes:
                    v = v.unsqueeze(ax)
                return v.broadcast_to([P, *dims])

            chosen = tmp1.rearrange("p (t e) -> p t e", t=NT)

            def rank_groups():
                dve.wait_ge(sig_rdy, 1)
                dve.wait_ge(rb_in, 16)
                dve.wait_ge(rc, N_RC)
                link(dve.tensor_tensor(biased, sig, bc(rbias, (NT, NE), 1), ALU.add))
                b_g = biased.rearrange("p t (g e) -> p (t g) e", g=NG)
                for i in range(NT * NG):
                    m = dve.max(g8[:, i, :], b_g[:, i, :])
                link(m)
                gs_f = gs.rearrange("p t g -> p (t g)")
                link(dve.tensor_tensor(gs_f, g8[:, :, 0], g8[:, :, 1], ALU.add))
                shape4 = dict(t=NT, g=NG)
                t1, t2 = (v.rearrange("p (t g e) -> p t g e", **shape4) for v in (tmp1, tmp2))
                other, own = bc(gs, (NT, NG, NG), 2), bc(gs, (NT, NG, NG), 3)
                link(dve.tensor_tensor(t1, other, own, ALU.is_gt))
                link(dve.tensor_tensor(t2, other, own, ALU.is_equal))
                link(dve.tensor_tensor(t2, t2, bc(tri, (NT, NG, NG), 1), ALU.mult))
                link(dve.tensor_tensor(t1, t1, t2, ALU.add))
                link(dve.tensor_reduce(gpen, t1, AX.X, ALU.add))
                link(dve.tensor_scalar(gpen, gpen, float(TOPG), -MASK, ALU.is_lt, ALU.mult))
                link(dve.tensor_scalar(gpen, gpen, MASK, None, ALU.add))
                b4 = biased.rearrange("p t (g e) -> p t g e", g=NG)
                link(dve.tensor_tensor(b4, b4, bc(gpen, (NT, NG, NG), 3), ALU.add))

            def choose_experts():
                for t in range(NT):
                    m = dve.max(g8[:, t, :], biased[:, t, :])
                link(m)
                for t in range(NT):
                    m = dve.match_replace(biased[:, t, :], g8[:, t, :], biased[:, t, :], FILL)
                link(m)
                link(dve.tensor_scalar(chosen, biased, 0.1 * FILL, None, ALU.is_lt))
                dve.tensor_copy(sel_b, chosen).then_inc(sel_rdy, 1)

            def weigh():
                link(dve.tensor_tensor(gate, sig, chosen, ALU.mult))
                link(dve.tensor_reduce(den8, gate, AX.X, ALU.add))
                link(dve.reciprocal(den8, den8))
                link(dve.tensor_scalar(den8, den8, ROUTED, None, ALU.mult))
                link(dve.tensor_tensor(gate, gate, bc(den8, (NT, NE), 2), ALU.mult))

            def count_blocks():
                dve.wait_ge(pos_rdy, 1)
                over = tmp2[:, 0:NE * 7].rearrange("p (e k) -> p e k", k=7)
                link(dve.tensor_tensor(over, bc(pa[0][:, NE:2 * NE], (NE, 7), 2), bc(thr, (NE, 7), 1), ALU.is_gt))
                link(dve.tensor_reduce(nblk, over, AX.X, ALU.add))
                link(dve.tensor_scalar(nblk, nblk, 1.0, None, ALU.add))
                link(dve.memset(bend[:, 0:1], float(SHB)))
                link(dve.tensor_tensor_scan(bend[:, 1:NE + 1], nblk, zer, float(SHB), ALU.add, ALU.add))
                ends = tmp3[:, 0:2 * (NE + 1)].rearrange("p (c e) -> p c e", c=2)
                link(dve.tensor_tensor(ends, bc(bend, (2, NE + 1), 1), bc(itg, (2, NE + 1), 2), ALU.is_le))
                link(dve.tensor_reduce(eobc, ends, AX.X, ALU.add))
                dve.tensor_scalar(eobc, eobc, float(NE), None, ALU.min).then_inc(eob_rdy, 1)

            def place_tokens():
                link(dve.tensor_tensor(nblk, bend[:, 1:NE + 1], nblk, ALU.subtract))
                link(dve.tensor_scalar(nblk, nblk, float(P), 1.0, ALU.mult, ALU.add))
                pos = tmp2.rearrange("p (t e) -> p t e", t=NT)
                link(dve.tensor_tensor(pos, lg[0][:, 512:1024].rearrange("p (t e) -> p t e", t=NT), bc(nblk, (NT, NE), 1), ALU.add))
                link(dve.tensor_tensor(pos, pos, chosen, ALU.mult))
                link(dve.tensor_scalar(slotm[:, :, 1:NE + 1], pos, -1.0, None, ALU.add))

            def write_tables():
                dve.wait_ge(eob_row, 1)
                dve.tensor_scalar(bend_i[0:1, :], bend[0:1, :], -float(SHB), None, ALU.add).then_inc(tab_rdy, 1)
                dve.tensor_copy(tab[0:1, :], pa[1][0:1, 256:256 + 2 * P]).then_inc(tab_rdy, 1)
                dve.wait_ge(tab_rdy, 2)

            def slots_of_tokens():
                for t in range(NT):
                    m = dve.max(slot8[:, t, :], slotm[:, t, 1:NE + 1])
                link(m)
                link(dve.tensor_copy(slot8i, slot8))

            def gates_by_slot():
                hit = tmp1.rearrange("p (k e) -> p k e", k=TOPK)
                for t in range(NT):
                    link(dve.tensor_tensor(hit, bc(slotm[:, t, 1:NE + 1], (TOPK, NE), 1), bc(slot8[:, t, :], (TOPK, NE), 2), ALU.is_equal))
                    link(dve.tensor_tensor(hit, hit, bc(gate[:, t, :], (TOPK, NE), 1), ALU.mult))
                    m = dve.tensor_reduce(gate8[:, t, :], hit, AX.X, ALU.add)
                    link(m)

            def one_hot(n, e):
                if isinstance(n, int) and n == 1:
                    dve.memset(gbase, float(SHB * P)).then_inc(gb_own, 1)
                else:
                    dve.wait_ge(tok_rdy, n - 1)
                dve.wait_ge(gb_own, n)
                column = slotm[:, :, bass.ds(e, 1)].broadcast_to([P, NT, P])
                dve.scalar_tensor_tensor(onehot, column, gbase, bc(iota_s, (NT, P), 1), ALU.subtract,
                                         ALU.is_equal).then_inc(oh_rdy, 1)
                dve.wait_ge(oh_rdy, n)
                dve.tensor_scalar(gbase, gbase, float(P), None, ALU.add).then_inc(gb_own, 1)

            def indices(n, i):
                dve.wait_ge(tok_rdy, n)
                dve.tensor_scalar(idx[:, i], pa[0][:, 0:1], pa[0][:, 1:2], None, ALU.add).then_inc(idx_rdy, 1)

            def hidden(g):
                dve.wait_ge(silu_rdy, g + 1)
                dve.tensor_tensor(hid, sg, lg[0][:, ED:2 * ED], ALU.mult).then_inc(hid_rdy, 1)

            def y_read(g):
                dve.wait_ge(down_done, g + 1)
                if not isinstance(g, int) or g > 0:
                    dve.wait_ge(y_st, g * 16)
                dve.tensor_copy(y_sb, lg[1][:, :]).then_inc(y_out, 1)

            def hidden_t(g):
                dve.wait_ge(hT_trn, g + 1)
                dve.tensor_copy(hidT, pa[1][:, 0:2 * P].rearrange("p (j q) -> p j q", j=2)).then_inc(hT_rdy, 1)

            def row_remainders(r):
                for b in range(2):
                    dve.wait_ge(xh_rdy, r * 2 + (b + 1))
                    dve.tensor_tensor(xTl[:, 4 * b:4 * b + 4, :], tp[b].rearrange("p (a b) -> p a b", b=P),
                                      xTh[:, 4 * b:4 * b + 4, :], ALU.subtract).then_inc(t_out, 1)

            def last_remainders(n, j):
                dve.wait_ge(uh_rdy, n * 6 + (3 * j + 3))
                dve.tensor_tensor(w_ul[j][:, CUT[2]:], w_ru[j][:, CUT[2]:], w_uh[j][:, CUT[2]:], ALU.subtract).then_inc(ud_rdy, 1)

            def shared(b):
                if b == 6:
                    indices(1, slice(1, 2))
                if b == 7:
                    indices(2, slice(0, 1))
                hidden(b)
                if b:
                    y_read(b - 1)
                hidden_t(b)
                if b == 2:
                    rank_groups()
                if b == 3:
                    choose_experts()
                    weigh()
                if b == 4:
                    count_blocks()
                    place_tokens()
                if b == 5:
                    write_tables()
                    one_hot(1, 1)
                    slots_of_tokens()
                if b == 6:
                    one_hot(2, dve.value_load(tab[0:1, SHB + 1:SHB + 2], min_val=0, max_val=NE))
                if b == 7:
                    one_hot(3, dve.value_load(tab[0:1, SHB + 2:SHB + 3], min_val=0, max_val=NE))
                    row_remainders(0)
                    last_remainders(0, 0)
                    indices(3, slice(1, 2))

            def sums_out(i, t):
                s = ssum[t % 2]
                dve.wait_ge(pv_done, i - 1)
                dve.wait_ge(e_rdy, (t + 1) * 16)
                link(dve.reciprocal(rsum, s))
                link(dve.tensor_tensor(mix[:, 0:512].rearrange("p (h c) -> p h c", h=AH),
                                       pa[0][:, :].rearrange("p (h c) -> p h c", h=AH),
                                       rsum[:, 0:AH].unsqueeze(2).broadcast_to([P, AH, HD]), ALU.mult))
                dve.tensor_tensor(mb, pa[1][:, :].rearrange("p (h c) -> p h c", h=BH),
                                  rsum[:, AH:AH + 2 * BH:2].unsqueeze(2).broadcast_to([P, BH, P]),
                                  ALU.mult).then_inc(sums_read, 1)
                dve.wait_ge(sums_read, t + 1)

            def head_norm():
                link(dve.tensor_tensor(sq, mb, mb, ALU.mult))
                link(dve.tensor_reduce(ms, sq, AX.X, ALU.add))
                dve.tensor_scalar(ms, ms, 1.0 / P, EPS, ALU.mult, ALU.add).then_inc(sq_rdy, 1)

            def head_scale(t):
                dve.wait_ge(rms_rdy, t + 1)
                link(dve.tensor_tensor(mb, mb, rms.unsqueeze(2).broadcast_to([P, BH, P]), ALU.mult))
                dve.tensor_tensor(mb, mb, subg.unsqueeze(1).broadcast_to([P, BH, P]), ALU.mult).then_inc(mix_rdy, 1)

            mb = mix[:, 512:1024].rearrange("p (h c) -> p h c", h=BH)
            lu = N_IDX
            n_exp = 0
            n_dl = [0]
            for what, i in order:
                if what == "task" and i < NTK:
                    t, k = TASKS[i]
                    n = P * (t + 1)
                    if k < AH:
                        q = prob[prob_at[i][0]]
                        dve.wait_ge(l_rdy, lu + 1)
                        if prob_prev[i] >= 0:
                            dve.wait_ge(t_rdy, turned_at["task", prob_prev[i]])
                        dve.tensor_tensor_reduce(out=q[:, 0:n], in0=lg[lu % 2][:, 0:n], in1=score[t], scale=1.0,
                                                 scalar=-3.0e38, op0=ALU.add, op1=ALU.max,
                                                 accum_out=mx[:, k:k + 1]).then_inc(l_dve, 1)
                        n_dl[0] += 1
                        dve.wait_ge(l_dve, n_dl[0])
                        dve.tensor_scalar(nmx[:, k:k + 1], mx[:, k:k + 1], -SCALE, None, ALU.mult).then_inc(mx_rdy, 1)
                        lu += 1
                        n_exp += 1
                    else:
                        for j in range(2):
                            c = AH + 2 * (k - AH) + j
                            dve.wait_ge(l_rdy, lu + 1)
                            link(dve.tensor_reduce(mx[:, c:c + 1], lg[lu % 2][:, 0:n], AX.X, ALU.max))
                            dve.tensor_scalar(nmx[:, c:c + 1], mx[:, c:c + 1], -SCALE, None, ALU.mult).then_inc(mx_rdy, 1)
                            lu += 1
                        n_exp += 2
                        dve.wait_ge(e_rdy, n_exp)
                        s = ssum[t % 2]
                        p0, p1 = (prob[q][:, 0:n] for q in prob_at[i])
                        link(dve.reciprocal(rsum[:, c:c + 1], s[:, c:c + 1]))
                        link(dve.scalar_tensor_tensor(cB[:, 0:1], s[:, c - 1:c], neglam, rsum[:, c:c + 1], ALU.mult, ALU.mult))
                        dve.scalar_tensor_tensor(p0, p1, cB[:, 0:1], p0, ALU.mult, ALU.add).then_inc(cmb_rdy, 1)
                        dve.wait_ge(cmb_rdy, BH * t + k - AH + 1)
                if what == "task" and (i >= NTK or TASKS[i][0] > 0):
                    t, k = TASKS[i] if i < NTK else (NT, i - NTK)
                    flush = i >= NTK
                    if k == 1:
                        sums_out(i, t - 1)
                    if k == (1 if flush else 2):
                        head_norm()
                    if k == (1 if flush else 3):
                        head_scale(t - 1)
                    if k == 4:
                        norm_stats(h1, 0)
                    if k == 5:
                        norm_scale(h1, h1, g1, 0)
                    if k == 6:
                        dve.tensor_tensor(h1, h1, b1, ALU.add).then_inc(h1_rdy, 1)
                if what == "mix":
                    dve.wait_ge(l_rdy, lu + 1)
                    dve.wait_ge(hin_s, 16 * (i + 1))
                    if i:
                        dve.wait_ge(h1_st, 16 * i)
                        dve.wait_ge(t_rdy, turned_at["rows", i - 1])
                    else:
                        dve.wait_ge(rows_in, 48)
                    dve.scalar_tensor_tensor(h1, h_in, ALPHA, lg[lu % 2][:, :], ALU.mult, ALU.add).then_inc(l_dve, 1)
                    n_dl[0] += 1
                    dve.wait_ge(l_dve, n_dl[0])
                    lu += 1
                    if i == NT - 1:
                        layer_norm(h1, h1, g1, b1, 0, h1_rdy)
                if what == "shared":
                    shared(i)

            n_routed = dve.value_load(bend_i[0:1, NE:NE + 1], min_val=NE, max_val=MAXB - SHB)

            def ahead(r):
                e3 = dve.value_load(tab[0:1, bass.ds(r + (SHB + 3), 1)], min_val=0, max_val=NE)
                one_hot(r + 4, e3)

            def routed(r):
                hidden(r + SHB)
                row_remainders(r + 1)
                indices(r + 4, bass.ds(dve.value_load(parity[0:1, bass.ds(r, 1)], min_val=0, max_val=1), 1))
                src = pa[1][:, 0:2 * P].rearrange("p (j q) -> p j q", j=2)
                dve.wait_ge(hT_trn, r + (SHB + 1))
                dve.tensor_copy(hidTh, src).then_inc(hh_rdy, 1)
                dve.wait_ge(hh_rdy, r + 1)
                dve.tensor_tensor(hidTl, src, hidTh, ALU.subtract).then_inc(hT_rdy, 1)

            def first(n, j, r):
                ahead(r)
                if j == 0:
                    last_remainders(n, 1)
                elif not isinstance(n, int) or n < NE // 2 - 1:
                    last_remainders(n + 1, 0)
                dve.wait_ge(dh_rdy, n * 2 + (j + 1))
                dve.tensor_tensor(w_dl[j], w_rd[j], w_dh[j], ALU.subtract).then_inc(dl_rdy, 1)
                routed(r)

            def more(n, j, r):
                ahead(r)
                routed(r)

            for_experts(dve, first, more)
            gates_by_slot()
            dve.wait_ge(ple_in, 16 * 5)

            def gate_argument(t):
                dve.wait_ge(g_mm, t + 1)
                if t:
                    dve.wait_ge(m_rdy, t)
                dve.tensor_tensor(zt, lg[t % 2][:, :], bp, ALU.add).then_inc(z_rdy, 1)

            def finish(t):
                dve.wait_ge(s_rdy, t + 1)
                if t >= 2:
                    dve.wait_ge(o_st[t % 2], 16 * (t // 2))
                dve.wait_ge(p_mm, t + 1)
                for c in range(2):
                    h = slice(512 * c, 512 * (c + 1))
                    m = dve.tensor_tensor(ot[t % 2][:, h], zt[:, h], pa[c][:, :], ALU.mult)
                m.then_inc(m_rdy, 1)

            for t in range(NT):
                a = acc[t % 3]
                dve.wait_ge(row_in[t % 3], 48 * (t // 3 + 1))
                link(dve.scalar_tensor_tensor(a, a, ALPHA, ysh[t % 3], ALU.mult, ALU.add))
                for k in range(TOPK):
                    dve.wait_ge(y_in[k], 16 * (t + 1))
                    dve.scalar_tensor_tensor(a, yk[k], gate8[:, t, k:k + 1], a, ALU.mult, ALU.add).then_inc(y_used, 1)
                    dve.wait_ge(y_used, 8 * t + k + 1)
                    if t >= 2 and k == 2:
                        gate_argument(t - 2)
                    if t >= 2 and k == 4:
                        finish(t - 2)
                layer_norm(a, a, g2, b2, 0, h2_rdy)
            for t in range(NT - 2, NT):
                gate_argument(t)
                finish(t)


_INS = ["x", "p", "positions", "ln_emb_g", "ln_emb_b", "w_in", "w_o", "diff_lq1", "diff_lk1", "diff_lq2", "diff_lk2",
        "diff_subln_g", "ln1_g", "ln1_b", "w_router", "router_bias", "w_exp_gate", "w_exp_up", "w_exp_down",
        "w_sh_gate", "w_sh_up", "w_sh_down", "ln2_g", "ln2_b", "w_ple_gate", "b_ple_gate", "w_ple_proj"]


def kernel(**inputs):
    import numpy as np
    import concourse.bacc as bacc
    from concourse.bass_utils import run_bass_kernel_spmd as run

    nc = bacc.Bacc("TRN2", target_bir_lowering=False, num_devices=1)
    arrays, args = {}, []
    host = {n: np.ascontiguousarray(inputs[n]) for n in _INS}
    host["inv_freq"] = np.float32(10000.0) ** (-np.arange(0, HD, 2, dtype=np.float32) / np.float32(HD))
    for name, a in host.items():
        arrays[f"in_{name}"] = a
        args.append(nc.dram_tensor(f"in_{name}", a.shape, mybir.dt.from_np(a.dtype), kind="ExternalInput").ap())
    args.append(nc.dram_tensor("out_0", (1, S, D), F32, kind="ExternalOutput").ap())
    build(nc, *args)
    return run(nc, [arrays], core_ids=[0]).results[0]["out_0"]
```
